# Optimizing a Trainium2 kernel written in Bass

```python
import functools
import jax, jax.numpy as jnp
from jax import lax
import numpy as np

D_MODEL = 1024
BATCH = 1
SEQ = 1024
DEPTH = 2
DEC_BATCH = 8
DEC_SEQ = 8
PAST_LEN = 2048
PAGE_SIZE = 128

CONV_DIM = D_MODEL // 4
CONV_GROUPS = 4
CONV_W = 3
HG_WIDTH = D_MODEL // 4
HG_HEADS = 4
HG_DK = HG_WIDTH // HG_HEADS
HG_DV = HG_WIDTH // HG_HEADS
HG_CHUNK = 64
ATT_WIDTH = D_MODEL // 2
HEAD_DIM = 64
N_HEADS = ATT_WIDTH // HEAD_DIM
N_KV = 4
KV_WIDTH = N_KV * HEAD_DIM
IDX_HEADS = 8
IDX_DIM = 32
TOPK_MAX = 256
Q_BLOCK = 128
MIX_WIDTH = CONV_DIM + HG_WIDTH + ATT_WIDTH
N_MEM = 256
X_HEADS = 4
X_HEAD_DIM = 128
X_WIDTH = X_HEADS * X_HEAD_DIM
D_FF = 4 * D_MODEL
ROPE_THETA = 10000.0
LN_EPS = 1e-5
DN_ALPHA = (2 * DEPTH) ** 0.25
DN_BETA = (8 * DEPTH) ** -0.25
SPLIT_SIZES = (CONV_DIM, CONV_DIM, CONV_DIM, HG_WIDTH, HG_WIDTH, HG_WIDTH, HG_WIDTH,
               ATT_WIDTH, KV_WIDTH, KV_WIDTH, IDX_HEADS * IDX_DIM, IDX_DIM, IDX_HEADS)
SPLIT_POINTS = tuple(int(s) for s in np.cumsum(SPLIT_SIZES)[:-1])
N_IN = sum(SPLIT_SIZES)

kernel_name = 'hymba_conv_hgrn2_dsa_deepnorm_step'

F32 = jnp.float32

def layer_norm(x, g, b):
    xf = x.astype(F32)
    mu = xf.mean(-1, keepdims=True)
    var = jnp.square(xf - mu).mean(-1, keepdims=True)
    return ((xf - mu) * lax.rsqrt(var + LN_EPS) * g.astype(F32) + b.astype(F32)).astype(x.dtype)

def rope(x, pos):
    half = x.shape[-1] // 2
    inv = ROPE_THETA ** (-jnp.arange(half, dtype=F32) / half)
    ang = pos.astype(F32)[:, None] * inv[None, :]
    cos, sin = jnp.cos(ang)[:, None, :], jnp.sin(ang)[:, None, :]
    x1, x2 = x[..., :half].astype(F32), x[..., half:].astype(F32)
    return jnp.concatenate([x1 * cos - x2 * sin, x2 * cos + x1 * sin], axis=-1).astype(x.dtype)

def short_gated_conv(h, bg, cg, w_conv, buf):
    u = cg * h
    ext = jnp.concatenate([buf.astype(u.dtype), u], axis=1)
    L = u.shape[1]
    y = sum(w_conv[j] * ext[:, j:j + L] for j in range(CONV_W))
    return bg * y, ext[:, ext.shape[1] - (CONV_W - 1):]

def hgrn_lower_bounds(logits):
    p = jax.nn.softmax(logits.astype(F32), axis=0)
    c = jnp.cumsum(p, axis=0)
    return c - c[0:1]

def hgrn2_chunked(q, k, v, logf, s0):
    B, L, H, DK = q.shape
    C = HG_CHUNK if L % HG_CHUNK == 0 else L
    n = L // C
    def chunks(a):
        return a.reshape(B, n, C, H, a.shape[-1]).transpose(1, 0, 3, 2, 4).astype(F32)
    causal = jnp.tril(jnp.ones((C, C), bool))[:, :, None]
    def step(S, inp):
        qi, ki, vi, gi = inp
        b = jnp.cumsum(gi, axis=2)
        inter = jnp.einsum('bhtk,bhkv->bhtv', qi * jnp.exp(b), S)
        diff = b[:, :, :, None, :] - b[:, :, None, :, :]
        decay = jnp.exp(jnp.where(causal, diff, -jnp.inf))
        att = jnp.einsum('bhtk,bhtsk,bhsk->bhts', qi, decay, ki)
        intra = jnp.einsum('bhts,bhsv->bhtv', att, vi)
        bC = b[:, :, -1:, :]
        S_new = jnp.exp(bC[:, :, 0, :])[..., None] * S + jnp.einsum('bhsk,bhsv->bhkv', ki * jnp.exp(bC - b), vi)
        return S_new, inter + intra
    S, o = lax.scan(step, s0.astype(F32), (chunks(q), chunks(k), chunks(v), chunks(logf)))
    o = o.transpose(1, 0, 3, 2, 4).reshape(B, L, H, v.shape[-1])
    return o, S

def index_scores(qi, ki, wi):
    dots = jnp.einsum('bthd,bsd->bths', qi.astype(F32), ki.astype(F32))
    return jnp.einsum('bth,bths->bts', wi.astype(F32), jax.nn.relu(dots))

def sparse_attend(q, kg, vg, ok):
    B, T = q.shape[:2]
    qg = q.reshape(B, T, N_KV, N_HEADS // N_KV, HEAD_DIM).astype(F32)
    s = jnp.einsum('btngd,btknd->btngk', qg, kg.astype(F32)) * (HEAD_DIM ** -0.5)
    s = jnp.where(ok[:, :, None, None, :], s, -jnp.inf)
    p = jax.nn.softmax(s, axis=-1)
    o = jnp.einsum('btngk,btknd->btngd', p, vg.astype(F32))
    return o.reshape(B, T, N_HEADS, HEAD_DIM).astype(q.dtype)

def take_rows(a, idx):
    return jax.vmap(lambda aa, ii: aa[ii])(a, idx)

def dsa_prompt(q, k, v, qi, ki, wi):
    B, T = q.shape[:2]
    ksel = min(TOPK_MAX, T // 4)
    key_pos = jnp.arange(T)
    def block(i):
        t0 = i * Q_BLOCK
        sl = lambda a: lax.dynamic_slice_in_dim(a, t0, Q_BLOCK, axis=1)
        qpos = t0 + jnp.arange(Q_BLOCK)
        score = index_scores(sl(qi), ki, sl(wi))
        score = jnp.where(key_pos[None, None, :] <= qpos[None, :, None], score, -jnp.inf)
        _, idx = lax.top_k(score, ksel)
        ok = idx <= qpos[None, :, None]
        return sparse_attend(sl(q), take_rows(k, idx), take_rows(v, idx), ok)
    out = lax.map(block, jnp.arange(T // Q_BLOCK))
    return jnp.moveaxis(out, 0, 1).reshape(B, T, N_HEADS, HEAD_DIM)

def dsa_sample(q, k, v, qi, ki, wi, cache_k, cache_v, cache_kidx, page_table, layer):
    DB, T = q.shape[:2]
    page = cache_k.shape[2]
    past = page_table.shape[1] * page
    L = past + T
    ksel = min(TOPK_MAX, L // 4)
    ki_past = cache_kidx[layer, page_table].reshape(DB, past, IDX_DIM)
    ki_all = jnp.concatenate([ki_past.astype(ki.dtype), ki], axis=1)
    qpos = past + jnp.arange(T)
    score = index_scores(qi, ki_all, wi)
    score = jnp.where(jnp.arange(L)[None, None, :] <= qpos[None, :, None], score, -jnp.inf)
    _, idx = lax.top_k(score, ksel)
    ok = idx <= qpos[None, :, None]
    is_new = (idx >= past)[..., None, None]
    pidx = jnp.minimum(idx, past - 1)
    phys = jax.vmap(lambda pt, j: pt[j])(page_table, pidx // page)
    off = pidx % page
    nidx = jnp.clip(idx - past, 0, T - 1)
    kg = jnp.where(is_new, take_rows(k, nidx), cache_k[layer, phys, off].astype(k.dtype))
    vg = jnp.where(is_new, take_rows(v, nidx), cache_v[layer, phys, off].astype(v.dtype))
    return sparse_attend(q, kg, vg, ok)

def token_mixer(x, pos, w_in_l, w_conv_l, lb_l, hg_norm_l, w_out_l, conv_buf, hg_s0, attend):
    B, L, _ = x.shape
    z = x @ w_in_l
    (c_h, c_b, c_c, g_q, g_f, g_i, g_g, a_q, a_k, a_v, a_qi, a_ki, a_w) = jnp.split(z, SPLIT_POINTS, axis=-1)
    y_conv, conv_state = short_gated_conv(c_h, c_b, c_c, w_conv_l, conv_buf)
    sig = jax.nn.sigmoid(g_f.astype(F32))
    f = lb_l + (1.0 - lb_l) * sig
    kk = (1.0 - lb_l) * (1.0 - sig)
    heads = lambda a: a.reshape(B, L, HG_HEADS, a.shape[-1] // HG_HEADS)
    o_hg, hg_state = hgrn2_chunked(heads(g_q), heads(kk), heads(g_i), heads(jnp.log(f)), hg_s0)
    o_hg = o_hg * lax.rsqrt(jnp.mean(jnp.square(o_hg), -1, keepdims=True) + LN_EPS)
    o_hg = o_hg * hg_norm_l.astype(F32).reshape(HG_HEADS, HG_DV)
    y_hg = (o_hg.reshape(B, L, HG_WIDTH) * jax.nn.sigmoid(g_g.astype(F32))).astype(x.dtype)
    q = rope(a_q.reshape(B, L, N_HEADS, HEAD_DIM), pos)
    k = rope(a_k.reshape(B, L, N_KV, HEAD_DIM), pos)
    v = a_v.reshape(B, L, N_KV, HEAD_DIM)
    qi = rope(a_qi.reshape(B, L, IDX_HEADS, IDX_DIM), pos) * (IDX_DIM ** -0.5)
    ki = rope(a_ki[:, :, None, :], pos)[:, :, 0, :]
    wi = a_w * (IDX_HEADS ** -0.5)
    y_att = attend(q, k, v, qi, ki, wi).reshape(B, L, ATT_WIDTH)
    y = jnp.concatenate([y_conv, y_hg, y_att.astype(x.dtype)], axis=-1) @ w_out_l
    return y, conv_state, hg_state, k, v, ki

def cross_and_ffn(h, mk, mv, w_xq_l, w_xo_l, g2, b2, w_up_l, w_down_l, g3, b3):
    B, T, _ = h.shape
    q = (h @ w_xq_l).reshape(B, T, X_HEADS, X_HEAD_DIM)
    s = jnp.einsum('bthd,bmhd->bhtm', q.astype(F32), mk.astype(F32)) * (X_HEAD_DIM ** -0.5)
    p = jax.nn.softmax(s, axis=-1)
    o = jnp.einsum('bhtm,bmhd->bthd', p, mv.astype(F32)).reshape(B, T, X_WIDTH).astype(h.dtype)
    h = layer_norm(DN_ALPHA * h + o @ w_xo_l, g2, b2)
    u = jax.nn.relu(h @ w_up_l)
    return layer_norm(DN_ALPHA * h + (u * u) @ w_down_l, g3, b3)

def setup_inputs(seed: int = 0) -> dict:
    key = jax.random.key(seed)
    ks = iter(jax.random.split(key, 40))
    nrm = lambda shape, scale=1.0: jax.random.normal(next(ks), shape, F32) * scale
    n_pages = PAST_LEN // PAGE_SIZE
    n_phys = (DEC_BATCH * n_pages * 5) // 4
    page_table = jax.random.permutation(next(ks), n_phys)[:DEC_BATCH * n_pages]
    page_table = page_table.reshape(DEC_BATCH, n_pages).astype(jnp.int32)
    return {
        'x_prompt': nrm((BATCH, SEQ, D_MODEL)),
        'x_sample': nrm((DEC_BATCH, DEC_SEQ, D_MODEL)),
        'cache_k': nrm((DEPTH, n_phys, PAGE_SIZE, N_KV, HEAD_DIM)),
        'cache_v': nrm((DEPTH, n_phys, PAGE_SIZE, N_KV, HEAD_DIM)),
        'cache_kidx': nrm((DEPTH, n_phys, PAGE_SIZE, IDX_DIM)),
        'state_hgrn': nrm((DEPTH, DEC_BATCH, HG_HEADS, HG_DK, HG_DV), 0.5),
        'state_conv': nrm((DEPTH, DEC_BATCH, CONV_W - 1, CONV_DIM)),
        'cache_mem_k': nrm((DEPTH, DEC_BATCH, N_MEM, X_HEADS, X_HEAD_DIM)),
        'cache_mem_v': nrm((DEPTH, DEC_BATCH, N_MEM, X_HEADS, X_HEAD_DIM)),
        'page_table': page_table,
        'mem_prompt': nrm((BATCH, N_MEM, D_MODEL)),
        'w_in': nrm((DEPTH, D_MODEL, N_IN), D_MODEL ** -0.5),
        'w_conv': nrm((DEPTH, CONV_W, CONV_DIM), CONV_W ** -0.5),
        'hg_lb_logits': nrm((DEPTH, HG_WIDTH), 0.5),
        'hg_norm': 1.0 + nrm((DEPTH, HG_WIDTH), 0.02),
        'w_out': nrm((DEPTH, MIX_WIDTH, D_MODEL), DN_BETA * MIX_WIDTH ** -0.5),
        'ln1_g': 1.0 + nrm((DEPTH, D_MODEL), 0.02),
        'ln1_b': nrm((DEPTH, D_MODEL), 0.02),
        'w_xq': nrm((DEPTH, D_MODEL, X_WIDTH), D_MODEL ** -0.5),
        'w_xk': nrm((DEPTH, D_MODEL, X_WIDTH), D_MODEL ** -0.5),
        'w_xv': nrm((DEPTH, D_MODEL, X_WIDTH), D_MODEL ** -0.5),
        'w_xo': nrm((DEPTH, X_WIDTH, D_MODEL), DN_BETA * X_WIDTH ** -0.5),
        'ln2_g': 1.0 + nrm((DEPTH, D_MODEL), 0.02),
        'ln2_b': nrm((DEPTH, D_MODEL), 0.02),
        'w_up': nrm((DEPTH, D_MODEL, D_FF), D_MODEL ** -0.5),
        'w_down': nrm((DEPTH, D_FF, D_MODEL), DN_BETA * D_FF ** -0.5),
        'ln3_g': 1.0 + nrm((DEPTH, D_MODEL), 0.02),
        'ln3_b': nrm((DEPTH, D_MODEL), 0.02),
    }

def reference(x_prompt, x_sample, cache_k, cache_v, cache_kidx, state_hgrn, state_conv, cache_mem_k, cache_mem_v,
              page_table, mem_prompt, w_in, w_conv, hg_lb_logits, hg_norm, w_out, ln1_g, ln1_b,
              w_xq, w_xk, w_xv, w_xo, ln2_g, ln2_b, w_up, w_down, ln3_g, ln3_b):
    Bp, Tp, _ = x_prompt.shape
    past = page_table.shape[1] * cache_k.shape[2]
    pos_p = jnp.arange(Tp)
    pos_s = past + jnp.arange(x_sample.shape[1])
    lower = hgrn_lower_bounds(hg_lb_logits)
    hp, hs = x_prompt, x_sample
    kp, vp, kip, ksl, vsl, kis, hgp, hgs, cvp, cvs, mkp, mvp = ([] for _ in range(12))
    for l in range(DEPTH):
        mixer_w = (w_in[l], w_conv[l], lower[l], hg_norm[l], w_out[l])
        tail_w = (w_xq[l], w_xo[l], ln2_g[l], ln2_b[l], w_up[l], w_down[l], ln3_g[l], ln3_b[l])
        conv0 = jnp.zeros((Bp, CONV_W - 1, CONV_DIM), hp.dtype)
        hg0 = jnp.zeros((Bp, HG_HEADS, HG_DK, HG_DV), F32)
        y, c_st, h_st, k, v, ki = token_mixer(hp, pos_p, *mixer_w, conv0, hg0, dsa_prompt)
        hp = layer_norm(DN_ALPHA * hp + y, ln1_g[l], ln1_b[l])
        mk = (mem_prompt @ w_xk[l]).reshape(Bp, N_MEM, X_HEADS, X_HEAD_DIM)
        mv = (mem_prompt @ w_xv[l]).reshape(Bp, N_MEM, X_HEADS, X_HEAD_DIM)
        hp = cross_and_ffn(hp, mk, mv, *tail_w)
        kp.append(k); vp.append(v); kip.append(ki); hgp.append(h_st); cvp.append(c_st); mkp.append(mk); mvp.append(mv)
        attend = functools.partial(dsa_sample, cache_k=cache_k, cache_v=cache_v, cache_kidx=cache_kidx,
                                   page_table=page_table, layer=l)
        y, c_st, h_st, k, v, ki = token_mixer(hs, pos_s, *mixer_w, state_conv[l], state_hgrn[l], attend)
        hs = layer_norm(DN_ALPHA * hs + y, ln1_g[l], ln1_b[l])
        hs = cross_and_ffn(hs, cache_mem_k[l], cache_mem_v[l], *tail_w)
        ksl.append(k); vsl.append(v); kis.append(ki); hgs.append(h_st); cvs.append(c_st)
    st = lambda xs: jnp.stack(xs, axis=0)
    return (hp, hs, st(kp), st(vp), st(kip), st(ksl), st(vsl), st(kis),
            st(hgp), st(hgs), st(cvp), st(cvs), st(mkp), st(mvp))


_drawn_inputs = setup_inputs


def setup_inputs(seed=0):
    import zlib

    import numpy as np

    out = dict(_drawn_inputs(seed))
    spreads = {}
    factors = {'hg_norm': 22.087, 'cache_k': 3.377, 'cache_kidx': 2.854}
    for name, (base, spread) in spreads.items():
        noise = np.random.default_rng([zlib.crc32(name.encode()), seed]).standard_normal(out[name].shape)
        drawn = base * np.exp(spread * noise) if base else spread * noise
        out[name] = __import__('jax').numpy.asarray(drawn.astype(out[name].dtype))
    for name, factor in factors.items():
        out[name] = (out[name] * factor).astype(out[name].dtype)
    return out
```

```python
from contextlib import ExitStack

import concourse.bass as bass
from concourse import mybir

F32 = mybir.dt.float32
F32R = mybir.dt.float32r
BF16 = mybir.dt.bfloat16
U8 = mybir.dt.uint8
I32 = mybir.dt.int32
ALU = mybir.AluOpType
ACT = mybir.ActivationFunctionType
AX = mybir.AxisListType.X

P = 128
D = 1024
DEPTH = 2
SEQ = 1024
DB, DT = 8, 8
NS = DB * DT
TOK = SEQ + NS
NT = SEQ // P + 1
KC = D // P
PAST, PAGE = 2048, 128
NPG = PAST // PAGE
NPHYS = DB * NPG * 5 // 4
TOPK = 256
HD, NKV, NH = 64, 4, 8
IH, ID = 8, 32
NMEM, XH, XD = 256, 4, 128
DFF = 4 * D
NIN = 3112
LS = PAST + NS
EPS = 1e-5
ALPHA = (2 * DEPTH) ** 0.25
NEG = -1e30
GONE = -3e38
PICKED = -2e38
C_H, C_B, C_C, G_Q, G_F, G_I, G_G, A_Q, A_KV, A_QI = 0, 256, 512, 768, 1024, 1280, 1536, 1792, 2304, 2816
LEVELS = [64, 32, 16, 8, 4, 2, 1]

CST = {}
_n = 0
for _name, _w in (("ident", 128), ("cos64", NT * 64), ("sin64", NT * 64), ("cos32", NT * 32), ("sin32", NT * 32),
                  ("causal", 128), ("own", NS), ("heads", 128), ("batch", DB)):
    CST[_name] = (_n, _n + _w)
    _n += _w
NCST = _n
NCST16 = 128 + TOK + 4 * 128
NMASK = 8 * 128
NPAR = 6 + 2 + 2 * DB * 2

OFF = {}
_n = 0
for _name, _w in (("X", NT * D), ("A", KC * TOK), ("W", 8192), ("S", 4224 + LS), ("M", 2304 + LS // 2),
                  ("C", 4 * 2 * TOK), ("U", 2 * (SEQ + 2) + 2 * DB * (DT + 2)), ("G", NT * 256)):
    OFF[_name] = _n
    _n += _w
NARENA = _n
NHEAD = OFF["W"]
RR = OFF["S"]


class Chain:

    def __init__(self, eng, sem):
        self.eng, self.sem, self.n = eng, sem, 0

    def mark(self, ins):
        self.n += 1
        ins.then_inc(self.sem, 1)

    def wait(self):
        self.eng.wait_ge(self.sem, self.n)

    def __call__(self, ins):
        self.mark(ins)
        self.wait()


def rows(t):
    return P if t < NT - 1 else NS


def build(nc, i, o):
    ctx = ExitStack()
    with ctx:
        ctx.enter_context(nc.allow_non_contiguous_dma(reason="small parameter rows"))
        ar = ctx.enter_context(nc.sbuf_tensor("arena", [P, NHEAD], F32))
        cst = ctx.enter_context(nc.sbuf_tensor("cst", [P, NCST], F32))
        cst16 = ctx.enter_context(nc.sbuf_tensor("cst16", [P, NCST16], BF16))
        msk = ctx.enter_context(nc.sbuf_tensor("msk", [P, NMASK], U8))
        par = ctx.enter_context(nc.sbuf_tensor("par", [P, NPAR], F32))
        small = ctx.enter_context(nc.sbuf_tensor("small", [P, 192], F32))
        pages = ctx.enter_context(nc.sbuf_tensor("pages", [1, DB * NPG], I32))
        ps = ctx.enter_context(nc.psum_tensor("ps", [P, 8 * 512], F32))
        sems, stacks, rest = [], [ctx], {}

        def sem(name):
            s = (stacks[-1]).enter_context(nc.semaphore(name))
            sems.append(s)
            return s

        def at(region, off, *dims):
            n = 1
            for x in dims:
                n *= x
            base = (OFF[region] if isinstance(region, str) else region) + off
            if base < NHEAD:
                v = ar[:, base:base + n]
            else:
                v = rest["f32"][:, base - NHEAD:base - NHEAD + n]
            if len(dims) == 2:
                v = v.rearrange("p (a b) -> p a b", a=dims[0])
            if len(dims) == 3:
                v = v.rearrange("p (a b c) -> p a b c", a=dims[0], b=dims[1])
            if len(dims) == 4:
                v = v.rearrange("p (a b c d) -> p a b c d", a=dims[0], b=dims[1], c=dims[2])
            return v

        def cs(name):
            return cst[:, CST[name][0]:CST[name][1]]

        def bank(n, w=512):
            return ps[:, n * 512:n * 512 + w]

        def tcol(t):
            return slice(t * P, t * P + rows(t))

        ident = cs("ident")
        ident16 = cst16[:, 0:128]
        start16 = cst16[:, 128:128 + TOK]
        spread = cst16[:, 128 + TOK:].rearrange("p (a b) -> p a b", a=4)
        causal, own = cs("causal"), cs("own")
        lb_tab = small[:, 0:4].rearrange("p (l c) -> p l c", l=2)
        lb, oml = small[:, 4:6], small[:, 6:8]
        eps_t = small[:, 8:9]
        w_idx = small[:, 16:16 + NT * IH].rearrange("p (t h) -> p t h", t=NT)
        stat = small[:, 96:192]

        chd, cha, chp = sem("chain_dve"), sem("chain_act"), sem("chain_pool")

        s_c, s_cn, s_x0, s_lb = sem("const_in"), sem("const_narrow_in"), sem("x_in_y"), sem("lb_steps")
        with nc.Block() as block:
            @block.sync
            def _(sp):
                sp.dma_start(cst[:, :], i["cst"]).then_inc(s_c, 16)
                sp.dma_start(at("X", 0, NCST16 + NMASK), i["cst_narrow"]).then_inc(s_cn, 16)
                sp.dma_start(pages[:, :], i["page_table"]).then_inc(s_c, 16)
                sp.dma_start(stat[:, 0:4], i["lb_logits"]).then_inc(s_lb, 16)
                sp.dma_start(o["y_prompt"][0], i["x_prompt"][0]).then_inc(s_x0, 16)
                sp.dma_start(o["y_sample"], i["x_sample"]).then_inc(s_x0, 16)
                sp.wait_ge(s_c, 32)
                sp.wait_ge(s_x0, 32)

            @block.vector
            def _(dve):
                ch = Chain(dve, chd)
                l0, l1 = stat[:, 0:2], stat[:, 2:4]
                dve.memset(eps_t, EPS)
                dve.wait_ge(s_cn, 16)
                dve.tensor_copy(cst16[:, :], at("X", 0, NCST16))
                dve.tensor_copy(msk[:, :], at("X", NCST16, NMASK))
                dve.wait_ge(s_lb, 16)
                ch(dve.tensor_tensor(stat[:, 4:6], l0, l1, ALU.max))
                ch.mark(dve.tensor_tensor(stat[:, 6:8], l0, stat[:, 4:6], ALU.subtract))
                dve.tensor_tensor(stat[:, 8:10], l1, stat[:, 4:6], ALU.subtract).then_inc(s_lb, 1)
                dve.wait_ge(s_lb, 18)
                ch(dve.tensor_tensor(stat[:, 10:12], stat[:, 6:8], stat[:, 8:10], ALU.add))
                ch(dve.reciprocal(stat[:, 12:14], stat[:, 10:12]))
                ch.mark(dve.tensor_tensor(stat[:, 14:16], stat[:, 6:8], stat[:, 12:14], ALU.mult))
                ch(dve.tensor_tensor(stat[:, 16:18], stat[:, 8:10], stat[:, 12:14], ALU.mult))
                ch.mark(dve.memset(lb_tab[:, 0, :], 0.0))
                ch(dve.tensor_tensor(stat[:, 18:20], stat[:, 14:16], stat[:, 16:18], ALU.add))
                ch(dve.tensor_tensor(lb_tab[:, 1, :], stat[:, 18:20], stat[:, 14:16], ALU.subtract))

            @block.scalar
            def _(act):
                act.wait_ge(s_lb, 17)
                act.wait_ge(chd, 2)
                act.activation(stat[:, 6:10], stat[:, 6:10], ACT.Exp).then_inc(s_lb, 1)

        def clear_all():
            with nc.Block() as block:
                @block.gpsimd
                def _(pool):
                    lo = min(s.num for s in sems)
                    hi = max(s.num for s in sems)
                    pool.sem_clear(range(lo, hi + 1))

        env = dict(nc=nc, i=i, o=o, at=at, cs=cs, bank=bank, tcol=tcol, ps=ps, sem=sem, ident=ident, ident16=ident16,
                   start16=start16, spread=spread, causal=causal, own=own, lb_tab=lb_tab, lb=lb, oml=oml,
                   eps_t=eps_t, w_idx=w_idx, stat=stat, chd=chd, cha=cha, chp=chp, msk=msk, par=par, pages=pages)
        clear_all()
        with nc.Fori(0, DEPTH) as layer:
            env["layer"] = layer
            with nc.sbuf_tensor("arena_rest", [P, NARENA - NHEAD], F32) as rest["f32"]:
                env["counts"] = {"dve": 0, "act": 0, "pool": 0}
                with ExitStack() as half:
                    stacks.append(half)
                    index_block(env)
                    mixer_block(env)
                    attend_block(env)
                    clear_all()
                del stacks[-1]
                env["counts"] = {"dve": 0, "act": 0, "pool": 0}
                half = ctx.enter_context(ExitStack())
                stacks.append(half)
                out_block(env)
                cross_block(env)
            with (nc.sbuf_tensor("ffn_raw", [P, FFN_RAW], F32) as rest["f32"],
                  nc.sbuf_tensor("ffn_parts", [P, FFN_PARTS], F32R) as env["parts"]):
                ffn_block(env)
            clear_all()


def chains(e, eng, which):
    c = Chain(eng, {"dve": e["chd"], "act": e["cha"], "pool": e["chp"]}[which])
    c.n = e["counts"][which]
    return c


def keep(e, c, which):
    e["counts"][which] = c.n


def for_pages(eng, e, b, load):
    with eng.Fori(0, NPG // 4) as q:
        phys = [eng.value_load(e["pages"][0:1, bass.ds(b * NPG + q * 4 + k, 1)], min_val=0, max_val=NPHYS - 1)
                for k in range(4)]
        for k in range(4):
            load(q * 4 + k, bass.ds(e["layer"] * NPHYS + phys[k], 1))


def lay(x, layer):
    return x[bass.ds(layer, 1)]


def score_jobs():
    jobs, off = [], 0
    for t in range(2, NT - 1):
        jobs.append((off, t, 0, (t + 1) * P))
        off += (t + 1) * P
    jobs += [(off, NT - 1, 0, 1024), (off + 1024, NT - 1, 1024, 1024), (off + 2048, NT - 1, 2048, NS)]
    return jobs, off


def index_block(e):
    nc, i, o, at, bank, tcol, sem, layer = (e[k] for k in ("nc", "i", "o", "at", "bank", "tcol", "sem", "layer"))
    ident, w_idx = e["ident"], e["w_idx"]
    X = at("X", 0, NT, D)
    XT = at("A", 0, KC, TOK)
    wb = at("W", 0, KC, 296)
    kitc = at("W", 4096, 2, PAST)
    QKI = at("C", 0, 3, TOK)
    QB = at("C", 3264, IH, 2, NS)
    zi = at("C", 4288, 2, 296)
    rr = at("C", 4880, 2, 288)
    kr = at("C", 5456, 2, 128)
    kio = at("C", 5712, NT, ID)
    t1 = at("C", 6000, 288)
    t2 = at("C", 6288, 288)
    r = at("X", 0, 2, 1024)
    S = at("S", 0, 4224 + LS)
    jobs, _ = score_jobs()
    steps = [(j, h) for j in range(len(jobs)) for h in range(IH)]

    s_x = [sem(f"x_tiles{n}") for n in range(3)]
    s_w, s_kit, s_par, s_kid = (sem(n) for n in ("w_index", "cached_kidx", "params", "kidx_out"))
    s_tp, s_ta, s_td = sem("xt_done"), sem("xt_copied_act"), sem("xt_copied_dve")
    s_zp, s_zi, s_ro, s_qp, s_qk = (sem(n) for n in ("zidx_done", "zidx_copied", "roped", "qk_turned", "qk_copied"))
    s_qb, s_qz = sem("sample_q_spread"), sem("sample_q_zeroed")
    s_sp, s_sr, s_sd = sem("score_done"), sem("score_relu"), sem("score_added")

    with nc.Block() as block:
        @block.sync
        def _(sp):
            for n in range(3):
                sp.dma_start(X[:, 3 * n:3 * n + (3 if n < 2 else 2), :],
                             o["y_prompt"][0].rearrange("(t p) d -> p t d", p=P)[:, 3 * n:3 * n + (3 if n < 2 else 2), :]
                             ).then_inc(s_x[n], 16)
            sp.dma_start(X[0:NS, NT - 1, :], o["y_sample"].rearrange("b t d -> (b t) d")).then_inc(s_x[2], 16)
            sp.dma_start(wb, lay(i["w_in"], layer).rearrange("l (k p) n -> p (l k) n", p=P)[:, :, A_QI:NIN]
                         ).then_inc(s_w, 16)
            sp.dma_start(e["par"][:, :], lay(i["params"], layer).rearrange("l p n -> (l p) n")).then_inc(s_par, 16)
            for b in range(DB):
                for_pages(sp, e, b, lambda pg, page: sp.dma_start(
                    kitc[32 * (b % 4):32 * (b % 4) + 32, b // 4, bass.ds(pg * PAGE, PAGE)],
                    i["kidxT"][page].rearrange("n d s -> (n d) s")).then_inc(s_kit, 16))
            sp.wait_ge(s_ro, NT)
            sp.dma_start(lay(o["kidx_prompt"], layer).rearrange("l b (t p) d -> p (l b t) d", p=P),
                         kio[:, 0:NT - 1, :]).then_inc(s_kid, 16)
            sp.dma_start(lay(o["kidx_sample"], layer).rearrange("l b t d -> (l b t) d"),
                         kio[0:NS, NT - 1, :]).then_inc(s_kid, 16)
            sp.wait_ge(s_kid, 32)
            sp.wait_ge(s_par, 16)
            sp.wait_ge(s_kit, 16 * DB * NPG)

        @block.tensor
        def _(pe):
            for t in range(NT):
                R = rows(t)
                if t % 3 == 0:
                    pe.wait_ge(s_x[t // 3], 16 * (1 + (t // 3 == 2)))
                for half in range(2):
                    g = 2 * t + half
                    if g >= 4:
                        pe.wait_ge((s_ta, s_td)[g % 2], g // 2 - 1)
                    for c in range(4):
                        ins = pe.transpose(bank(g % 4)[:, c * P:c * P + R],
                                           X[0:R, t, (4 * half + c) * P:(4 * half + c + 1) * P], ident[0:R, 0:R])
                    ins.then_inc(s_tp, 1)
            pe.wait_ge(s_w, 16)

            def turn(t):
                R = rows(t)
                pe.wait_ge(s_ro, t + 1)
                if t >= 2:
                    pe.wait_ge(s_qk, t - 1)
                for n, src in enumerate((rr[0:R, t % 2, 0:128], rr[0:R, t % 2, 128:256], kr[0:R, t % 2, :])):
                    ins = pe.transpose(bank(6 + t % 2)[:, n * P:n * P + R], src, ident[0:R, 0:R])
                ins.then_inc(s_qp, 1)

            for t in range(NT):
                R = rows(t)
                pe.wait_ge(s_ta, t + 1)
                pe.wait_ge(s_td, t + 1)
                if t >= 2:
                    pe.wait_ge(s_zi, t - 1)
                for k in range(KC):
                    ins = pe.matmul(bank(4 + t % 2, 296)[0:R, :], XT[:, k, tcol(t)], wb[:, k, :],
                                    start=(k == 0), stop=(k == KC - 1))
                ins.then_inc(s_zp, 1)
                if t:
                    turn(t - 1)
            turn(NT - 1)
            pe.wait_ge(s_qk, NT)
            for n, (j, h) in enumerate(steps):
                _, t, k0, w = jobs[j]
                if n >= 2:
                    pe.wait_ge(s_sr, n - 1)
                if j == 6 and h == 0:
                    pe.wait_ge(s_qb, 1)
                    pe.wait_ge(s_kit, 16 * DB * NPG)
                out = e["ps"][:, (n % 2) * 1024:(n % 2) * 1024 + w]
                part = slice(32 * (h % 4), 32 * (h % 4) + 32)
                if t < NT - 1:
                    for a in range(0, w, 512):
                        b = min(a + 512, w)
                        ins = pe.matmul(out[:, a:b], QKI[part, h // 4, tcol(t)], QKI[part, 2, a:b],
                                        start=True, stop=True)
                elif k0 < PAST:
                    for a in range(0, w, 512):
                        for g in range(2):
                            ins = pe.matmul(out[0:NS, a:a + 512], QB[:, h, g, :], kitc[:, g, k0 + a:k0 + a + 512],
                                            start=(g == 0), stop=(g == 1))
                else:
                    ins = pe.matmul(out[0:NS, :], QKI[part, h // 4, SEQ:TOK], QKI[part, 2, SEQ:TOK],
                                    start=True, stop=True)
                ins.then_inc(s_sp, 1)

        @block.scalar
        def _(act):
            ch = chains(e, act, "act")
            for t in range(NT):
                act.wait_ge(s_tp, 2 * t + 1)
                act.copy(XT[:, 0:4, tcol(t)], bank((2 * t) % 4).rearrange("p (c n) -> p c n", c=4)[:, :, 0:rows(t)]
                         ).then_inc(s_ta, 1)

            def qk(t):
                act.wait_ge(s_qp, t + 1)
                act.copy(QKI[:, :, tcol(t)], bank(6 + t % 2, 384).rearrange("p (c n) -> p c n", c=3)[:, :, 0:rows(t)]
                         ).then_inc(s_qk, 1)

            for t in range(NT):
                R = rows(t)
                act.wait_ge(s_zp, t + 1)
                if t >= 2:
                    act.wait_ge(s_ro, t - 1)
                act.mul(w_idx[0:R, t, :], bank(4 + t % 2, 296)[0:R, 288:296], (ID * IH) ** -0.5)
                act.copy(zi[0:R, t % 2, 0:288], bank(4 + t % 2, 296)[0:R, 0:288]).then_inc(s_zi, 1)
                if t:
                    qk(t - 1)
            qk(NT - 1)
            for n, (j, h) in enumerate(steps):
                _, t, k0, w = jobs[j]
                act.wait_ge(s_sp, n + 1)
                if n >= 2:
                    act.wait_ge(s_sd, n - 1)
                act.activation(r[0:rows(t), n % 2, 0:w], e["ps"][0:rows(t), (n % 2) * 1024:(n % 2) * 1024 + w],
                               ACT.Relu).then_inc(s_sr, 1)
            keep(e, ch, "act")

        @block.gpsimd
        def _(pool):
            pool.memset(at("C", 3264, IH * 2 * NS), 0.0).then_inc(s_qz, 1)

        @block.vector
        def _(dve):
            ch = chains(e, dve, "dve")
            for t in range(NT):
                dve.wait_ge(s_tp, 2 * t + 2)
                dve.tensor_copy(XT[:, 4:8, tcol(t)],
                                bank((2 * t + 1) % 4).rearrange("p (c n) -> p c n", c=4)[:, :, 0:rows(t)]
                                ).then_inc(s_td, 1)
            ch(dve.tensor_copy(e["lb"], e["lb_tab"][:, bass.ds(layer, 1), :].rearrange("p l c -> p (l c)")))
            ch(dve.tensor_scalar(e["oml"], e["lb"], -1.0, 1.0, ALU.mult, ALU.add))
            cos = e["cs"]("cos32").rearrange("p (t n) -> p t n", t=NT)
            sin = e["cs"]("sin32").rearrange("p (t n) -> p t n", t=NT)
            for t in range(NT):
                R = rows(t)
                z = zi[0:R, t % 2, 0:288].rearrange("p (h n) -> p h n", h=9)
                a = t1[0:R].rearrange("p (h n) -> p h n", h=9)
                b = t2[0:R].rearrange("p (h n) -> p h n", h=9)
                dve.wait_ge(s_zi, t + 1)
                ch.mark(dve.tensor_tensor(a, z, cos[0:R, t, :].unsqueeze(1).broadcast_to([R, 9, 32]), ALU.mult))
                ch.mark(dve.tensor_tensor(b[:, :, 0:16], z[:, :, 16:32],
                                          sin[0:R, t, 0:16].unsqueeze(1).broadcast_to([R, 9, 16]), ALU.mult))
                ch(dve.tensor_tensor(b[:, :, 16:32], z[:, :, 0:16],
                                     sin[0:R, t, 16:32].unsqueeze(1).broadcast_to([R, 9, 16]), ALU.mult))
                if t >= 2:
                    dve.wait_ge(s_qp, t - 1)
                ch(dve.tensor_tensor(rr[0:R, t % 2, :], t1[0:R], t2[0:R], ALU.add))
                ch(dve.tensor_copy(kio[0:R, t, :], rr[0:R, t % 2, 256:288]))
                dve.tensor_copy(kr[0:R, t % 2, :].rearrange("p (a n) -> p a n", a=4),
                                rr[0:R, t % 2, 256:288].unsqueeze(1).broadcast_to([R, 4, 32])).then_inc(s_ro, 1)
            dve.wait_ge(s_qk, NT)
            dve.wait_ge(s_qz, 1)
            for b in range(4):
                for q in range(4):
                    for g in range(2):
                        ins = dve.tensor_copy(QB[32 * b:32 * b + 32, q:IH:4, g, (4 * g + b) * DT:(4 * g + b + 1) * DT],
                                              QKI[32 * q:32 * q + 32, 0:2,
                                                  SEQ + (4 * g + b) * DT:SEQ + (4 * g + b + 1) * DT])
                        ch.mark(ins)
            ch.wait()
            dve.engine_nop().then_inc(s_qb, 1)
            for n, (j, h) in enumerate(steps):
                off, t, k0, w = jobs[j]
                R = rows(t)
                acc = S[0:R, off:off + w]
                dve.wait_ge(s_sr, n + 1)
                if n:
                    dve.wait_ge(s_sd, n)
                if h == 0:
                    ins = dve.tensor_scalar(acc, r[0:R, n % 2, 0:w], w_idx[0:R, t, h:h + 1], None, ALU.mult)
                else:
                    ins = dve.scalar_tensor_tensor(acc, r[0:R, n % 2, 0:w], w_idx[0:R, t, h:h + 1], acc,
                                                   ALU.mult, ALU.add)
                ins.then_inc(s_sd, 1)
            dve.wait_ge(s_sd, len(steps))
            for off, t, k0, w in jobs:
                if t < NT - 1:
                    d = S[:, off + w - P:off + w]
                    ch(dve.tensor_tensor(d, d, e["causal"], ALU.add))
                elif k0 == PAST:
                    d = S[0:NS, off:off + w]
                    ch(dve.tensor_tensor(d, d, e["own"][0:NS], ALU.add))
            keep(e, ch, "dve")


FEAT = [C_H, C_H + P, C_B, C_B + P, C_C, C_C + P, G_Q, G_Q + P, G_F, G_F + P, G_G, G_G + P]
WBLK = [(C_H, 512), (C_C, 512), (A_KV, 512), (A_Q, 512), (G_F, 512), (G_G, 256)]
HG_GROUPS = [(0, 3), (3, 6), (6, 9)]


def mixer_block(e):
    nc, i, o, at, bank, tcol, sem, layer = (e[k] for k in ("nc", "i", "o", "at", "bank", "tcol", "sem", "layer"))
    ident, par, ps = e["ident"], e["par"], e["ps"]
    XT = at("A", 0, KC, TOK)
    WB = [at("W", 4096 * n, KC, 512) for n in range(2)]
    qT = at("X", 0, 4, TOK)
    kT = at("X", 4 * TOK, 2, TOK)
    V = at("X", 6 * TOK, NT, 256)
    S = at("S", 0, 4224 + LS)
    M16 = at("M", 0, 2304 + LS // 2).bitcast(BF16)
    CH, CB, CC, GQ = (at("C", n * 2 * TOK, 2, TOK) for n in range(4))
    GF, GG = CH, CC
    nU = 2 * (SEQ + 2)
    UP = at("U", 0, 2, SEQ + 2)
    US = at("U", nU, 2, DB, DT + 2)
    GI = at("G", 0, NT, 256)
    w0 = par[:, 0:6].rearrange("p (j c) -> p j c", j=3)
    hgn = par[:, 6:8]
    cst0 = par[:, 8:8 + 4 * DB].rearrange("p (c b j) -> p c b j", c=2, b=DB)

    s_wl = [sem(f"w_mix{n}") for n in range(2)]
    s_fp, s_fe, s_up, s_ue, s_rp, s_re, s_rot = (sem(n) for n in (
        "feat_done", "feat_copied", "tok_done", "tok_copied", "rot_turned", "rot_copied", "rotated"))
    s_krd = [sem(f"k_rows_out{n}") for n in range(2)]
    s_qs = sem("hg_qk_scaled")
    s_cu, s_cv, s_co = (sem(n) for n in ("conv_u", "conv_done", "mix_out"))
    s_hin, s_oa = sem("hg_state_in"), sem("hg_sample_att_o")
    s_k1, s_k2 = sem("topk_max"), sem("topk_gone")
    s_sg, s_lf, s_kk, s_b, s_D, s_E, s_G = (sem(n) for n in (
        "hg_sigmoid", "hg_logf", "hg_gate", "hg_cumsum", "hg_diff", "hg_exp", "hg_level"))
    s_hz, s_ap, s_ad, s_kp, s_ke, s_pp, s_sv, s_op, s_oe = (sem(n) for n in (
        "hg_zeroed", "hg_att", "hg_att_kept", "hg_k_turned", "hg_k_copied", "hg_update", "hg_state", "hg_o", "hg_o_copied"))
    s_vb, s_n1, s_n2, s_n3, s_n4 = (sem(n) for n in ("hg_v_spread", "hg_sq", "hg_sum", "hg_rs", "hg_norm"))

    BB = at("W", 0, 2, TOK)
    QT = at("W", 2 * TOK, 2, TOK)
    KH = at("W", 4 * TOK, 2, TOK)
    S0 = at("W", 6 * TOK, DB, 2, HD)
    VB = at("W", 6 * TOK + 1024, DB, HD)
    E0 = at("A", 4 * TOK, 2, TOK)
    GL = [at("A", 6 * TOK + 768 * n, 2, 384) for n in range(2)]
    KK = CB
    YT = at("A", 0, KC, TOK)
    att = at("U", 0, 4, 512)
    slot = lambda t: t % 3 if t < NT - 1 else 3
    KHT = at("M", 1792, 2, 256)
    lvl = lambda n: e["msk"][:, n * P:(n + 1) * P]

    def st(n):
        return (at("U", 2048, 2, 64), at("W", 6 * TOK + 1536, 2, 64))[n % 2]

    zk, rk, tr = at("G", 0, 2, 512), at("G", 1024, 2, 512), at("M", 1792, 2, 512)

    def products_until(g, n):
        c = 0
        for gg, (ta, tb) in enumerate(HG_GROUPS):
            for nn in range(8):
                for t in range(ta, tb):
                    c += not (t == NT - 1 and nn and LEVELS[nn - 1] >= DT)
                if (gg, nn) == (g, n):
                    return c

    with nc.Block() as block:
        @block.sync
        def _(sp):
            for n, (c0, w) in enumerate(WBLK):
                if n >= 2:
                    if n == 2:
                        sp.wait_ge(s_fp, 4)
                    if n == 3:
                        sp.wait_ge(s_fp, 8)
                    if n == 4:
                        sp.wait_ge(s_up, NT)
                    if n == 5:
                        sp.wait_ge(s_up, 2 * NT)
                sp.dma_start(WB[n % 2][:, :, 0:w],
                             lay(i["w_in"], layer).rearrange("l (k p) n -> p (l k) n", p=P)[:, :, c0:c0 + w]
                             ).then_inc(s_wl[n % 2], 16)
                if n == 3:
                    for t in range(NT):
                        sp.wait_ge(s_rot, t + 1)
                        dst = (lay(o["k_prompt"], layer)[:, 0, tcol(t)].rearrange("l s d -> (l s) d") if t < NT - 1
                               else lay(o["k_sample"], layer).rearrange("l b s d -> (l b s) d"))
                        sp.dma_start(dst, rk[0:rows(t), t % 2, 0:256]).then_inc(s_krd[t % 2], 16)
                    sp.dma_start(lay(o["v_prompt"], layer).rearrange("l b (t p) d -> p (l b t) d", p=P),
                                 V[:, 0:NT - 1, :]).then_inc(s_co, 16)
                    sp.dma_start(lay(o["v_sample"], layer).rearrange("l b s d -> (l b s) d"),
                                 V[0:NS, NT - 1, :]).then_inc(s_co, 16)
            sp.wait_ge(s_cv, 1)
            sp.dma_start(lay(o["conv_prompt"], layer).rearrange("l p (c j) -> p (l c) j", c=2),
                         UP[:, :, SEQ:SEQ + 2]).then_inc(s_co, 16)
            sp.dma_start(lay(o["conv_sample"], layer).rearrange("l p (c b j) -> p (l c) b j", c=2, b=DB),
                         US[:, :, :, DT:DT + 2]).then_inc(s_co, 16)
            sp.wait_ge(s_fp, 12)
            sp.wait_ge(s_up, 3 * NT)
            sp.dma_start(S0.rearrange("p b c v -> p (b c) v"),
                         lay(i["state_hgrn"], layer).rearrange("l b (c h) k v -> (h k) (l b c) v", c=2)
                         ).then_inc(s_hin, 16)
            sp.wait_ge(s_sv, NT - 1)
            sp.dma_start(lay(o["hgrn_prompt"], layer).rearrange("l b (c h) k v -> (h k) (l b c) v", c=2),
                         st(NT - 1)).then_inc(s_co, 16)
            sp.wait_ge(s_sv, NT)
            sp.dma_start(lay(o["hgrn_sample"], layer).rearrange("l b (c h) k v -> (h k) (l b c) v", c=2),
                         S0.rearrange("p b c v -> p (b c) v")).then_inc(s_co, 16)
            sp.wait_ge(s_co, 16 * 6)
            sp.wait_ge(s_krd[0], 16 * 5)
            sp.wait_ge(s_krd[1], 16 * 4)

        @block.tensor
        def _(pe):
            def feat(f, buf, c):
                if f >= 2:
                    pe.wait_ge(s_fe, f - 1)
                for k in range(KC):
                    for a, b in ((0, 512), (512, 1024), (1024, TOK)):
                        ins = pe.matmul(ps[:, (f % 2) * 1536 + a:(f % 2) * 1536 + b],
                                        buf[:, k, c * P:(c + 1) * P], XT[:, k, a:b],
                                        start=(k == 0), stop=(k == KC - 1))
                ins.then_inc(s_fp, 1)

            def tok(u, t, buf, c0, w):
                R = rows(t)
                if u >= 2:
                    pe.wait_ge(s_ue, u - 1)
                for k in range(KC):
                    ins = pe.matmul(bank(6 + u % 2, w)[0:R, :], XT[:, k, tcol(t)], buf[:, k, c0:c0 + w],
                                    start=(k == 0), stop=(k == KC - 1))
                ins.then_inc(s_up, 1)

            def turn(n, t, chunks):
                R = rows(t)
                pe.wait_ge(s_rot, n + 1)
                if n >= 2:
                    pe.wait_ge(s_re, n - 1)
                for c in range(chunks):
                    ins = pe.transpose(bank(n % 2)[:, c * P:c * P + R], rk[0:R, n % 2, c * P:(c + 1) * P],
                                       ident[0:R, 0:R])
                ins.then_inc(s_rp, 1)

            for n in range(2):
                pe.wait_ge(s_wl[n], 16)
                for c in range(4):
                    feat(4 * n + c, WB[n], c)
            pe.wait_ge(s_fe, 8)
            for n in range(2):
                pe.wait_ge(s_wl[n], 32)
                for t in range(NT):
                    tok(NT * n + t, t, WB[n], 0, 512)
                    if t >= 2:
                        turn(NT * n + t - 2, t - 2, 2 + 2 * n)
                for t in (NT - 2, NT - 1):
                    turn(NT * n + t, t, 2 + 2 * n)
            pe.wait_ge(s_re, 2 * NT)
            pe.wait_ge(s_wl[0], 48)
            for c in range(2):
                feat(8 + c, WB[0], c)
            for t in range(NT):
                tok(2 * NT + t, t, WB[0], 256, 256)
            pe.wait_ge(s_wl[1], 48)
            for c in range(2):
                feat(10 + c, WB[1], c)
            pe.wait_ge(s_fe, 12)
            pe.wait_ge(s_ue, 3 * NT)
            na = 0

            def heads_att(t, lhs, rhs, c0):
                nonlocal na
                R = rows(t)
                if na >= 2:
                    pe.wait_ge(s_ad, na - 1)
                cols = slice(t * P - c0, t * P - c0 + R)
                for h in range(4):
                    c, hh = h // 2, h % 2
                    part = slice(64 * hh, 64 * hh + 64)
                    ins = pe.matmul(bank(2 * (na % 2) + hh)[0:R, c * P:c * P + R], lhs[part, c, cols],
                                    rhs[part, c, cols], start=True, stop=True)
                ins.then_inc(s_ap, 1)
                na += 1

            def tile_out(t):
                R = rows(t)
                if t >= 1:
                    pe.wait_ge(s_ke, t)
                for c in range(2):
                    ins = pe.transpose(bank(4)[0:R, c * P:(c + 1) * P], KH[:, c, tcol(t)], ident)
                ins.then_inc(s_kp, 1)
                if t:
                    pe.wait_ge(s_sv, t)
                    pe.wait_ge(s_oe, t)
                for c in range(2):
                    for hh in range(2):
                        h, part = 2 * c + hh, slice(64 * hh, 64 * hh + 64)
                        out = bank(5 + hh)[part, c * P:c * P + R]
                        if hh == 0 and c and t == NT - 1:
                            pe.wait_ge(s_oa, 2)
                        ins = pe.matmul(out, GI[0:R, t, h * HD:(h + 1) * HD],
                                        att[0:R, slot(t), hh * 256 + c * P:hh * 256 + c * P + R],
                                        start=True, stop=False, skip_group_check=True)
                        if t < NT - 1:
                            ins = pe.matmul(out, st(t)[part, c, :], QT[part, c, tcol(t)], start=False, stop=True,
                                            skip_group_check=True)
                    if t == NT - 1:
                        ins.then_inc(s_oa, 1)
                        pe.wait_ge(s_oa, 2 * c + 1)
                        for hh in range(2):
                            part = slice(64 * hh, 64 * hh + 64)
                            for b in range(DB):
                                ins = pe.matmul(bank(5 + hh)[part, c * P + b * DT:c * P + (b + 1) * DT],
                                                S0[part, b, c, :], QT[part, c, SEQ + b * DT:SEQ + (b + 1) * DT],
                                                start=False, stop=(b == DB - 1), skip_group_check=True)
                        if c == 0:
                            ins.then_inc(s_oa, 1)
                ins.then_inc(s_op, 1)
                pe.wait_ge(s_ke, t + 1)
                if t < NT - 1:
                    for h in range(4):
                        c, hh = h // 2, h % 2
                        ins = pe.matmul(bank(7)[64 * hh:64 * hh + 64, c * HD:(c + 1) * HD],
                                        KHT[:, t % 2, h * HD:(h + 1) * HD], GI[:, t, h * HD:(h + 1) * HD],
                                        start=True, stop=True)
                    ins.then_inc(s_pp, 1)
                else:
                    for c in range(2):
                        for hh in range(2):
                            h = 2 * c + hh
                            pe.wait_ge(s_vb, h + 1)
                            ins = pe.matmul(bank((7, 4)[c])[64 * hh:64 * hh + 64, :],
                                            KHT[0:NS, t % 2, h * HD:(h + 1) * HD],
                                            VB[0:NS].rearrange("p b v -> p (b v)"), start=True, stop=True)
                            ins.then_inc(s_pp, 1)

            for g, (ta, tb) in enumerate(HG_GROUPS):
                for n in range(8):
                    m = LEVELS[n - 1] if n else 0
                    if n:
                        pe.wait_ge(s_G, 7 * g + n)
                    else:
                        pe.wait_ge(s_kk, 1)
                        if g == 0:
                            pe.wait_ge(s_hz, 1)
                    for t in range(ta, tb):
                        if t == NT - 1 and m >= DT:
                            continue
                        if n:
                            heads_att(t, GL[n % 2], GL[n % 2], ta * P)
                        else:
                            heads_att(t, KK, GQ, 0)
                pe.wait_ge(s_ad, na)
                if g == 0:
                    pe.wait_ge(s_qs, 1)
                    pe.wait_ge(s_hin, 16)
                for t in range(ta, tb):
                    tile_out(t)
            pe.wait_ge(s_n1, 1)
            pe.wait_ge(s_sv, NT)
            for n in range(2):
                for a, b in ((0, 512), (512, 1024), (1024, TOK)):
                    ins = pe.matmul(ps[:, n * 1536 + a:n * 1536 + b], e["cs"]("heads"), QT[:, n, a:b],
                                    start=True, stop=True)
            ins.then_inc(s_n2, 1)

        @block.scalar
        def _(act):
            ch = chains(e, act, "act")
            dst = [CH, CB, CC, GQ, GF, GG]
            nf = [0]

            def feat():
                f = nf[0]
                nf[0] += 1
                act.wait_ge(s_fp, f + 1)
                if f == 8:
                    act.wait_ge(s_cu, 1)
                act.copy(dst[f // 2][:, f % 2, :], ps[:, (f % 2) * 1536:(f % 2) * 1536 + TOK]).then_inc(s_fe, 1)

            def turned(n, t, chunks):
                act.wait_ge(s_rp, n + 1)
                src = bank(n % 2, chunks * P).rearrange("p (c s) -> p c s", c=chunks)[:, :, 0:rows(t)]
                if chunks == 2:
                    act.copy(kT[:, :, tcol(t)], src).then_inc(s_re, 1)
                else:
                    act.mul(qT[:, :, tcol(t)], src, HD ** -0.5).then_inc(s_re, 1)

            for _ in range(8):
                feat()
            for n in range(2):
                for t in range(NT):
                    u, R = NT * n + t, rows(t)
                    act.wait_ge(s_up, u + 1)
                    if u >= 2:
                        act.wait_ge(s_rot, u - 1)
                    if n == 0:
                        act.copy(V[0:R, t, :], bank(6 + u % 2)[0:R, 256:512])
                        act.copy(zk[0:R, u % 2, 0:256], bank(6 + u % 2)[0:R, 0:256]).then_inc(s_ue, 1)
                    else:
                        act.copy(zk[0:R, u % 2, :], bank(6 + u % 2)[0:R, :]).then_inc(s_ue, 1)
                    if t >= 2:
                        turned(NT * n + t - 2, t - 2, 2 + 2 * n)
                for t in (NT - 2, NT - 1):
                    turned(NT * n + t, t, 2 + 2 * n)
            feat()
            feat()
            for t in range(NT):
                u, R = 2 * NT + t, rows(t)
                act.wait_ge(s_up, u + 1)
                act.copy(GI[0:R, t, :], bank(6 + u % 2, 256)[0:R, :]).then_inc(s_ue, 1)
            feat()
            feat()
            act.wait_ge(s_fe, 12)
            act.activation(GG, GG, ACT.Sigmoid)
            act.activation(GF, GF, ACT.Sigmoid).then_inc(s_sg, 1)
            act.wait_ge(s_cv, 2)
            act.wait_ge(s_kk, 1)
            act.activation(GF, GF, ACT.Ln).then_inc(s_lf, 1)
            act.wait_ge(s_b, 1)
            act.activation(E0, BB, ACT.Exp).then_inc(s_E, 1)
            act.wait_ge(s_D, 1)
            act.activation(KH, KH, ACT.Exp).then_inc(s_E, 1)
            nt = 0
            for g, (ta, tb) in enumerate(HG_GROUPS):
                w = min(tb * P, TOK) - ta * P
                for n in range(1, 8):
                    ww = w if LEVELS[n - 1] < DT or g < 2 else 2 * P
                    act.wait_ge(s_D, 1 + 7 * g + n)
                    act.activation(GL[n % 2][:, :, 0:ww], GL[n % 2][:, :, 0:ww], ACT.Exp).then_inc(s_E, 1)
                for t in range(ta, tb):
                    R = rows(t)
                    act.wait_ge(s_kp, t + 1)
                    if t >= 2:
                        act.wait_ge(s_pp, t - 1)
                    act.copy(KHT[0:R, t % 2, :], bank(4, 256)[0:R, :]).then_inc(s_ke, 1)
                    act.wait_ge(s_op, t + 1)
                    for hh in range(2):
                        part = slice(64 * hh, 64 * hh + 64)
                        ins = act.copy(YT[part, 2:4, tcol(t)],
                                       bank(5 + hh, 256)[part].rearrange("p (c s) -> p c s", c=2)[:, :, 0:R])
                    ins.then_inc(s_oe, 1)
            act.wait_ge(s_oe, NT)
            act.activation(QT, YT[:, 2:4, :], ACT.Square).then_inc(s_n1, 1)
            act.wait_ge(s_n2, 1)
            for n in range(2):
                ins = act.activation(E0[:, n, :], ps[:, n * 1536:n * 1536 + TOK], ACT.Identity,
                                     bias=e["eps_t"], scale=1.0 / HD)
                ch.mark(ins)
            ch.wait()
            ch(act.activation(KH, E0, ACT.Ln))
            act.activation(KH, KH, ACT.Exp, scale=-0.5).then_inc(s_n3, 1)
            keep(e, ch, "act")

        @block.gpsimd
        def _(pool):
            ch = chains(e, pool, "pool")
            ch.mark(pool.memset(UP[:, :, 0:2], 0.0))
            ch.mark(pool.tensor_copy(US[:, 0, :, 0:2], cst0[:, 0]))
            ch.mark(pool.tensor_copy(US[:, 1, :, 0:2], cst0[:, 1]))
            pool.wait_ge(s_fe, 6)
            for c in range(2):
                ch.mark(pool.tensor_tensor(UP[:, c, 2:], CH[:, c, 0:SEQ], CC[:, c, 0:SEQ], ALU.mult))
                ins = pool.tensor_tensor(US[:, c, :, 2:], CH[:, c, SEQ:TOK].rearrange("p (b s) -> p b s", b=DB),
                                         CC[:, c, SEQ:TOK].rearrange("p (b s) -> p b s", b=DB), ALU.mult)
                ch(ins)
            pool.engine_nop().then_inc(s_cu, 1)

            def rotate(n, t, w):
                R, H = rows(t), w // HD
                cos = e["cs"]("cos64").rearrange("p (t n) -> p t n", t=NT)[0:R, t]
                sin = e["cs"]("sin64").rearrange("p (t n) -> p t n", t=NT)[0:R, t]
                z = zk[0:R, n % 2, 0:w].rearrange("p (h n) -> p h n", h=H)
                a = tr[0:R, 0, 0:w].rearrange("p (h n) -> p h n", h=H)
                b = tr[0:R, 1, 0:w].rearrange("p (h n) -> p h n", h=H)
                pool.wait_ge(s_ue, n + 1)
                if n:
                    pool.wait_ge(s_rot, n)
                ch.mark(pool.tensor_tensor(a, z, cos.unsqueeze(1).broadcast_to([R, H, 64]), ALU.mult))
                ch.mark(pool.tensor_tensor(b[:, :, 0:32], z[:, :, 32:64],
                                           sin[:, 0:32].unsqueeze(1).broadcast_to([R, H, 32]), ALU.mult))
                ch(pool.tensor_tensor(b[:, :, 32:64], z[:, :, 0:32],
                                      sin[:, 32:64].unsqueeze(1).broadcast_to([R, H, 32]), ALU.mult))
                if n >= 2:
                    pool.wait_ge(s_rp, n - 1)
                if w == 256:
                    if n >= 2:
                        pool.wait_ge(s_krd[n % 2], 16 * (n // 2))
                    pool.tensor_tensor(rk[0:R, n % 2, 0:w], tr[0:R, 0, 0:w], tr[0:R, 1, 0:w], ALU.add
                                       ).then_inc(s_rot, 1)
                else:
                    if n < NT + 2:
                        pool.wait_ge(s_krd[0], 16 * 5)
                        pool.wait_ge(s_krd[1], 16 * 4)
                    for p in range(2):
                        sl = slice(p * 256, p * 256 + 256)
                        ins = pool.tensor_tensor(
                            rk[0:R, n % 2, sl].rearrange("p (g k n) -> p k g n", g=2, k=2),
                            tr[0:R, 0, sl].rearrange("p (k g n) -> p k g n", g=2, k=2),
                            tr[0:R, 1, sl].rearrange("p (k g n) -> p k g n", g=2, k=2), ALU.add)
                        if p == 0:
                            ch.mark(ins)
                        else:
                            ch(ins)
                    pool.engine_nop().then_inc(s_rot, 1)

            for t in range(NT):
                rotate(t, t, 256)
            for t in range(NT):
                rotate(NT + t, t, 512)
            for c in range(2):
                for part in range(3):
                    a = 512 * part
                    if part < 2:
                        dst, src, n = CB[:, c, a:a + 512], lambda j: UP[:, c, a + j:a + j + 512], 512
                    else:
                        dst, src, n = (CB[:, c, SEQ:TOK].rearrange("p (b s) -> p b s", b=DB),
                                       lambda j: US[:, c, :, j:j + DT], NS)
                    a0, a1 = tr[:, 0, 0:n], tr[:, 1, 0:n]
                    if part == 2:
                        a0, a1 = (x.rearrange("p (b s) -> p b s", b=DB) for x in (a0, a1))
                    ch(pool.tensor_scalar(a0, src(0), w0[:, 0, c:c + 1], None, ALU.mult))
                    ch(pool.tensor_scalar(a1, src(1), w0[:, 1, c:c + 1], None, ALU.mult))
                    ch(pool.tensor_tensor(a0, a0, a1, ALU.add))
                    ch(pool.tensor_scalar(a1, src(2), w0[:, 2, c:c + 1], None, ALU.mult))
                    ch(pool.tensor_tensor(a0, a0, a1, ALU.add))
                    ch(pool.tensor_tensor(dst, dst, a0, ALU.mult))
            pool.engine_nop().then_inc(s_cv, 1)
            pool.wait_ge(s_fp, 12)
            pool.wait_ge(s_up, 3 * NT)
            ch(pool.tensor_copy(YT[:, 0:2, :], CB))
            pool.engine_nop().then_inc(s_cv, 1)
            pool.wait_ge(s_co, 64)
            ch(pool.memset(st(0), 0.0))
            pool.memset(at("U", 0, 2048), 0.0).then_inc(s_hz, 1)
            pool.wait_ge(s_sg, 1)
            ch(pool.tensor_scalar(KK, GF, -1.0, 1.0, ALU.mult, ALU.add))
            for c in range(2):
                ch.mark(pool.tensor_scalar(KK[:, c, :], KK[:, c, :], e["oml"][:, c:c + 1], None, ALU.mult))
                ch.mark(pool.tensor_scalar(GF[:, c, :], GF[:, c, :], e["oml"][:, c:c + 1], e["lb"][:, c:c + 1],
                                           ALU.mult, ALU.add))
            ch.wait()
            pool.engine_nop().then_inc(s_kk, 1)
            pool.wait_ge(s_b, 1)
            for c in range(2):
                for v, n, m in ((slice(0, SEQ), NT - 1, P), (slice(SEQ, TOK), DB, DT)):
                    bv = BB[:, c, v].rearrange("p (n m) -> p n m", m=m)
                    ch.mark(pool.tensor_tensor(KH[:, c, v].rearrange("p (n m) -> p n m", m=m),
                                               bv[:, :, m - 1:m].broadcast_to([P, n, m]), bv, ALU.subtract))
            ch.wait()
            pool.engine_nop().then_inc(s_D, 1)
            pool.wait_ge(s_E, 2)
            ch.mark(pool.tensor_tensor(QT, GQ, E0, ALU.mult))
            ch(pool.tensor_tensor(KH, KK, KH, ALU.mult))
            pool.engine_nop().then_inc(s_qs, 1)
            for g, (ta, tb) in enumerate(HG_GROUPS):
                w = min(tb * P, TOK) - ta * P

                def views(n, x, c0):
                    m = LEVELS[n - 1]
                    ww = w if m < DT or g < 2 else 2 * P
                    return [x[:, c, c0:c0 + ww].rearrange("p (n a m) -> p n a m", a=2, m=m) for c in range(2)]

                def diff(n):
                    m = LEVELS[n - 1]
                    out, b = views(n, GL[n % 2], 0), views(n, BB, ta * P)
                    for c in range(2):
                        nb = b[c].shape[1]
                        ref = b[c][:, :, 0, m - 1:m].broadcast_to([P, nb, m])
                        ch.mark(pool.tensor_tensor(out[c][:, :, 0, :], ref, b[c][:, :, 0, :], ALU.subtract))
                        ch.mark(pool.tensor_tensor(out[c][:, :, 1, :], b[c][:, :, 1, :], ref, ALU.subtract))
                    ch.wait()
                    pool.engine_nop().then_inc(s_D, 1)

                def mult(n):
                    out, k, q = views(n, GL[n % 2], 0), views(n, KK, ta * P), views(n, GQ, ta * P)
                    for c in range(2):
                        ch.mark(pool.tensor_tensor(out[c][:, :, 0, :], out[c][:, :, 0, :], k[c][:, :, 0, :], ALU.mult))
                        ch.mark(pool.tensor_tensor(out[c][:, :, 1, :], out[c][:, :, 1, :], q[c][:, :, 1, :], ALU.mult))
                    ch.wait()
                    pool.engine_nop().then_inc(s_G, 1)

                for n in range(8):
                    if n < 7:
                        if n >= 2:
                            pool.wait_ge(s_ap, products_until(g, n - 1))
                        elif g:
                            pool.wait_ge(s_ap, products_until(g - 1, 7 - n))
                        diff(n + 1)
                    if n:
                        pool.wait_ge(s_E, 2 + 7 * g + n)
                        mult(n)
            for h in range(4):
                if h == 0:
                    pool.wait_ge(s_hin, 16)
                else:
                    pool.wait_ge(s_pp, NT - 1 + h)
                pool.tensor_tensor(VB[0:NS], GI[0:NS, NT - 1, h * HD:(h + 1) * HD].unsqueeze(1).broadcast_to([NS, DB, HD]),
                                   e["cs"]("batch")[0:NS].unsqueeze(2).broadcast_to([NS, DB, HD]), ALU.mult
                                   ).then_inc(s_vb, 1)
            pool.wait_ge(s_oe, NT)
            for c in range(2):
                ch.mark(pool.tensor_scalar(GG[:, c, :], GG[:, c, :], hgn[:, c:c + 1], None, ALU.mult))
            ch.wait()
            pool.wait_ge(s_n1, 1)
            pool.tensor_tensor(YT[:, 2:4, :], YT[:, 2:4, :], GG, ALU.mult).then_inc(s_n4, 1)
            keep(e, ch, "pool")

        @block.vector
        def _(dve):
            ch = chains(e, dve, "dve")
            jobs, soff = score_jobs()
            sel = [(off, w, P, t * (t + 1) // 2 * P) for off, t, _, w in jobs[:6]] + [(soff, LS, NS, 4608)]
            top = e["stat"][:, 0:8]

            def rounds(x, count):
                off, w, R, _ = x
                s = S[0:R, off:off + w]
                for k in range(count):
                    dve.max(top[0:R], s).then_inc(s_k1, 1)
                    dve.wait_ge(s_k1, k + 1)
                    dve.match_replace(s, top[0:R], s, GONE).then_inc(s_k2, 1)
                    dve.wait_ge(s_k2, k + 1)
                dve.sem_clear(s_k1)
                dve.sem_clear(s_k2)

            def mark_picked(x):
                off, w, R, moff = x
                ch.mark(dve.tensor_scalar(M16[0:R, moff:moff + w], S[0:R, off:off + w], PICKED, NEG,
                                          ALU.is_gt, ALU.mult))

            ch.mark(dve.tensor_copy(M16[:, 0:P], e["causal"]))
            ch.mark(dve.memset(M16[:, P:2 * P], 0.0))
            ch.mark(dve.tensor_copy(M16[:, 2 * P:3 * P], e["causal"]))
            for x in sel[:5]:
                with dve.Fori(0, TOPK // 8 // 4) as _:
                    rounds(x, 4)
                mark_picked(x)
            with dve.Fori(0, TOPK // 8 // 8) as _:
                rounds(sel[6], 4)
            dve.wait_ge(s_lf, 1)
            dve.wait_ge(s_fp, 12)
            dve.wait_ge(s_up, 3 * NT)
            for c in range(2):
                ins = dve.tensor_tensor_scan(BB[:, c, :], e["start16"], GF[:, c, :], 0.0, ALU.mult, ALU.add)
            ins.then_inc(s_b, 1)
            na = 0
            dve.wait_ge(s_hz, 1)
            for g, (ta, tb) in enumerate(HG_GROUPS):
                for n in range(8):
                    m = LEVELS[n - 1] if n else 0
                    for t in range(ta, tb):
                        if t == NT - 1 and m >= DT:
                            continue
                        R = rows(t)
                        dve.wait_ge(s_ap, na + 1)
                        if g and n == 0:
                            dve.wait_ge(s_op, t - 2)
                        src = ps[:, 1024 * (na % 2):1024 * (na % 2) + 1024].rearrange("p (b s) -> p b s", b=2)
                        out = att[:, slot(t), :].rearrange("p (b s) -> p b s", b=2)
                        for b in range(2):
                            ins = dve.copy_predicated(
                                out[0:R, b, :].rearrange("p (c s) -> p c s", c=2)[:, :, 0:R],
                                lvl(n)[0:R, 0:R].unsqueeze(1).broadcast_to([R, 2, R]),
                                src[0:R, b, 0:256].rearrange("p (c s) -> p c s", c=2)[:, :, 0:R])
                        ins.then_inc(s_ad, 1)
                        na += 1
                    if g == 0:
                        rounds(sel[6], TOPK // 8 // 16)
                    else:
                        rounds(sel[5], TOPK // 8 // 16)
                for t in range(ta, tb):
                    if t < NT - 1:
                        dve.wait_ge(s_pp, t + 1)
                        if t == 0:
                            dve.wait_ge(s_E, 1)
                        if t >= 1:
                            dve.wait_ge(s_op, t)
                            dve.wait_ge(s_sv, t)
                        for c in range(2):
                            ins = dve.scalar_tensor_tensor(st(t + 1)[:, c, :], st(t)[:, c, :],
                                                           E0[:, c, t * P + P - 1:t * P + P],
                                                           bank(7)[:, c * HD:(c + 1) * HD], ALU.mult, ALU.add)
                            if c == 0:
                                ch.mark(ins)
                        ins.then_inc(s_sv, 1)
                    else:
                        dve.wait_ge(s_op, NT)
                        for c in range(2):
                            x = S0[:, :, c, :]
                            last = E0[:, c, SEQ:TOK].rearrange("p (b s) -> p b s", b=DB)[:, :, DT - 1:DT]
                            ch(dve.tensor_tensor(x, x, last.broadcast_to([P, DB, HD]), ALU.mult))
                        dve.wait_ge(s_pp, NT - 1 + 4)
                        for c in range(2):
                            x = S0[:, :, c, :]
                            ins = dve.tensor_tensor(x, x, bank((7, 4)[c]).rearrange("p (b s) -> p b s", b=DB), ALU.add)
                            if c == 0:
                                ch.mark(ins)
                        ins.then_inc(s_sv, 1)
            dve.wait_ge(s_n3, 1)
            ch.wait()
            for c in range(2):
                ch(dve.tensor_tensor(QT[:, c, :], KH[:, c, :], E0[:, c, :], ALU.mult))
                ch(dve.scalar_tensor_tensor(QT[:, c, :], QT[:, c, :], -0.5, KH[:, c, :], ALU.mult, ALU.mult))
                ch(dve.scalar_tensor_tensor(QT[:, c, :], QT[:, c, :], 1.5, KH[:, c, :], ALU.add, ALU.mult))
            dve.wait_ge(s_n4, 1)
            ch(dve.tensor_tensor(YT[:, 2:4, :], YT[:, 2:4, :], QT, ALU.mult))
            for x in sel[5:]:
                mark_picked(x)
            ch.wait()
            keep(e, ch, "dve")


def attend_block(e):
    nc, i, o, at, bank, tcol, sem, layer = (e[k] for k in ("nc", "i", "o", "at", "bank", "tcol", "sem", "layer"))
    ident, ident16, ps = e["ident"], e["ident16"], e["ps"]
    qT, kT, V = at("X", 0, 4, TOK), at("X", 4 * TOK, 2, TOK), at("X", 6 * TOK, NT, 256)
    YT = at("A", 0, KC, TOK)
    M16 = at("M", 0, 2304 + LS // 2).bitcast(BF16)
    KC_ = [at("W", 4096 * n, 2, PAST) for n in range(2)]
    VC = [at("C", 4096 * n, NPG, 256) for n in range(2)]
    Pb, PT = at("S", 0, 2, SEQ), at("S", 2 * SEQ, 2, SEQ)
    PS, PTS = at("S", 4 * SEQ, LS), at("G", 0, NPG + 1, P)
    yo, QA = at("U", 0, 2, 512), at("U", 1024, DB, 2, 32)
    RS, NM, RI = e["stat"][:, 0:16], e["stat"][:, 16:18], e["stat"][:, 24:40]
    nsteps = (NT - 1) * NH

    s_kc, s_vc = [sem(f"k_cached{n}") for n in range(2)], [sem(f"v_cached{n}") for n in range(2)]
    s_ss, s_mx, s_ex, s_tg, s_ga, s_gd, s_pv, s_on = (sem(n) for n in (
        "s_done", "s_max", "s_exp", "p_turned", "p_copied_act", "p_copied_dve", "pv_done", "o_scaled"))
    s_qz, s_qa = sem("qa_zeroed"), sem("qa_ready")
    s_zs, s_zm, s_ze, s_zn, s_zt, s_zp, s_zo = (sem(n) for n in (
        "ss_done", "ss_max", "ss_exp", "ss_scaled", "ss_turned", "ss_pv", "ss_out"))
    s_zt_copied = sem("ss_turned_copied")

    groups, by_step = [], {}
    for n in range(nsteps + 1):
        mine = []
        if n < nsteps:
            for j0 in range(0, n // NH + 1, 4):
                mine.append(("p", n, j0, min(4, n // NH + 1 - j0)))
        if n % NH == 0 and n:
            mine.append(("y", n // NH - 1, 0, 4))
        by_step[n] = [(len(groups) + k, g) for k, g in enumerate(mine)]
        groups += mine
    ngp = len(groups)

    def values_in(eng, b):
        for_pages(eng, e, b, lambda pg, page: eng.dma_start(
            VC[b % 2][:, bass.ds(pg, 1), :].rearrange("p a n -> p (a n)"),
            i["cache_v"][page].rearrange("n s d -> (n s) d")).then_inc(s_vc[b % 2], 16))

    def waits_group(eng, q):
        eng.wait_ge((s_ga, s_gd)[q % 2], q // 2 + 1)

    def copy_group(eng, copy, q, g):
        eng.wait_ge(s_tg, q + 1)
        kind, n, j0, cnt = g
        if kind == "p":
            if n >= 2:
                eng.wait_ge(s_pv, n - 1)
            ins = copy(PT[:, n % 2, j0 * P:(j0 + cnt) * P], bank(4 + q % 2, cnt * P))
        else:
            ins = copy(YT[:, 4:8, tcol(n)], bank(4 + q % 2).rearrange("p (c s) -> p c s", c=4))
        ins.then_inc((s_ga, s_gd)[q % 2], 1)

    with nc.Block() as block:
        @block.sync
        def _(sp):
            for b in range(DB):
                if b >= 2:
                    sp.wait_ge(s_zs, b // 2)
                for_pages(sp, e, b, lambda pg, page: sp.dma_start(
                    KC_[b % 2][:, :, bass.ds(pg * PAGE, PAGE)],
                    i["kT"][page].rearrange("n (c p) s -> p (n c) s", c=2)).then_inc(s_kc[b % 2], 16))
                if b < 2:
                    values_in(sp, b)

        @block.tensor
        def _(pe):
            def scores(n):
                t, h = divmod(n, NH)
                W = (t + 1) * P
                kv, g = divmod(h, 2)
                part = slice(64 * (kv % 2), 64 * (kv % 2) + 64)
                if n >= 2:
                    pe.wait_ge(s_ex, n - 1)
                m0 = t * (t + 1) // 2 * P
                for a in range(0, W, 512):
                    b = min(a + 512, W)
                    out = ps[:, (n % 2) * 1024 + a:(n % 2) * 1024 + b]
                    pe.matmul(out, ident16, M16[:, m0 + a:m0 + b], start=True, stop=False)
                    ins = pe.matmul(out, qT[part, (kv // 2) * 2 + g, tcol(t)], kT[part, kv // 2, a:b],
                                    start=False, stop=True)
                ins.then_inc(s_ss, 1)

            scores(0)
            for n in range(nsteps + 1):
                if n + 1 < nsteps:
                    scores(n + 1)
                for q, (kind, x, j0, cnt) in by_step[n]:
                    if q >= 2:
                        waits_group(pe, q - 2)
                    if kind == "p":
                        pe.wait_ge(s_ex, n + 1)
                        for k in range(cnt):
                            ins = pe.transpose(bank(4 + q % 2)[:, k * P:(k + 1) * P],
                                               Pb[:, n % 2, (j0 + k) * P:(j0 + k + 1) * P], ident)
                    else:
                        pe.wait_ge(s_on, x + 1)
                        for k in range(4):
                            ins = pe.transpose(bank(4 + q % 2)[:, k * P:(k + 1) * P],
                                               yo[:, x % 2, k * P:(k + 1) * P], ident)
                    ins.then_inc(s_tg, 1)
                if n < nsteps:
                    t, h = divmod(n, NH)
                    if h == 0 and t >= 2:
                        pe.wait_ge(s_on, t - 1)
                    for q, (kind, x, j0, cnt) in by_step[n]:
                        if kind != "p":
                            continue
                        waits_group(pe, q)
                        for j in range(j0, j0 + cnt):
                            ins = pe.matmul(bank(6 + t % 2)[:, h * HD:(h + 1) * HD], PT[:, n % 2, j * P:(j + 1) * P],
                                            V[:, j, (h // 2) * HD:(h // 2 + 1) * HD],
                                            start=(j == 0), stop=(j == t))
                    ins.then_inc(s_pv, 1)
            pe.wait_ge(s_qa, 1)
            pe.wait_ge(s_ga, (ngp + 1) // 2)
            pe.wait_ge(s_gd, ngp // 2)
            pe.wait_ge(s_on, NT - 1)
            for bp in range(DB // 2):
                for n in range(2):
                    pe.wait_ge(s_kc[n], 16 * NPG * (bp + 1))
                if bp:
                    pe.wait_ge(s_ze, bp)
                for a in range(0, LS, 512):
                    b = min(a + 512, LS)
                    pe.matmul(ps[:, a:b], e["spread"][0:NS, bp, :], M16[0:NS, 4608 + a:4608 + b],
                              start=True, stop=False, skip_group_check=True)
                    for b2 in range(2):
                        for pair in range(2):
                            r0 = 32 * (2 * b2 + pair)
                            keys = KC_[b2][:, pair, a:b] if a < PAST else kT[:, pair, SEQ:TOK]
                            ins = pe.matmul(ps[r0:r0 + 32, a:b], QA[:, 2 * bp + b2, pair, :], keys,
                                            start=False, stop=True, skip_group_check=True)
                ins.then_inc(s_zs, 1)
                pe.wait_ge(s_zn, bp + 1)
                for g in range(5):
                    cnt = min(4, NPG + 1 - 4 * g)
                    if 5 * bp + g >= 2:
                        pe.wait_ge(s_zt_copied, 5 * bp + g - 1)
                    for k in range(cnt):
                        j = 4 * g + k
                        w = P if j < NPG else NS
                        ins = pe.transpose(bank(5 + (5 * bp + g) % 2)[0:w, k * P:(k + 1) * P],
                                           PS[:, j * P:j * P + w], ident)
                    ins.then_inc(s_zt, 1)
                pe.wait_ge(s_zt_copied, 5 * bp + 5)
                if bp:
                    pe.wait_ge(s_zo, bp)
                for b2 in range(2):
                    pe.wait_ge(s_vc[b2], 16 * NPG * (bp + 1))
                    for pair in range(2):
                        c0 = 32 * (2 * b2 + pair)
                        for j in range(NPG + 1):
                            if j < NPG:
                                lhs, rhs = VC[b2][:, j, pair * P:(pair + 1) * P], PTS[:, j, c0:c0 + 32]
                            else:
                                lhs, rhs = V[0:NS, NT - 1, pair * P:(pair + 1) * P], PTS[0:NS, j, c0:c0 + 32]
                            ins = pe.matmul(bank(7)[:, c0:c0 + 32], lhs, rhs, start=(j == 0), stop=(j == NPG))
                ins.then_inc(s_zp, 1)

        @block.scalar
        def _(act):
            def exp(n):
                W = (n // NH + 1) * P
                act.wait_ge(s_mx, n + 1)
                if n >= 2:
                    act.wait_ge(s_tg, max(q for q, g in by_step[n - 2] if g[0] == "p") + 1)
                if n % NH == 0 and n >= 2 * NH:
                    act.wait_ge(s_on, n // NH - 1)
                act.activation(Pb[:, n % 2, 0:W], ps[:, (n % 2) * 1024:(n % 2) * 1024 + W], ACT.Exp,
                               bias=NM[:, n % 2:n % 2 + 1],
                               accum_out=RS[:, (n // NH % 2) * 8 + n % NH:(n // NH % 2) * 8 + n % NH + 1]
                               ).then_inc(s_ex, 1)

            exp(0)
            for n in range(nsteps + 1):
                if n + 1 < nsteps:
                    exp(n + 1)
                for q, g in by_step[n]:
                    if q % 2 == 0:
                        copy_group(act, act.copy, q, g)
            for bp in range(DB // 2):
                act.wait_ge(s_zm, bp + 1)
                if bp:
                    act.wait_ge(s_zt, 5 * bp)
                act.activation(PS, ps[:, 0:LS], ACT.Exp, bias=NM[:, 0:1], accum_out=RS[:, 0:1]).then_inc(s_ze, 1)
                for g in range(5):
                    cnt, w = (4, P) if g < 4 else (1, NS)
                    act.wait_ge(s_zt, 5 * bp + g + 1)
                    if bp and g == 0:
                        act.wait_ge(s_zp, bp)
                    act.copy(PTS[0:w, 4 * g:4 * g + cnt, :].rearrange("p a b -> p (a b)"),
                             bank(5 + (5 * bp + g) % 2, cnt * P)[0:w]).then_inc(s_zt_copied, 1)
                if bp < DB // 2 - 1:
                    act.wait_ge(s_zp, bp + 1)
                    values_in(act, 2 * bp + 2)
                    values_in(act, 2 * bp + 3)

        @block.gpsimd
        def _(pool):
            pool.memset(at("U", 1024, DB * 64), 0.0).then_inc(s_qz, 1)

        @block.vector
        def _(dve):
            ch = chains(e, dve, "dve")
            dve.wait_ge(s_qz, 1)
            for k in range(2):
                part = slice(64 * k, 64 * k + 64)
                for pair in range(2):
                    for g in range(2):
                        c = k * 16 + g * 8
                        ch.mark(dve.tensor_copy(QA[part, :, pair, c:c + 8],
                                                qT[part, 2 * pair + g, SEQ:TOK].rearrange("p (b s) -> p b s", b=DB)))
            ch.wait()
            dve.engine_nop().then_inc(s_qa, 1)

            def rowmax(n):
                W = (n // NH + 1) * P
                dve.wait_ge(s_ss, n + 1)
                if n >= 2:
                    dve.wait_ge(s_ex, n - 1)
                dve.tensor_reduce(NM[:, n % 2:n % 2 + 1], ps[:, (n % 2) * 1024:(n % 2) * 1024 + W], AX, ALU.max,
                                  negate=True).then_inc(s_mx, 1)

            rowmax(0)
            for n in range(nsteps + 1):
                if n + 1 < nsteps:
                    rowmax(n + 1)
                if n and n % NH == 0:
                    t = n // NH - 1
                    rs, ri = RS[:, (t % 2) * 8:(t % 2) * 8 + 8], RI[:, (t % 2) * 8:(t % 2) * 8 + 8]
                    dve.wait_ge(s_pv, n)
                    dve.wait_ge(s_ex, n)
                    ch(dve.reciprocal(ri, rs))
                    if t >= 2:
                        y = next(q for q, g in enumerate(groups) if g[0] == "y" and g[1] == t - 2)
                        dve.wait_ge(s_tg, y + 1)
                    dve.tensor_tensor(yo[:, t % 2, :].rearrange("p (h d) -> p h d", h=NH),
                                      bank(6 + t % 2).rearrange("p (h d) -> p h d", h=NH),
                                      ri.unsqueeze(2).broadcast_to([P, NH, HD]), ALU.mult).then_inc(s_on, 1)
                for q, g in by_step[n]:
                    if q % 2:
                        copy_group(dve, dve.tensor_copy, q, g)
            for bp in range(DB // 2):
                dve.wait_ge(s_zs, bp + 1)
                dve.tensor_reduce(NM[:, 0:1], ps[:, 0:LS], AX, ALU.max, negate=True).then_inc(s_zm, 1)
                dve.wait_ge(s_ze, bp + 1)
                ch(dve.reciprocal(RI[:, 0:1], RS[:, 0:1]))
                dve.tensor_scalar(PS, PS, RI[:, 0:1], None, ALU.mult).then_inc(s_zn, 1)
                dve.wait_ge(s_zp, bp + 1)
                for k in range(2):
                    for g in range(2):
                        for b2 in range(2):
                            src = bank(7, P)[64 * k:64 * k + 64, 64 * b2:64 * b2 + 64].rearrange(
                                "p (a x s) -> p a x s", a=2, s=DT)[:, :, 2 * k + g, :]
                            s0 = SEQ + (2 * bp + b2) * DT
                            ins = dve.tensor_copy(YT[64 * g:64 * g + 64, 4 + k:8:2, s0:s0 + DT], src)
                            if (k, g, b2) != (1, 1, 1):
                                ch.mark(ins)
                ins.then_inc(s_zo, 1)
            dve.wait_ge(s_zo, DB // 2)
            keep(e, ch, "dve")


class Norm:

    def __init__(self, e, name, X, lnt):
        self.e, self.X, self.g, self.b = e, X, lnt[:, 0:D], lnt[:, D:2 * D]
        sem = e["sem"]
        self.in_, self.var, self.root, self.unit, self.ready = (
            sem(name + x) for x in ("_params", "_var", "_root", "_unit", "_ready"))
        self.st = e["stat"][:, 40:64].rearrange("p (a b) -> p a b", a=2)
        self.mv = e["stat"][:, 64:72]
        self.rt = e["stat"][:, 72:80]

    def load(self, sp, n, layer):
        sp.dma_start(self.g, lay(self.e["i"]["ln"], layer)[:, n, :].broadcast_to([P, D])).then_inc(self.in_, 16)
        sp.dma_start(self.b, lay(self.e["i"]["ln"], layer)[:, n + 1, :].broadcast_to([P, D])).then_inc(self.in_, 16)

    def stats(self, ch, dve, t):
        R, k = rows(t), t % 2
        for a in range(2):
            ins = dve.bn_stats(self.st[0:R, k, 6 * a:6 * a + 6], self.X[0:R, t, 512 * a:512 * a + 512])
            ch.mark(ins)
        ch.wait()
        mv = self.mv[0:R, 4 * k:4 * k + 4]
        ch(dve.bn_aggr(mv[:, 0:2], self.st[0:R, k, :]))
        dve.tensor_scalar(mv[:, 2:3], mv[:, 1:2], EPS, None, ALU.add).then_inc(self.var, 1)

    def act(self, act, ch, t):
        R, k = rows(t), t % 2
        act.wait_ge(self.var, t + 1)
        ch(act.activation(self.rt[0:R, 4 * k:4 * k + 1], self.mv[0:R, 4 * k + 2:4 * k + 3], ACT.Ln))
        act.activation(self.rt[0:R, 4 * k + 1:4 * k + 2], self.rt[0:R, 4 * k:4 * k + 1], ACT.Exp,
                       scale=-0.5).then_inc(self.root, 1)

    def unit_rows(self, ch, dve, t):
        R, k = rows(t), t % 2
        v, r = self.mv[0:R, 4 * k + 2:4 * k + 3], self.rt[0:R, 4 * k + 1:4 * k + 2]
        a, b = self.rt[0:R, 4 * k + 2:4 * k + 3], self.rt[0:R, 4 * k + 3:4 * k + 4]
        dve.wait_ge(self.root, t + 1)
        ch(dve.scalar_tensor_tensor(a, r, v, r, ALU.mult, ALU.mult))
        ch(dve.tensor_scalar(a, a, -0.5, 1.5, ALU.mult, ALU.add))
        ch(dve.tensor_tensor(b, r, a, ALU.mult))
        x = self.X[0:R, t, :]
        dve.tensor_scalar(x, x, self.mv[0:R, 4 * k:4 * k + 1], b, ALU.subtract, ALU.mult).then_inc(self.unit, 1)

    def pool(self, ch, pool, t):
        R = rows(t)
        x = self.X[0:R, t, :]
        if t == 0:
            pool.wait_ge(self.in_, 32)
        pool.wait_ge(self.unit, t + 1)
        ch(pool.tensor_tensor(x, x, self.g[0:R], ALU.mult))
        pool.tensor_tensor(x, x, self.b[0:R], ALU.add).then_inc(self.ready, 1)


def out_block(e):
    nc, i, o, at, bank, tcol, sem, layer = (e[k] for k in ("nc", "i", "o", "at", "bank", "tcol", "sem", "layer"))
    ident, ps = e["ident"], e["ps"]
    X, YT = at("X", 0, NT, D), at("A", 0, KC, TOK)
    WO = at("W", 0, KC, D)
    MV, MKT = at(RR, 0, 2, 512), at(RR, 1024, XH, NMEM)
    MK = at(RR, 2048, 2, 512)
    MT = at(RR, 3072, KC, NMEM)
    WK, WV = at(RR, 5120, KC, 512), at(RR, 9216, KC, 512)
    ln = Norm(e, "ln1", X, at(RR, 13312, 2 * D))
    s_m = [sem(f"mem_in{n}") for n in range(3)]
    s_wo, s_xi = [sem(f"w_out{n}") for n in range(2)], [sem(f"x_back{n}") for n in range(2)]
    s_mp, s_me, s_mt, s_mte, s_mo = (sem(n) for n in ("mem_done", "mem_copied", "mem_turned", "mem_turn_copied", "mem_out"))
    s_op, s_oa, s_ht, s_he = (sem(n) for n in ("out_done", "out_added", "h_turned", "h_copied"))

    with nc.Block() as block:
        @block.sync
        def _(sp):
            w = lambda n: lay(i[n], layer).rearrange("l (k p) n -> p (l k) n", p=P)
            sp.dma_start(MT, i["memT"].rearrange("(k p) m -> p k m", p=P)).then_inc(s_m[0], 16)
            sp.dma_start(WK, w("w_xk")).then_inc(s_m[1], 16)
            sp.dma_start(WV, w("w_xv")).then_inc(s_m[2], 16)
            for n in range(2):
                sp.dma_start(WO[:, 4 * n:4 * n + 4, :], w("w_out")[:, 4 * n:4 * n + 4, :]).then_inc(s_wo[n], 16)
            sp.dma_start(X[:, 0:NT - 1, :], o["y_prompt"][0].rearrange("(t p) d -> p t d", p=P)).then_inc(s_xi[0], 16)
            sp.dma_start(X[0:NS, NT - 1, :], o["y_sample"].rearrange("b t d -> (b t) d")).then_inc(s_xi[1], 16)
            ln.load(sp, 0, layer)
            sp.wait_ge(s_me, 4)
            sp.dma_start(lay(o["mem_k"], layer).rearrange("l b (m p) d -> p (l b m) d", p=P), MK).then_inc(s_mo, 16)
            sp.dma_start(lay(o["mem_v"], layer).rearrange("l b (m p) d -> p (l b m) d", p=P), MV).then_inc(s_mo, 16)
            sp.wait_ge(s_mo, 32)

        @block.tensor
        def _(pe):
            pe.wait_ge(s_m[0], 16)
            for n in range(4):
                w = (WK, WV)[n // 2]
                if n % 2 == 0:
                    pe.wait_ge(s_m[1 + n // 2], 16)
                for k in range(KC):
                    ins = pe.matmul(bank(n), MT[:, k, (n % 2) * P:(n % 2 + 1) * P], w[:, k, :],
                                    start=(k == 0), stop=(k == KC - 1))
                ins.then_inc(s_mp, 1)
            for m in range(2):
                pe.wait_ge(s_me, m + 1)
                for h in range(XH):
                    ins = pe.transpose(bank(4 + m)[:, h * P:(h + 1) * P], MK[:, m, h * P:(h + 1) * P], ident)
                ins.then_inc(s_mt, 1)
            pe.wait_ge(s_me, 4)
            pe.wait_ge(s_mte, 2)

            def turn(t):
                R = rows(t)
                pe.wait_ge(ln.ready, t + 1)
                if t:
                    pe.wait_ge(s_he, 2 * t)
                for half in range(2):
                    for c in range(4):
                        k = 4 * half + c
                        ins = pe.transpose(bank(4 + half)[:, c * P:c * P + R], X[0:R, t, k * P:(k + 1) * P],
                                           ident[0:R, 0:R])
                    ins.then_inc(s_ht, 1)

            for t in range(NT):
                R = rows(t)
                if t >= 2:
                    pe.wait_ge(s_oa, t - 1)
                for k in range(KC):
                    if t == 0 and k % 4 == 0:
                        pe.wait_ge(s_wo[k // 4], 16)
                    for a in range(2):
                        ins = pe.matmul(bank(2 * (t % 2) + a)[0:R, :], YT[:, k, tcol(t)], WO[:, k, 512 * a:512 * a + 512],
                                        start=(k == 0), stop=(k == KC - 1))
                ins.then_inc(s_op, 1)
                if t >= 2:
                    turn(t - 2)
            turn(NT - 2)
            turn(NT - 1)

        @block.scalar
        def _(act):
            ch = chains(e, act, "act")
            for n in range(4):
                act.wait_ge(s_mp, n + 1)
                act.copy((MK, MV)[n // 2][:, n % 2, :], bank(n)).then_inc(s_me, 1)
            for m in range(2):
                act.wait_ge(s_mt, m + 1)
                act.copy(MKT[:, :, m * P:(m + 1) * P], bank(4 + m).rearrange("p (h s) -> p h s", h=XH)
                         ).then_inc(s_mte, 1)

            def hcopy(t):
                for half in range(2):
                    act.wait_ge(s_ht, 2 * t + half + 1)
                    act.copy(YT[:, 4 * half:4 * half + 4, tcol(t)],
                             bank(4 + half).rearrange("p (c s) -> p c s", c=4)[:, :, 0:rows(t)]).then_inc(s_he, 1)

            for t in range(NT):
                ln.act(act, ch, t)
                if t >= 2:
                    hcopy(t - 2)
            hcopy(NT - 2)
            hcopy(NT - 1)
            keep(e, ch, "act")

        @block.gpsimd
        def _(pool):
            ch = chains(e, pool, "pool")
            for t in range(NT):
                ln.pool(ch, pool, t)
            keep(e, ch, "pool")

        @block.vector
        def _(dve):
            ch = chains(e, dve, "dve")
            dve.wait_ge(s_xi[0], 16)
            dve.wait_ge(s_xi[1], 16)
            for t in range(NT + 1):
                if t < NT:
                    R = rows(t)
                    dve.wait_ge(s_op, t + 1)
                    ins = dve.scalar_tensor_tensor(X[0:R, t, :], X[0:R, t, :], ALPHA,
                                                   ps[0:R, 1024 * (t % 2):1024 * (t % 2) + 1024], ALU.mult, ALU.add)
                    ins.then_inc(s_oa, 1)
                    dve.wait_ge(s_oa, t + 1)
                    ln.stats(ch, dve, t)
                if t:
                    ln.unit_rows(ch, dve, t - 1)
            keep(e, ch, "dve")


def cross_block(e):
    nc, i, o, at, bank, tcol, sem, layer = (e[k] for k in ("nc", "i", "o", "at", "bank", "tcol", "sem", "layer"))
    ident, ps = e["ident"], e["ps"]
    X, HT = at("X", 0, NT, D), at("A", 0, KC, TOK)
    WQ, WO = at("W", 0, KC, 512), at("W", 4096, 4, D)
    MV, MKT = at(RR, 0, 2, 512), at(RR, 1024, XH, NMEM)
    QX = at(RR, 2048, XH, TOK)
    r0 = 2048 + XH * TOK
    QM = at(RR, r0, DB, XH, NS)
    SK = [at(RR, r0 + 2048 + 1024 * n, XH, NMEM) for n in range(2)]
    SV = [at(RR, r0 + 4096 + 1024 * n, 2, 512) for n in range(2)]
    Pb, PT = at(RR, r0 + 6144, 2, XH * NMEM), at(RR, r0 + 8192, 2 * XH, P)
    OT = at(RR, r0 + 9216, XH, P)
    ln = Norm(e, "ln2", X, at(RR, r0 + 9728, 2 * D))
    NM, RS, RI = e["stat"][:, 0:8], e["stat"][:, 8:16], e["stat"][:, 16:24]
    s_wq, s_wo = sem("w_xq"), sem("w_xo")
    s_sk, s_sv = [sem(f"mem_keys{n}") for n in range(2)], [sem(f"mem_values{n}") for n in range(2)]
    s_qp, s_qe, s_qz, s_qm = (sem(n) for n in ("xq_done", "xq_copied", "xq_zeroed", "xq_masked"))
    s_sp, s_sb, s_mx, s_ex, s_pn, s_tp, s_te, s_pv, s_pe, s_xp, s_xa, s_ht, s_he, s_vb = (sem(n) for n in (
        "xs_done", "xs_batch", "xs_max", "xs_exp", "xp_scaled", "xp_turned", "xp_copied", "xo_done", "xo_copied",
        "xproj_done", "xproj_added", "h2_turned", "h2_copied", "xv_batch"))

    with nc.Block() as block:
        @block.sync
        def _(sp):
            sp.dma_start(WQ, lay(i["w_xq"], layer).rearrange("l (k p) n -> p (l k) n", p=P)).then_inc(s_wq, 16)
            sp.dma_start(WO, lay(i["w_xo"], layer).rearrange("l (k p) n -> p (l k) n", p=P)).then_inc(s_wo, 16)
            ln.load(sp, 2, layer)
            for b in range(DB):
                if b >= 2:
                    sp.wait_ge(s_sb, b - 1)
                sp.dma_start(SK[b % 2], lay(i["mem_kT"], layer)[:, b].rearrange("l h d m -> d (l h) m")
                             ).then_inc(s_sk[b % 2], 16)
                if b < 2:
                    sp.dma_start(SV[b % 2], lay(i["mem_v"], layer)[:, b].rearrange("l (a p) d -> p (l a) d", p=P)
                                 ).then_inc(s_sv[b % 2], 16)
            for b in range(2, DB):
                sp.wait_ge(s_vb, b - 1)
                sp.dma_start(SV[b % 2], lay(i["mem_v"], layer)[:, b].rearrange("l (a p) d -> p (l a) d", p=P)
                             ).then_inc(s_sv[b % 2], 16)

        @block.tensor
        def _(pe):
            pe.wait_ge(s_wq, 16)
            for c in range(XH):
                if c >= 2:
                    pe.wait_ge(s_qe, c - 1)
                for k in range(KC):
                    for a, b in ((0, 512), (512, 1024), (1024, TOK)):
                        ins = pe.matmul(ps[:, (c % 2) * 1536 + a:(c % 2) * 1536 + b], WQ[:, k, c * P:(c + 1) * P],
                                        HT[:, k, a:b], start=(k == 0), stop=(k == KC - 1))
                ins.then_inc(s_qp, 1)
            pe.wait_ge(s_qe, XH)

            def scores(t):
                R = rows(t)
                if t:
                    pe.wait_ge(s_ex, t)
                if t < NT - 1:
                    for h in range(XH):
                        ins = pe.matmul(ps[:, h * NMEM:(h + 1) * NMEM], QX[:, h, tcol(t)], MKT[:, h, :],
                                        start=True, stop=True)
                else:
                    pe.wait_ge(s_qm, 1)
                    for b in range(DB):
                        pe.wait_ge(s_sk[b % 2], 16 * (b // 2 + 1))
                        for h in range(XH):
                            ins = pe.matmul(ps[0:R, h * NMEM:(h + 1) * NMEM], QM[:, b, h, :], SK[b % 2][:, h, :],
                                            start=(b == 0 and h % 2 == 0), stop=(b == DB - 1),
                                            skip_group_check=True)
                        ins.then_inc(s_sb, 1)
                ins.then_inc(s_sp, 1) if t < NT - 1 else None

            def turn(t):
                R = rows(t)
                pe.wait_ge(ln.ready, t + 1)
                for half in range(2):
                    if 2 * t + half >= 1:
                        pe.wait_ge(s_he, 2 * t + half)
                    for c in range(4):
                        k = 4 * half + c
                        ins = pe.transpose(bank(7)[:, c * P:c * P + R], X[0:R, t, k * P:(k + 1) * P], ident[0:R, 0:R])
                    ins.then_inc(s_ht, 1)

            scores(0)
            for t in range(NT):
                R = rows(t)
                if t + 1 < NT:
                    scores(t + 1)
                pe.wait_ge(s_pn, t + 1)
                if t:
                    pe.wait_ge(s_te, t)
                for n in range(8):
                    ins = pe.transpose(bank(2 + n // 4)[:, (n % 4) * P:(n % 4) * P + R],
                                       Pb[0:R, t % 2, n * P:(n + 1) * P], ident[0:R, 0:R])
                ins.then_inc(s_tp, 1)
                pe.wait_ge(s_te, t + 1)
                if t:
                    pe.wait_ge(s_pe, t)
                if t < NT - 1:
                    for h in range(XH):
                        for a in range(2):
                            ins = pe.matmul(bank(4)[:, h * P:(h + 1) * P], MV[:, a, h * P:(h + 1) * P],
                                            PT[:, 2 * h + a, :], start=(a == 0), stop=(a == 1))
                    ins.then_inc(s_pv, 1)
                else:
                    for b in range(DB):
                        pe.wait_ge(s_sv[b % 2], 16 * (b // 2 + 1))
                        for h in range(XH):
                            for a in range(2):
                                ins = pe.matmul(bank(4)[:, h * P + b * DT:h * P + (b + 1) * DT],
                                                SV[b % 2][:, a, h * P:(h + 1) * P],
                                                PT[:, 2 * h + a, b * DT:(b + 1) * DT], start=(a == 0), stop=(a == 1))
                        ins.then_inc(s_vb, 1)
                pe.wait_ge(s_pe, t + 1)
                if t == 0:
                    pe.wait_ge(s_wo, 16)
                else:
                    pe.wait_ge(s_xa, t)
                for k in range(XH):
                    for a in range(2):
                        ins = pe.matmul(bank(5 + a)[0:R, :], OT[:, k, 0:R], WO[:, k, 512 * a:512 * a + 512],
                                        start=(k == 0), stop=(k == XH - 1))
                ins.then_inc(s_xp, 1)
                if t:
                    turn(t - 1)
            turn(NT - 1)

        @block.scalar
        def _(act):
            ch = chains(e, act, "act")
            for c in range(XH):
                act.wait_ge(s_qp, c + 1)
                act.mul(QX[:, c, :], ps[:, (c % 2) * 1536:(c % 2) * 1536 + TOK], XD ** -0.5).then_inc(s_qe, 1)

            def exp(t):
                R, k = rows(t), t % 2
                act.wait_ge(s_mx, t + 1)
                if t >= 2:
                    act.wait_ge(s_tp, t - 1)
                for h in range(XH):
                    ins = act.activation(Pb[0:R, k, h * NMEM:(h + 1) * NMEM], ps[0:R, h * NMEM:(h + 1) * NMEM],
                                         ACT.Exp, bias=NM[0:R, 4 * k + h:4 * k + h + 1],
                                         accum_out=RS[0:R, 4 * k + h:4 * k + h + 1])
                ins.then_inc(s_ex, 1)

            def hcopy(t):
                for half in range(2):
                    act.wait_ge(s_ht, 2 * t + half + 1)
                    act.copy(HT[:, 4 * half:4 * half + 4, tcol(t)],
                             bank(7).rearrange("p (c s) -> p c s", c=4)[:, :, 0:rows(t)]).then_inc(s_he, 1)

            exp(0)
            for t in range(NT):
                R = rows(t)
                if t + 1 < NT:
                    exp(t + 1)
                act.wait_ge(s_tp, t + 1)
                if t:
                    act.wait_ge(s_pv, t)
                act.copy(PT[:, :, 0:R], ps[:, 1024:2048].rearrange("p (n s) -> p n s", n=8)[:, :, 0:R]
                         ).then_inc(s_te, 1)
                if t < NT - 1:
                    act.wait_ge(s_pv, t + 1)
                else:
                    act.wait_ge(s_vb, DB)
                if t:
                    act.wait_ge(s_xp, t)
                act.copy(OT[:, :, 0:R], bank(4).rearrange("p (h s) -> p h s", h=XH)[:, :, 0:R]).then_inc(s_pe, 1)
                ln.act(act, ch, t)
                if t:
                    hcopy(t - 1)
            hcopy(NT - 1)
            keep(e, ch, "act")

        @block.gpsimd
        def _(pool):
            ch = chains(e, pool, "pool")
            ch(pool.memset(at(RR, r0, DB * XH * NS), 0.0))
            pool.wait_ge(s_qe, XH)
            for b in range(DB):
                c = slice(b * DT, (b + 1) * DT)
                ch.mark(pool.tensor_copy(QM[:, b, :, c], QX[:, :, SEQ + b * DT:SEQ + (b + 1) * DT]))
            ch.wait()
            pool.engine_nop().then_inc(s_qm, 1)
            for t in range(NT):
                ln.pool(ch, pool, t)
            keep(e, ch, "pool")

        @block.vector
        def _(dve):
            ch = chains(e, dve, "dve")

            def rowmax(t):
                R, k = rows(t), t % 2
                if t < NT - 1:
                    dve.wait_ge(s_sp, t + 1)
                else:
                    dve.wait_ge(s_sb, DB)
                if t >= 2:
                    dve.wait_ge(s_ex, t - 1)
                dve.tensor_reduce(NM[0:R, 4 * k:4 * k + 4], ps[0:R, 0:1024].rearrange("p (h m) -> p h m", h=XH), AX,
                                  ALU.max, negate=True).then_inc(s_mx, 1)

            rowmax(0)
            for t in range(NT + 1):
                if t < NT:
                    R, k = rows(t), t % 2
                    dve.wait_ge(s_ex, t + 1)
                    ch(dve.reciprocal(RI[0:R, 4 * k:4 * k + 4], RS[0:R, 4 * k:4 * k + 4]))
                    p = Pb[0:R, k, :].rearrange("p (h m) -> p h m", h=XH)
                    dve.tensor_tensor(p, p, RI[0:R, 4 * k:4 * k + 4].unsqueeze(2).broadcast_to([R, XH, NMEM]),
                                      ALU.mult).then_inc(s_pn, 1)
                    if t + 1 < NT:
                        rowmax(t + 1)
                    dve.wait_ge(s_xp, t + 1)
                    dve.scalar_tensor_tensor(X[0:R, t, :], X[0:R, t, :], ALPHA, ps[0:R, 2560:3584],
                                             ALU.mult, ALU.add).then_inc(s_xa, 1)
                    dve.wait_ge(s_xa, t + 1)
                    ln.stats(ch, dve, t)
                if t:
                    ln.unit_rows(ch, dve, t - 1)
            keep(e, ch, "dve")


FFC = 2
FFG = DFF // (FFC * P)
FFN_RAW = KC * FFC * P + TOK
FFN_PARTS = 2 * (KC * TOK + FFC * TOK + FFC * D + KC * P)
SEG = [(0, 384), (384, 768), (768, TOK)]


def ffn_block(e):
    nc, i, o, at, bank, tcol, sem, layer = (e[k] for k in ("nc", "i", "o", "at", "bank", "tcol", "sem", "layer"))
    ps = e["ps"]
    X, HT = at("X", 0, NT, D), at("A", 0, KC, TOK)
    WU = [at(NHEAD, 0, KC, FFC * P), at("A", 0, KC, FFC * P)]
    WD = at("A", 2048, FFC, D)
    SQ = [at("A", 4096, TOK), at(NHEAD, 2048, TOK)]
    ln = Norm(e, "ln3", X, at("A", 4096 + TOK, 2 * D))
    parts, n = [], 0
    for c, w in ((KC, TOK), (FFC, TOK), (FFC, D), (KC, P)):
        parts.append([e["parts"][:, n + k * c * w:n + (k + 1) * c * w].rearrange("p (a b) -> p a b", a=c)
                      for k in range(2)])
        n += 2 * c * w
    (HH, HL), (UH, UL), (DH, DL), (WH, WL) = parts

    s_wu, s_wd = [sem(f"w_up{n}") for n in range(2)], sem("w_down")
    s_th, s_tl, s_hi, s_uh, s_dhi, s_dl = (sem(n) for n in (
        "h_high", "h_low", "w_up_high", "w_up_low", "w_down_high", "w_down_low"))
    s_ub, s_rl, s_sq, s_qh, s_ql, s_dn, s_ad, s_yo = (sem(n) for n in (
        "up_halves", "up_relu", "u_squared", "u_high", "u_low", "down_done", "down_added", "y_out"))
    UB0, DN0, AD0 = 2, 1, 2

    with nc.Block() as block:
        @block.sync
        def _(sp):
            wu = lay(i["w_up"], layer).rearrange("l (k p) n -> p (l k) n", p=P)
            wd = lay(i["w_down"], layer).rearrange("l (k p) n -> p (l k) n", p=P)

            def up_in(g, n):
                sp.dma_start(WU[n], wu[:, :, bass.ds(g * (FFC * P), FFC * P)]).then_inc(s_wu[n], 16)

            def down_in(g):
                sp.dma_start(WD, wd[:, bass.ds(g * FFC, FFC), :]).then_inc(s_wd, 16)

            up_in(0, 0)
            sp.wait_ge(s_tl, KC)
            down_in(0)
            ln.load(sp, 4, layer)
            up_in(1, 1)
            with sp.Fori(0, FFG // 2 - 1) as g2:
                for n in range(2):
                    sp.wait_ge(s_uh, g2 * (4 * FFC) + (n + 1) * (2 * FFC))
                    sp.nop()
                    up_in(g2 * 2 + (n + 2), n)
                    sp.wait_ge(s_dl, g2 * (2 * FFC) + (n + 1) * FFC)
                    sp.nop()
                    down_in(g2 * 2 + (n + 1))
            sp.wait_ge(s_dl, (FFG - 1) * FFC)
            down_in(FFG - 1)
            for t in range(NT):
                sp.wait_ge(ln.ready, t + 1)
                if t < NT - 1:
                    sp.dma_start(o["y_prompt"][0][tcol(t)], X[:, t, :]).then_inc(s_yo, 16)
                else:
                    sp.dma_start(o["y_sample"].rearrange("b t d -> (b t) d"), X[0:NS, t, :]).then_inc(s_yo, 16)
            sp.wait_ge(s_yo, 16 * NT)

        @block.tensor
        def _(pe):
            pe.wait_ge(s_tl, KC)
            with pe.Fori(0, FFG // 2) as g2:
                for n in range(2):
                    for c in range(FFC):
                        if c == 0:
                            pe.wait_ge(s_ad, g2 * (2 * NT) + (n * NT + AD0 - 1))
                        for half in range(2):
                            pe.wait_ge(s_uh, g2 * (4 * FFC) + (2 * (FFC * n + c) + half + 1))
                            for k in range(4 * half, 4 * half + 4):
                                for w, h in ((WH, HH), (WH, HL), (WL, HH)):
                                    for b, (x, y) in enumerate(SEG):
                                        ins = pe.matmul(bank(3 * c + b, y - x), w[:, k, :], h[:, k, x:y],
                                                        start=(k == 0 and h is HH and w is WH),
                                                        stop=(k == KC - 1 and w is WL))
                            ins.then_inc(s_ub, 1)
                    pe.wait_ge(s_dl, g2 * (2 * FFC) + (n + 1) * FFC)
                    for t in range(NT):
                        R, b0 = rows(t), (6, 0)[t % 2]
                        if t % 3 == 0:
                            pe.wait_ge(s_ql, g2 * (6 * FFC) + (3 * (FFC * n + FFC - 1) + t // 3 + 1))
                        if t == 0:
                            pe.wait_ge(s_ad, g2 * (2 * NT) + (n * NT + AD0))
                        if t >= 2:
                            pe.wait_ge(s_ad, g2 * (2 * NT) + (n * NT + t - 1 + AD0))
                        for c in range(FFC):
                            for u, d in ((UH, DH), (UH, DL), (UL, DH)):
                                for a in range(2):
                                    ins = pe.matmul(bank(b0 + a)[0:R, :], u[:, c, tcol(t)],
                                                    d[:, c, 512 * a:512 * a + 512],
                                                    start=(c == 0 and u is UH and d is DH),
                                                    stop=(c == FFC - 1 and u is UL))
                        ins.then_inc(s_dn, 1)

        @block.scalar
        def _(act):
            ch = chains(e, act, "act")
            for k in range(KC):
                act.copy(HH[:, k, :], HT[:, k, :]).then_inc(s_th, 1)
            with act.Fori(0, FFG // 2) as g2:
                for n in range(2):
                    def up_high(c, half):
                        act.wait_ge(s_ub, g2 * (4 * FFC) + (2 * (FFC * n + c) + half - 1 + UB0))
                        ks = slice(4 * half, 4 * half + 4)
                        act.copy(WH[:, ks, :], WU[n][:, ks, c * P:(c + 1) * P]).then_inc(s_hi, 1)

                    def down_high(c):
                        act.copy(DH[:, c, :], WD[:, c, :]).then_inc(s_dhi, 1)

                    act.wait_ge(s_wu[n], g2 * 16 + 16)
                    up_high(0, 0)
                    up_high(0, 1)
                    act.wait_ge(s_wd, g2 * 32 + 16 * (n + 1))
                    act.wait_ge(s_dn, g2 * (2 * NT) + (n * NT + DN0))
                    down_high(0)
                    up_high(1, 0)
                    down_high(1)
                    up_high(1, 1)
                    for c in range(FFC):
                        def square_high(b):
                            x, y = SEG[b]
                            act.wait_ge(s_sq, g2 * (6 * FFC) + (3 * (FFC * n + c) + b + 1))
                            act.copy(UH[:, c, x:y], SQ[c][:, x:y]).then_inc(s_qh, 1)

                        act.wait_ge(s_ub, g2 * (4 * FFC) + (2 * (FFC * n + c) + 2 + UB0))
                        for b, (x, y) in enumerate(SEG):
                            act.activation(SQ[c][:, x:y], bank(3 * c + b, y - x), ACT.Relu).then_inc(s_rl, 1)
                            if b:
                                square_high(b - 1)
                        square_high(2)
            for t in range(NT):
                ln.act(act, ch, t)
            keep(e, ch, "act")

        @block.gpsimd
        def _(pool):
            ch = chains(e, pool, "pool")
            with pool.Fori(0, FFG // 2) as g2:
                for n in range(2):
                    def up_low(c, half):
                        pool.wait_ge(s_hi, g2 * (4 * FFC) + (2 * (FFC * n + c) + half + 1))
                        ks = slice(4 * half, 4 * half + 4)
                        pool.tensor_tensor(WL[:, ks, :], WU[n][:, ks, c * P:(c + 1) * P], WH[:, ks, :], ALU.subtract
                                           ).then_inc(s_uh, 1)

                    def down_low(c):
                        pool.wait_ge(s_dhi, g2 * (2 * FFC) + (FFC * n + c + 1))
                        pool.tensor_tensor(DL[:, c, :], WD[:, c, :], DH[:, c, :], ALU.subtract).then_inc(s_dl, 1)

                    up_low(0, 0)
                    up_low(0, 1)
                    down_low(0)
                    up_low(1, 0)
                    down_low(1)
                    up_low(1, 1)
            for t in range(NT):
                ln.pool(ch, pool, t)
            keep(e, ch, "pool")

        @block.vector
        def _(dve):
            ch = chains(e, dve, "dve")
            dve.engine_nop().then_inc(s_ub, UB0)
            dve.engine_nop().then_inc(s_dn, DN0)
            for k in range(KC):
                dve.wait_ge(s_th, k + 1)
                dve.tensor_tensor(HL[:, k, :], HT[:, k, :], HH[:, k, :], ALU.subtract).then_inc(s_tl, 1)
            for t in range(NT):
                R = rows(t)
                ch.mark(dve.tensor_scalar(X[0:R, t, :], X[0:R, t, :], ALPHA, None, ALU.mult))
            ch.wait()
            dve.engine_nop().then_inc(s_ad, AD0)
            with dve.Fori(0, FFG // 2) as g2:
                for n in range(2):
                    dve.wait_ge(s_ad, g2 * (2 * NT) + (n * NT + AD0))
                    for c in range(FFC):
                        def low(b):
                            x, y = SEG[b]
                            dve.wait_ge(s_qh, g2 * (6 * FFC) + (3 * (FFC * n + c) + b + 1))
                            dve.tensor_tensor(UL[:, c, x:y], SQ[c][:, x:y], UH[:, c, x:y], ALU.subtract
                                              ).then_inc(s_ql, 1)

                        for b, (x, y) in enumerate(SEG):
                            z = SQ[c][:, x:y]
                            dve.wait_ge(s_rl, g2 * (6 * FFC) + (3 * (FFC * n + c) + b + 1))
                            dve.tensor_tensor(z, z, z, ALU.mult).then_inc(s_sq, 1)
                            if b:
                                low(b - 1)
                        low(2)
                    for t in range(NT):
                        R = rows(t)
                        dve.wait_ge(s_dn, g2 * (2 * NT) + (n * NT + t + 1 + DN0))
                        b0 = (6, 0)[t % 2] * 512
                        dve.tensor_tensor(X[0:R, t, :], X[0:R, t, :], ps[0:R, b0:b0 + 1024], ALU.add).then_inc(s_ad, 1)
            dve.wait_ge(s_ad, FFG * NT + AD0)
            for t in range(NT + 1):
                if t < NT:
                    ln.stats(ch, dve, t)
                if t:
                    ln.unit_rows(ch, dve, t - 1)
            keep(e, ch, "dve")


def constants():
    import numpy as np

    f4 = np.float32
    c = np.zeros((P, NCST), f4)

    def put(name, x):
        a, b = CST[name]
        c[:x.shape[0], a:b] = x.reshape(x.shape[0], b - a)

    put("ident", np.eye(P, dtype=f4))
    pos = np.zeros((P, NT), np.int64)
    for t in range(NT - 1):
        pos[:, t] = t * P + np.arange(P)
    pos[:NS, NT - 1] = PAST + np.arange(NS) % DT
    for n, half in ((64, 32), (32, 16)):
        inv = (f4(10000.0) ** (-np.arange(half, dtype=f4) / f4(half))).astype(f4)
        ang = pos.astype(f4)[:, :, None] * inv
        co, si = np.cos(ang).astype(f4), np.sin(ang).astype(f4)
        put(f"cos{n}", np.concatenate([co, co], -1))
        put(f"sin{n}", np.concatenate([-si, si], -1))
    a = np.arange(P)
    put("causal", np.where(a[None] <= a[:, None], 0.0, NEG).astype(f4))
    b = np.arange(NS)
    put("own", np.where((b[None] // DT == b[:, None] // DT) & (b[None] <= b[:, None]), 0.0, NEG).astype(f4))
    put("heads", (a[None] // 64 == a[:, None] // 64).astype(f4))
    put("batch", (b[:, None] // DT == np.arange(DB)[None]).astype(f4))

    c16 = np.zeros((P, NCST16), f4)
    c16[:, 0:P] = np.eye(P)
    start = np.ones(TOK)
    start[0:SEQ:P] = 0
    start[SEQ::DT] = 0
    c16[:, P:P + TOK] = start
    col = np.arange(P)
    for bp in range(4):
        c16[:NS, P + TOK + bp * P:P + TOK + (bp + 1) * P] = (
            b[:, None] == (2 * bp + col // 64)[None] * DT + (col % DT)[None])
    m = np.zeros((P, NMASK), f4)
    m[:, 0:P] = np.eye(P)
    for n, s in enumerate(LEVELS):
        m[:, (n + 1) * P:(n + 2) * P] = ((a[:, None] // (2 * s) == a[None] // (2 * s)) & (a[:, None] % (2 * s) < s)
                                         & (a[None] % (2 * s) >= s))
    return c, c16, m


_OUTS = [("y_prompt", (1, SEQ, D)), ("y_sample", (DB, DT, D)),
         ("k_prompt", (DEPTH, 1, SEQ, 256)), ("v_prompt", (DEPTH, 1, SEQ, 256)), ("kidx_prompt", (DEPTH, 1, SEQ, ID)),
         ("k_sample", (DEPTH, DB, DT, 256)), ("v_sample", (DEPTH, DB, DT, 256)), ("kidx_sample", (DEPTH, DB, DT, ID)),
         ("hgrn_prompt", (DEPTH, 1, 4, 64, 64)), ("hgrn_sample", (DEPTH, DB, 4, 64, 64)),
         ("conv_prompt", (DEPTH, P, 4)), ("conv_sample", (DEPTH, P, 2 * DB * 2)),
         ("mem_k", (DEPTH, 1, NMEM, 512)), ("mem_v", (DEPTH, 1, NMEM, 512))]


def kernel(**inputs):
    import numpy as np
    import concourse.bacc as bacc
    from concourse.bass_utils import run_bass_kernel_spmd

    x = {k: np.asarray(v) for k, v in inputs.items()}
    f4 = np.float32
    chunks = lambda a: np.moveaxis(a.reshape(*a.shape[:-1], 2, P), -1, 1)
    cst, cst16, masks = constants()
    par = np.concatenate([chunks(x["w_conv"]).reshape(DEPTH, P, 6), chunks(x["hg_norm"]).reshape(DEPTH, P, 2),
                          np.transpose(x["state_conv"].reshape(DEPTH, DB, 2, 2, P), (0, 4, 3, 1, 2)).reshape(DEPTH, P, 32)],
                         axis=2)
    arrays = {
        "x_prompt": x["x_prompt"], "x_sample": x["x_sample"],
        "w_in": x["w_in"], "w_out": x["w_out"], "w_xq": x["w_xq"], "w_xk": x["w_xk"], "w_xv": x["w_xv"],
        "w_xo": x["w_xo"], "w_up": x["w_up"], "w_down": x["w_down"],
        "kidxT": np.swapaxes(x["cache_kidx"].reshape(DEPTH * NPHYS, PAGE, ID), 1, 2),
        "kT": np.swapaxes(x["cache_k"].reshape(DEPTH * NPHYS, PAGE, NKV * HD), 1, 2),
        "cache_v": x["cache_v"].reshape(DEPTH * NPHYS, PAGE, NKV * HD),
        "state_hgrn": x["state_hgrn"],
        "mem_kT": np.transpose(x["cache_mem_k"], (0, 1, 3, 4, 2)),
        "mem_v": x["cache_mem_v"].reshape(DEPTH, DB, NMEM, XH * XD),
        "memT": x["mem_prompt"][0].T,
        "page_table": x["page_table"].reshape(1, DB * NPG),
        "params": par,
        "lb_logits": np.transpose(x["hg_lb_logits"].reshape(DEPTH, 2, P), (2, 0, 1)).reshape(P, 4),
        "ln": np.stack([x[k] for k in ("ln1_g", "ln1_b", "ln2_g", "ln2_b", "ln3_g", "ln3_b")], axis=1),
        "cst": cst, "cst_narrow": np.concatenate([cst16, masks], axis=1),
    }
    arrays = {k: np.ascontiguousarray(v) for k, v in arrays.items()}
    nc = bacc.Bacc("TRN2", target_bir_lowering=False, num_devices=1)
    ins = {k: nc.dram_tensor("in_" + k, v.shape, mybir.dt.from_np(v.dtype), kind="ExternalInput").ap()
           for k, v in arrays.items()}
    outs = {k: nc.dram_tensor("out_" + k, s, F32, kind="ExternalOutput").ap() for k, s in _OUTS}
    build(nc, ins, outs)
    r = run_bass_kernel_spmd(nc, [{"in_" + k: v for k, v in arrays.items()}], core_ids=[0]).results[0]
    g = {k: r["out_" + k] for k, _ in _OUTS}
    conv_p = np.transpose(g["conv_prompt"].reshape(DEPTH, P, 2, 2), (0, 3, 2, 1)).reshape(DEPTH, 1, 2, 256)
    conv_s = np.transpose(g["conv_sample"].reshape(DEPTH, P, 2, DB, 2), (0, 3, 4, 2, 1)).reshape(DEPTH, DB, 2, 256)
    kv = lambda a, b, s: a.reshape(DEPTH, b, s, NKV, HD)
    return (g["y_prompt"], g["y_sample"], kv(g["k_prompt"], 1, SEQ), kv(g["v_prompt"], 1, SEQ), g["kidx_prompt"],
            kv(g["k_sample"], DB, DT), kv(g["v_sample"], DB, DT), g["kidx_sample"],
            g["hgrn_prompt"], g["hgrn_sample"], conv_p, conv_s,
            g["mem_k"].reshape(DEPTH, 1, NMEM, XH, XD), g["mem_v"].reshape(DEPTH, 1, NMEM, XH, XD))
```

```python
from contextlib import ExitStack, contextmanager

import concourse.bass as bass
from concourse import mybir

F32 = mybir.dt.float32
F32R = mybir.dt.float32r
BF16 = mybir.dt.bfloat16
U8 = mybir.dt.uint8
I32 = mybir.dt.int32
ALU = mybir.AluOpType
ACT = mybir.ActivationFunctionType
AX = mybir.AxisListType.X

P = 128
D = 1024
DEPTH = 2
SEQ = 1024
DB, DT = 8, 8
NS = DB * DT
TOK = SEQ + NS
NT = SEQ // P + 1
KC = D // P
PAST, PAGE = 2048, 128
NPG = PAST // PAGE
NPHYS = DB * NPG * 5 // 4
TOPK = 256
HD, NKV, NH = 64, 4, 8
IH, ID = 8, 32
NMEM, XH, XD = 256, 4, 128
DFF = 4 * D
NIN = 3112
LS = PAST + NS
EPS = 1e-5
ALPHA = (2 * DEPTH) ** 0.25
NEG = -1e30
GONE = -3e38
PICKED = -2e38
C_H, C_B, C_C, G_Q, G_F, G_I, G_G, A_Q, A_KV, A_QI = 0, 256, 512, 768, 1024, 1280, 1536, 1792, 2304, 2816
LEVELS = [64, 32, 16, 8, 4, 2, 1]

CST = {}
_n = 0
for _name, _w in (("ident", 128), ("cos64", NT * 64), ("sin64", NT * 64), ("cos32", NT * 32), ("sin32", NT * 32),
                  ("causal", 128), ("own", NS), ("heads", 128), ("batch", DB)):
    CST[_name] = (_n, _n + _w)
    _n += _w
NCST = _n
NCST16 = 128 + TOK + 4 * 128
NMASK = 8 * 128
NPAR = 6 + 2 + 2 * DB * 2

OFF = {}
_n = 0
for _name, _w in (("X", NT * D), ("A", KC * TOK), ("W", 8192), ("S", 4224 + LS), ("M", 2304 + LS // 2),
                  ("C", 4 * 2 * TOK), ("U", 2 * (SEQ + 2) + 2 * DB * (DT + 2)), ("G", NT * 256)):
    OFF[_name] = _n
    _n += _w
NARENA = _n
NHEAD = OFF["W"]
RR = OFF["S"]


class Chain:

    def __init__(self, eng, sem):
        self.eng, self.sem, self.n = eng, sem, 0

    def mark(self, ins):
        self.n += 1
        ins.then_inc(self.sem, 1)

    def wait(self):
        self.eng.wait_ge(self.sem, self.n)

    def __call__(self, ins):
        self.mark(ins)
        self.wait()


def rows(t):
    return P if t < NT - 1 else NS


def build(nc, i, o):
    ctx = ExitStack()
    with ctx:
        ctx.enter_context(nc.allow_non_contiguous_dma(reason="small parameter rows"))
        ar = ctx.enter_context(nc.sbuf_tensor("arena", [P, NHEAD], F32))
        cst = ctx.enter_context(nc.sbuf_tensor("cst", [P, NCST], F32))
        cst16 = ctx.enter_context(nc.sbuf_tensor("cst16", [P, NCST16], BF16))
        msk = ctx.enter_context(nc.sbuf_tensor("msk", [P, NMASK], U8))
        par = ctx.enter_context(nc.sbuf_tensor("par", [P, NPAR], F32))
        small = ctx.enter_context(nc.sbuf_tensor("small", [P, 192], F32))
        pages = ctx.enter_context(nc.sbuf_tensor("pages", [1, DB * NPG], I32))
        ps = ctx.enter_context(nc.psum_tensor("ps", [P, 8 * 512], F32))
        sems, stacks, rest = [], [ctx], {}

        def sem(name):
            s = stacks[-1].enter_context(nc.semaphore(name))
            sems.append(s)
            return s

        def at(region, off, *dims):
            n = 1
            for x in dims:
                n *= x
            base = (OFF[region] if isinstance(region, str) else region) + off
            if base < NHEAD:
                v = ar[:, base:base + n]
            else:
                v = rest["f32"][:, base - NHEAD:base - NHEAD + n]
            if len(dims) == 2:
                v = v.rearrange("p (a b) -> p a b", a=dims[0])
            if len(dims) == 3:
                v = v.rearrange("p (a b c) -> p a b c", a=dims[0], b=dims[1])
            if len(dims) == 4:
                v = v.rearrange("p (a b c d) -> p a b c d", a=dims[0], b=dims[1], c=dims[2])
            return v

        def cs(name):
            return cst[:, CST[name][0]:CST[name][1]]

        def bank(n, w=512):
            return ps[:, n * 512:n * 512 + w]

        def tcol(t):
            return slice(t * P, t * P + rows(t))

        ident = cs("ident")
        ident16 = cst16[:, 0:128]
        start16 = cst16[:, 128:128 + TOK]
        spread = cst16[:, 128 + TOK:].rearrange("p (a b) -> p a b", a=4)
        causal, own = cs("causal"), cs("own")
        lb_tab = small[:, 0:4].rearrange("p (l c) -> p l c", l=2)
        lb, oml = small[:, 4:6], small[:, 6:8]
        eps_t = small[:, 8:9]
        w_idx = small[:, 16:16 + NT * IH].rearrange("p (t h) -> p t h", t=NT)
        stat = small[:, 96:192]

        chd, cha, chp = sem("chain_dve"), sem("chain_act"), sem("chain_pool")

        s_c, s_cn, s_x0, s_lb = sem("const_in"), sem("const_narrow_in"), sem("x_in_y"), sem("lb_steps")
        with nc.Block() as block:
            @block.sync
            def _(sp):
                sp.dma_start(cst[:, :], i["cst"]).then_inc(s_c, 16)
                sp.dma_start(at("A", 0, NCST16 + NMASK), i["cst_narrow"]).then_inc(s_cn, 16)
                sp.dma_start(pages[:, :], i["page_table"]).then_inc(s_c, 16)
                sp.dma_start(stat[:, 0:4], i["lb_logits"]).then_inc(s_lb, 16)
                sp.dma_start(at("X", 0, NT, D)[:, 0:NT - 1, :], i["x_prompt"][0].rearrange("(t p) d -> p t d", p=P)
                             ).then_inc(s_x0, 16)
                sp.dma_start(at("X", 0, NT, D)[0:NS, NT - 1, :], i["x_sample"].rearrange("b t d -> (b t) d")
                             ).then_inc(s_x0, 16)
                sp.wait_ge(s_c, 32)
                sp.wait_ge(s_x0, 32)

            @block.vector
            def _(dve):
                ch = Chain(dve, chd)
                l0, l1 = stat[:, 0:2], stat[:, 2:4]
                dve.memset(eps_t, EPS)
                dve.wait_ge(s_cn, 16)
                dve.tensor_copy(cst16[:, :], at("A", 0, NCST16))
                dve.tensor_copy(msk[:, :], at("A", NCST16, NMASK))
                dve.wait_ge(s_lb, 16)
                ch(dve.tensor_tensor(stat[:, 4:6], l0, l1, ALU.max))
                ch.mark(dve.tensor_tensor(stat[:, 6:8], l0, stat[:, 4:6], ALU.subtract))
                dve.tensor_tensor(stat[:, 8:10], l1, stat[:, 4:6], ALU.subtract).then_inc(s_lb, 1)
                dve.wait_ge(s_lb, 18)
                ch(dve.tensor_tensor(stat[:, 10:12], stat[:, 6:8], stat[:, 8:10], ALU.add))
                ch(dve.reciprocal(stat[:, 12:14], stat[:, 10:12]))
                ch.mark(dve.tensor_tensor(stat[:, 14:16], stat[:, 6:8], stat[:, 12:14], ALU.mult))
                ch(dve.tensor_tensor(stat[:, 16:18], stat[:, 8:10], stat[:, 12:14], ALU.mult))
                ch.mark(dve.memset(lb_tab[:, 0, :], 0.0))
                ch(dve.tensor_tensor(stat[:, 18:20], stat[:, 14:16], stat[:, 16:18], ALU.add))
                ch(dve.tensor_tensor(lb_tab[:, 1, :], stat[:, 18:20], stat[:, 14:16], ALU.subtract))

            @block.scalar
            def _(act):
                act.wait_ge(s_lb, 17)
                act.wait_ge(chd, 2)
                act.activation(stat[:, 6:10], stat[:, 6:10], ACT.Exp).then_inc(s_lb, 1)

        def clear_all():
            with nc.Block() as block:
                @block.gpsimd
                def _(pool):
                    lo = min(s.num for s in sems)
                    hi = max(s.num for s in sems)
                    pool.sem_clear(range(lo, hi + 1))

        @contextmanager
        def own_semaphores():
            env["counts"] = {"dve": 0, "act": 0, "pool": 0}
            with ExitStack() as part:
                stacks.append(part)
                yield
                clear_all()
            del stacks[-1]

        env = dict(nc=nc, i=i, o=o, at=at, cs=cs, bank=bank, tcol=tcol, ps=ps, sem=sem, ident=ident, ident16=ident16,
                   start16=start16, spread=spread, causal=causal, own=own, lb_tab=lb_tab, lb=lb, oml=oml,
                   eps_t=eps_t, w_idx=w_idx, stat=stat, chd=chd, cha=cha, chp=chp, msk=msk, par=par, pages=pages)
        clear_all()
        with nc.Fori(0, DEPTH) as layer:
            env["layer"] = layer
            with nc.sbuf_tensor("arena_rest", [P, NARENA - NHEAD], F32) as rest["f32"]:
                with own_semaphores():
                    index_block(env)
                    mixer_block(env)
                    attend_block(env)
                with own_semaphores():
                    out_block(env)
                    cross_block(env)
            with (own_semaphores(), nc.sbuf_tensor("ffn_raw", [P, FFN_RAW], F32) as rest["f32"],
                  nc.sbuf_tensor("ffn_parts", [P, FFN_PARTS], F32R) as env["parts"]):
                ffn_block(env)

        s_yo = sem("y_out")
        with nc.Block() as block:
            @block.sync
            def _(sp):
                X = at("X", 0, NT, D)
                sp.dma_start(o["y_prompt"][0].rearrange("(t p) d -> p t d", p=P), X[:, 0:NT - 1, :]).then_inc(s_yo, 16)
                sp.dma_start(o["y_sample"].rearrange("b t d -> (b t) d"), X[0:NS, NT - 1, :]).then_inc(s_yo, 16)
                sp.wait_ge(s_yo, 32)


def chains(e, eng, which):
    c = Chain(eng, {"dve": e["chd"], "act": e["cha"], "pool": e["chp"]}[which])
    c.n = e["counts"][which]
    return c


def keep(e, c, which):
    e["counts"][which] = c.n


def selections():
    jobs, soff = score_jobs()
    return [(off, w, P, t * (t + 1) // 2 * P) for off, t, _, w in jobs[:6]], (soff, LS, NS, 4608)


def topk(e, dve, ch):
    S, M16, top = e["at"]("S", 0, 4224 + LS), e["at"]("M", 0, 2304 + LS // 2).bitcast(BF16), e["stat"][:, 80:88]
    s_k1, s_k2 = e["s_topk"]

    def rounds(x, count):
        off, w, R, _ = x
        s = S[0:R, off:off + w]
        for k in range(count):
            dve.max(top[0:R], s).then_inc(s_k1, 1)
            dve.wait_ge(s_k1, k + 1)
            dve.match_replace(s, top[0:R], s, GONE).then_inc(s_k2, 1)
            dve.wait_ge(s_k2, k + 1)
        dve.sem_clear(s_k1)
        dve.sem_clear(s_k2)

    def mark_picked(x):
        off, w, R, moff = x
        ch(dve.tensor_scalar(M16[0:R, moff:moff + w], S[0:R, off:off + w], PICKED, NEG, ALU.is_gt, ALU.mult))

    return rounds, mark_picked


def for_pages(eng, e, first, load, until=None):
    phys = [eng.value_load(e["pages"][0:1, first + k:first + k + 1], min_val=0, max_val=NPHYS - 1)
            for k in range(NPG // 2)]
    if until:
        until()
    for k in range(NPG // 2):
        load(k, bass.ds(e["layer"] * NPHYS + phys[k], 1))


def lay(x, layer):
    return x[bass.ds(layer, 1)]


def score_jobs():
    jobs, off = [], 0
    for t in range(2, NT - 1):
        jobs.append((off, t, 0, (t + 1) * P))
        off += (t + 1) * P
    jobs += [(off, NT - 1, 0, 1024), (off + 1024, NT - 1, 1024, 1024), (off + 2048, NT - 1, 2048, NS)]
    return jobs, off


def index_block(e):
    nc, i, o, at, bank, tcol, sem, layer = (e[k] for k in ("nc", "i", "o", "at", "bank", "tcol", "sem", "layer"))
    ident, w_idx = e["ident"], e["w_idx"]
    X = at("X", 0, NT, D)
    XT = at("A", 0, KC, TOK)
    wb = at("W", 0, KC, 296)
    kitc = at("W", 4096, 2, PAST)
    QKI = at("C", 0, 3, TOK)
    QB = at("C", 3264, IH, 2, NS)
    zi = at("C", 4288, 2, 296)
    rr = at("C", 4880, 2, 288)
    kr = at("C", 5456, 2, 128)
    kio = at("C", 5712, NT, ID)
    t1 = at("C", 6000, 288)
    t2 = at("C", 6288, 288)
    r = at("X", 0, 2, 1024)
    S = at("S", 0, 4224 + LS)
    jobs, _ = score_jobs()
    steps = [(j, h) for j in range(len(jobs)) for h in range(IH)]

    s_xo = sem("x_out")
    e["s_wl"] = [sem(f"w_mix{n}") for n in range(2)]
    s_w, s_kit, s_par, s_kid = (sem(n) for n in ("w_index", "cached_kidx", "params", "kidx_out"))
    s_tp, s_ta, s_td = sem("xt_done"), sem("xt_copied_act"), sem("xt_copied_dve")
    s_zp, s_zi, s_ro, s_qp, s_qk = (sem(n) for n in ("zidx_done", "zidx_copied", "roped", "qk_turned", "qk_copied"))
    s_qb, s_qz = sem("sample_q_spread"), sem("sample_q_zeroed")
    s_sp, s_sr, s_sd = sem("score_done"), sem("score_relu"), sem("score_added")

    with nc.Block() as block:
        @block.sync
        def _(sp):
            sp.dma_start(wb, lay(i["w_in"], layer).rearrange("l (k p) n -> p (l k) n", p=P)[:, :, A_QI:NIN]
                         ).then_inc(s_w, 16)
            sp.dma_start(e["par"][:, :], lay(i["params"], layer).rearrange("l p n -> (l p) n")).then_inc(s_par, 16)
            sp.dma_start(o["y_prompt"][0].rearrange("(t p) d -> p t d", p=P), X[:, 0:NT - 1, :]).then_inc(s_xo, 16)
            sp.dma_start(o["y_sample"].rearrange("b t d -> (b t) d"), X[0:NS, NT - 1, :]).then_inc(s_xo, 16)
            for b in range(DB):
                for half in range(2):
                    k0 = half * (PAST // 2)
                    for_pages(sp, e, b * NPG + half * (NPG // 2), lambda pg, page: sp.dma_start(
                        kitc[32 * (b % 4):32 * (b % 4) + 32, b // 4, k0 + pg * PAGE:k0 + (pg + 1) * PAGE],
                        i["kidxT"][page].rearrange("n d s -> (n d) s")).then_inc(s_kit, 16))
            sp.wait_ge(s_ro, NT)
            sp.dma_start(lay(o["kidx_prompt"], layer).rearrange("l b (t p) d -> p (l b t) d", p=P),
                         kio[:, 0:NT - 1, :]).then_inc(s_kid, 16)
            sp.dma_start(lay(o["kidx_sample"], layer).rearrange("l b t d -> (l b t) d"),
                         kio[0:NS, NT - 1, :]).then_inc(s_kid, 16)
            sp.wait_ge(s_zp, NT)
            sp.dma_start(at("W", 0, KC, 512),
                         lay(i["w_in"], layer).rearrange("l (k p) n -> p (l k) n", p=P)[:, :, WBLK[0][0]:WBLK[0][0] + 512]
                         ).then_inc(e["s_wl"][0], 16)
            sp.wait_ge(s_kid, 32)
            sp.wait_ge(s_par, 16)
            sp.wait_ge(s_kit, 16 * DB * NPG)

        @block.tensor
        def _(pe):
            for t in range(NT):
                R = rows(t)
                for half in range(2):
                    g = 2 * t + half
                    if g >= 4:
                        pe.wait_ge((s_ta, s_td)[g % 2], g // 2 - 1)
                    for c in range(4):
                        ins = pe.transpose(bank(g % 4)[:, c * P:c * P + R],
                                           X[0:R, t, (4 * half + c) * P:(4 * half + c + 1) * P], ident[0:R, 0:R])
                    ins.then_inc(s_tp, 1)
            pe.wait_ge(s_w, 16)

            def turn(t):
                R = rows(t)
                pe.wait_ge(s_ro, t + 1)
                if t >= 2:
                    pe.wait_ge(s_qk, t - 1)
                for n, src in enumerate((rr[0:R, t % 2, 0:128], rr[0:R, t % 2, 128:256], kr[0:R, t % 2, :])):
                    ins = pe.transpose(bank(6 + t % 2)[:, n * P:n * P + R], src, ident[0:R, 0:R])
                ins.then_inc(s_qp, 1)

            for t in range(NT):
                R = rows(t)
                pe.wait_ge(s_ta, t + 1)
                pe.wait_ge(s_td, t + 1)
                if t >= 2:
                    pe.wait_ge(s_zi, t - 1)
                for k in range(KC):
                    ins = pe.matmul(bank(4 + t % 2, 296)[0:R, :], XT[:, k, tcol(t)], wb[:, k, :],
                                    start=(k == 0), stop=(k == KC - 1))
                ins.then_inc(s_zp, 1)
                if t:
                    turn(t - 1)
            turn(NT - 1)
            pe.wait_ge(s_qk, NT)
            for n, (j, h) in enumerate(steps):
                _, t, k0, w = jobs[j]
                if n >= 2:
                    pe.wait_ge(s_sr, n - 1)
                if j == 6 and h == 0:
                    pe.wait_ge(s_qb, 1)
                    pe.wait_ge(s_kit, 16 * DB * NPG)
                out = e["ps"][:, (n % 2) * 1024:(n % 2) * 1024 + w]
                part = slice(32 * (h % 4), 32 * (h % 4) + 32)
                if t < NT - 1:
                    for a in range(0, w, 512):
                        b = min(a + 512, w)
                        ins = pe.matmul(out[:, a:b], QKI[part, h // 4, tcol(t)], QKI[part, 2, a:b],
                                        start=True, stop=True)
                elif k0 < PAST:
                    for a in range(0, w, 512):
                        for g in range(2):
                            ins = pe.matmul(out[0:NS, a:a + 512], QB[:, h, g, :], kitc[:, g, k0 + a:k0 + a + 512],
                                            start=(g == 0), stop=(g == 1))
                else:
                    ins = pe.matmul(out[0:NS, :], QKI[part, h // 4, SEQ:TOK], QKI[part, 2, SEQ:TOK],
                                    start=True, stop=True)
                ins.then_inc(s_sp, 1)

        @block.scalar
        def _(act):
            ch = chains(e, act, "act")
            for t in range(NT):
                act.wait_ge(s_tp, 2 * t + 1)
                act.copy(XT[:, 0:4, tcol(t)], bank((2 * t) % 4).rearrange("p (c n) -> p c n", c=4)[:, :, 0:rows(t)]
                         ).then_inc(s_ta, 1)

            def qk(t):
                act.wait_ge(s_qp, t + 1)
                act.copy(QKI[:, :, tcol(t)], bank(6 + t % 2, 384).rearrange("p (c n) -> p c n", c=3)[:, :, 0:rows(t)]
                         ).then_inc(s_qk, 1)

            for t in range(NT):
                R = rows(t)
                act.wait_ge(s_zp, t + 1)
                if t >= 2:
                    act.wait_ge(s_ro, t - 1)
                act.mul(w_idx[0:R, t, :], bank(4 + t % 2, 296)[0:R, 288:296], (ID * IH) ** -0.5)
                act.copy(zi[0:R, t % 2, 0:288], bank(4 + t % 2, 296)[0:R, 0:288]).then_inc(s_zi, 1)
                if t:
                    qk(t - 1)
            qk(NT - 1)
            for n, (j, h) in enumerate(steps):
                _, t, k0, w = jobs[j]
                act.wait_ge(s_sp, n + 1)
                if n == 0:
                    act.wait_ge(s_xo, 32)
                if n >= 2:
                    act.wait_ge(s_sd, n - 1)
                act.activation(r[0:rows(t), n % 2, 0:w], e["ps"][0:rows(t), (n % 2) * 1024:(n % 2) * 1024 + w],
                               ACT.Relu).then_inc(s_sr, 1)
            keep(e, ch, "act")

        @block.gpsimd
        def _(pool):
            pool.memset(at("C", 3264, IH * 2 * NS), 0.0).then_inc(s_qz, 1)

        @block.vector
        def _(dve):
            ch = chains(e, dve, "dve")
            for t in range(NT):
                dve.wait_ge(s_tp, 2 * t + 2)
                dve.tensor_copy(XT[:, 4:8, tcol(t)],
                                bank((2 * t + 1) % 4).rearrange("p (c n) -> p c n", c=4)[:, :, 0:rows(t)]
                                ).then_inc(s_td, 1)
            ch(dve.tensor_copy(e["lb"], e["lb_tab"][:, bass.ds(layer, 1), :].rearrange("p l c -> p (l c)")))
            ch(dve.tensor_scalar(e["oml"], e["lb"], -1.0, 1.0, ALU.mult, ALU.add))
            cos = e["cs"]("cos32").rearrange("p (t n) -> p t n", t=NT)
            sin = e["cs"]("sin32").rearrange("p (t n) -> p t n", t=NT)
            for t in range(NT):
                R = rows(t)
                z = zi[0:R, t % 2, 0:288].rearrange("p (h n) -> p h n", h=9)
                a = t1[0:R].rearrange("p (h n) -> p h n", h=9)
                b = t2[0:R].rearrange("p (h n) -> p h n", h=9)
                dve.wait_ge(s_zi, t + 1)
                ch.mark(dve.tensor_tensor(a, z, cos[0:R, t, :].unsqueeze(1).broadcast_to([R, 9, 32]), ALU.mult))
                ch.mark(dve.tensor_tensor(b[:, :, 0:16], z[:, :, 16:32],
                                          sin[0:R, t, 0:16].unsqueeze(1).broadcast_to([R, 9, 16]), ALU.mult))
                ch(dve.tensor_tensor(b[:, :, 16:32], z[:, :, 0:16],
                                     sin[0:R, t, 16:32].unsqueeze(1).broadcast_to([R, 9, 16]), ALU.mult))
                if t >= 2:
                    dve.wait_ge(s_qp, t - 1)
                ch(dve.tensor_tensor(rr[0:R, t % 2, :], t1[0:R], t2[0:R], ALU.add))
                ch(dve.tensor_copy(kio[0:R, t, :], rr[0:R, t % 2, 256:288]))
                dve.tensor_copy(kr[0:R, t % 2, :].rearrange("p (a n) -> p a n", a=4),
                                rr[0:R, t % 2, 256:288].unsqueeze(1).broadcast_to([R, 4, 32])).then_inc(s_ro, 1)
            dve.wait_ge(s_qk, NT)
            dve.wait_ge(s_qz, 1)
            for b in range(4):
                for q in range(4):
                    for g in range(2):
                        ins = dve.tensor_copy(QB[32 * b:32 * b + 32, q:IH:4, g, (4 * g + b) * DT:(4 * g + b + 1) * DT],
                                              QKI[32 * q:32 * q + 32, 0:2,
                                                  SEQ + (4 * g + b) * DT:SEQ + (4 * g + b + 1) * DT])
                        ch.mark(ins)
            ch.wait()
            dve.engine_nop().then_inc(s_qb, 1)
            for n, (j, h) in enumerate(steps):
                off, t, k0, w = jobs[j]
                R = rows(t)
                acc = S[0:R, off:off + w]
                dve.wait_ge(s_sr, n + 1)
                if n:
                    dve.wait_ge(s_sd, n)
                if h == 0:
                    ins = dve.tensor_scalar(acc, r[0:R, n % 2, 0:w], w_idx[0:R, t, h:h + 1], None, ALU.mult)
                else:
                    ins = dve.scalar_tensor_tensor(acc, r[0:R, n % 2, 0:w], w_idx[0:R, t, h:h + 1], acc,
                                                   ALU.mult, ALU.add)
                ins.then_inc(s_sd, 1)
            dve.wait_ge(s_sd, len(steps))
            for off, t, k0, w in jobs:
                if t < NT - 1:
                    d = S[:, off + w - P:off + w]
                    ch(dve.tensor_tensor(d, d, e["causal"], ALU.add))
                elif k0 == PAST:
                    d = S[0:NS, off:off + w]
                    ch(dve.tensor_tensor(d, d, e["own"][0:NS], ALU.add))
            keep(e, ch, "dve")


FEAT = [C_H, C_H + P, C_B, C_B + P, C_C, C_C + P, G_Q, G_Q + P, G_F, G_F + P, G_G, G_G + P]
WBLK = [(C_H, 512), (C_C, 512), (A_KV, 512), (A_Q, 512), (G_F, 512), (G_G, 256)]
HG_GROUPS = [(0, 3), (3, 6), (6, 9)]


def second(x, m):
    if not m:
        return x
    if len(x.shape) == 2:
        return x.rearrange("p (n a m) -> p n a m", a=2, m=m)[:, :, 1, :]
    return x.rearrange("p c (n a m) -> p c n a m", a=2, m=m)[:, :, :, 1, :]


def mixer_block(e):
    nc, i, o, at, bank, tcol, sem, layer = (e[k] for k in ("nc", "i", "o", "at", "bank", "tcol", "sem", "layer"))
    ident, par, ps = e["ident"], e["par"], e["ps"]
    XT = at("A", 0, KC, TOK)
    WB = [at("W", 4096 * n, KC, 512) for n in range(2)]
    qT = at("X", 0, 4, TOK)
    kT = at("X", 4 * TOK, 2, TOK)
    V = at("X", 6 * TOK, NT, 256)
    M16 = at("M", 0, 2304 + LS // 2).bitcast(BF16)
    CH, CB, CC, GQ = (at("C", n * 2 * TOK, 2, TOK) for n in range(4))
    GF, GG = CH, CC
    nU = 2 * (SEQ + 2)
    UP = at("U", 0, 2, SEQ + 2)
    US = at("U", nU, 2, DB, DT + 2)
    GI = at("G", 0, NT, 256)
    w0 = par[:, 0:6].rearrange("p (j c) -> p j c", j=3)
    hgn = par[:, 6:8]
    cst0 = par[:, 8:8 + 4 * DB].rearrange("p (c b j) -> p c b j", c=2, b=DB)

    s_wl = e["s_wl"]
    s_fp, s_fe, s_up, s_ue, s_rp, s_re, s_rot = (sem(n) for n in (
        "feat_done", "feat_copied", "tok_done", "tok_copied", "rot_turned", "rot_copied", "rotated"))
    s_krd = [sem(f"k_rows_out{n}") for n in range(2)]
    s_qs, s_kd, s_tk = sem("hg_qk_scaled"), sem("hg_end_diff"), sem("topk_tiles_done")
    s_cu, s_cv, s_co = (sem(n) for n in ("conv_u", "conv_done", "mix_out"))
    s_hin, s_oa = sem("hg_state_in"), sem("hg_sample_att_o")
    e["s_topk"] = sem("topk_max"), sem("topk_gone")
    s_sg, s_lf, s_kk, s_b, s_D, s_E, s_G = (sem(n) for n in (
        "hg_sigmoid", "hg_logf", "hg_gate", "hg_cumsum", "hg_diff", "hg_exp", "hg_level"))
    s_hz, s_ap, s_ad, s_kp, s_ke, s_pp, s_sv, s_op, s_oe = (sem(n) for n in (
        "hg_zeroed", "hg_att", "hg_att_kept", "hg_k_turned", "hg_k_copied", "hg_update", "hg_state", "hg_o", "hg_o_copied"))
    s_vb, s_n1, s_n2, s_n3, s_n4 = (sem(n) for n in ("hg_v_spread", "hg_sq", "hg_sum", "hg_rs", "hg_norm"))

    BB = at("W", 0, 2, TOK)
    QT = at("W", 2 * TOK, 2, TOK)
    KH = at("W", 4 * TOK, 2, TOK)
    S0 = at("W", 6 * TOK, DB, 2, HD)
    VB = at("W", 6 * TOK + 1024, DB, HD)
    E0 = at("A", 4 * TOK, 2, TOK)
    GL = [at("A", 6 * TOK, 2, 384), at("S", 2 * TOK, 2, 384), at("A", 6 * TOK + 768, 2, 384)]
    KK = at("S", 0, 2, TOK)
    YT = at("A", 0, KC, TOK)
    att = at("U", 0, 4, 512)
    slot = lambda t: t % 3 if t < NT - 1 else 3
    KHT = at("M", 1792, 2, 256)
    lvl = lambda n: e["msk"][:, n * P:(n + 1) * P]

    def st(n):
        return (at("U", 2048, 2, 64), at("W", 6 * TOK + 1536, 2, 64))[n % 2]

    zk, rk, tr = at("G", 0, 2, 512), at("G", 1024, 2, 512), at("M", 1792, 2, 512)

    def products_until(g, n):
        c = 0
        for gg, (ta, tb) in enumerate(HG_GROUPS):
            for nn in range(8):
                for t in range(ta, tb):
                    c += not (t == NT - 1 and nn and LEVELS[nn - 1] >= DT)
                if (gg, nn) == (g, n):
                    return c

    with nc.Block() as block:
        @block.sync
        def _(sp):
            for n, (c0, w) in enumerate(WBLK):
                if n >= 2:
                    if n == 2:
                        sp.wait_ge(s_fp, 4)
                    if n == 3:
                        sp.wait_ge(s_fp, 8)
                    if n == 4:
                        sp.wait_ge(s_up, NT)
                    if n == 5:
                        sp.wait_ge(s_up, 2 * NT)
                if n:
                    sp.dma_start(WB[n % 2][:, :, 0:w],
                                 lay(i["w_in"], layer).rearrange("l (k p) n -> p (l k) n", p=P)[:, :, c0:c0 + w]
                                 ).then_inc(s_wl[n % 2], 16)
                if n == 3:
                    for t in range(NT):
                        sp.wait_ge(s_rot, t + 1)
                        dst = (lay(o["k_prompt"], layer)[:, 0, tcol(t)].rearrange("l s d -> (l s) d") if t < NT - 1
                               else lay(o["k_sample"], layer).rearrange("l b s d -> (l b s) d"))
                        sp.dma_start(dst, rk[0:rows(t), t % 2, 0:256]).then_inc(s_krd[t % 2], 16)
                    sp.dma_start(lay(o["v_prompt"], layer).rearrange("l b (t p) d -> p (l b t) d", p=P),
                                 V[:, 0:NT - 1, :]).then_inc(s_co, 16)
                    sp.dma_start(lay(o["v_sample"], layer).rearrange("l b s d -> (l b s) d"),
                                 V[0:NS, NT - 1, :]).then_inc(s_co, 16)
            sp.wait_ge(s_cv, 1)
            sp.dma_start(lay(o["conv_prompt"], layer).rearrange("l p (c j) -> p (l c) j", c=2),
                         UP[:, :, SEQ:SEQ + 2]).then_inc(s_co, 16)
            sp.dma_start(lay(o["conv_sample"], layer).rearrange("l p (c b j) -> p (l c) b j", c=2, b=DB),
                         US[:, :, :, DT:DT + 2]).then_inc(s_co, 16)
            sp.wait_ge(s_fp, 12)
            sp.wait_ge(s_up, 3 * NT)
            sp.dma_start(S0.rearrange("p b c v -> p (b c) v"),
                         lay(i["state_hgrn"], layer).rearrange("l b (c h) k v -> (h k) (l b c) v", c=2)
                         ).then_inc(s_hin, 16)
            sp.wait_ge(s_sv, NT - 1)
            sp.dma_start(lay(o["hgrn_prompt"], layer).rearrange("l b (c h) k v -> (h k) (l b c) v", c=2),
                         st(NT - 1)).then_inc(s_co, 16)
            sp.wait_ge(s_sv, NT)
            sp.dma_start(lay(o["hgrn_sample"], layer).rearrange("l b (c h) k v -> (h k) (l b c) v", c=2),
                         S0.rearrange("p b c v -> p (b c) v")).then_inc(s_co, 16)
            sp.wait_ge(s_co, 16 * 6)
            sp.wait_ge(s_krd[0], 16 * 5)
            sp.wait_ge(s_krd[1], 16 * 4)

        @block.tensor
        def _(pe):
            def feat(f, buf, c):
                if f >= 2:
                    pe.wait_ge(s_fe, f - 1)
                for k in range(KC):
                    for a, b in ((0, 512), (512, 1024), (1024, TOK)):
                        ins = pe.matmul(ps[:, (f % 2) * 1536 + a:(f % 2) * 1536 + b],
                                        buf[:, k, c * P:(c + 1) * P], XT[:, k, a:b],
                                        start=(k == 0), stop=(k == KC - 1))
                ins.then_inc(s_fp, 1)

            def tok(u, t, buf, c0, w):
                R = rows(t)
                if u >= 2:
                    pe.wait_ge(s_ue, u - 1)
                for k in range(KC):
                    ins = pe.matmul(bank(6 + u % 2, w)[0:R, :], XT[:, k, tcol(t)], buf[:, k, c0:c0 + w],
                                    start=(k == 0), stop=(k == KC - 1))
                ins.then_inc(s_up, 1)

            def turn(n, t, chunks):
                R = rows(t)
                pe.wait_ge(s_rot, n + 1)
                if n >= 2:
                    pe.wait_ge(s_re, n - 1)
                for c in range(chunks):
                    ins = pe.transpose(bank(n % 2)[:, c * P:c * P + R], rk[0:R, n % 2, c * P:(c + 1) * P],
                                       ident[0:R, 0:R])
                ins.then_inc(s_rp, 1)

            for n in range(2):
                pe.wait_ge(s_wl[n], 16)
                for c in range(4):
                    feat(4 * n + c, WB[n], c)
            pe.wait_ge(s_fe, 8)
            for n in range(2):
                pe.wait_ge(s_wl[n], 32)
                for t in range(NT):
                    tok(NT * n + t, t, WB[n], 0, 512)
                    if t >= 2:
                        turn(NT * n + t - 2, t - 2, 2 + 2 * n)
                for t in (NT - 2, NT - 1):
                    turn(NT * n + t, t, 2 + 2 * n)
            pe.wait_ge(s_re, 2 * NT)
            pe.wait_ge(s_wl[0], 48)
            for c in range(2):
                feat(8 + c, WB[0], c)
            for t in range(NT):
                tok(2 * NT + t, t, WB[0], 256, 256)
            pe.wait_ge(s_wl[1], 48)
            for c in range(2):
                feat(10 + c, WB[1], c)
            pe.wait_ge(s_fe, 12)
            pe.wait_ge(s_ue, 3 * NT)
            na = 0

            def heads_att(t, lhs, rhs, c0, m):
                nonlocal na
                R = rows(t)
                if na >= 2:
                    pe.wait_ge(s_ad, na - 1)
                cols = slice(t * P - c0, t * P - c0 + R)
                for h in range(4):
                    c, hh = h // 2, h % 2
                    part = slice(64 * hh, 64 * hh + 64)
                    ins = pe.matmul(second(bank(2 * (na % 2) + hh)[0:R, c * P:c * P + R], m), lhs[part, c, cols],
                                    second(rhs[part, c, cols], m), start=True, stop=True)
                ins.then_inc(s_ap, 1)
                na += 1

            def tile_out(t):
                R = rows(t)
                if t >= 1:
                    pe.wait_ge(s_ke, t)
                for c in range(2):
                    ins = pe.transpose(bank(4)[0:R, c * P:(c + 1) * P], KH[:, c, tcol(t)], ident)
                ins.then_inc(s_kp, 1)
                if t:
                    pe.wait_ge(s_sv, t)
                    pe.wait_ge(s_oe, t)
                for c in range(2):
                    for hh in range(2):
                        h, part = 2 * c + hh, slice(64 * hh, 64 * hh + 64)
                        out = bank(5 + hh)[part, c * P:c * P + R]
                        if hh == 0 and c and t == NT - 1:
                            pe.wait_ge(s_oa, 2)
                        ins = pe.matmul(out, GI[0:R, t, h * HD:(h + 1) * HD],
                                        att[0:R, slot(t), hh * 256 + c * P:hh * 256 + c * P + R],
                                        start=True, stop=False, skip_group_check=True)
                        if t < NT - 1:
                            ins = pe.matmul(out, st(t)[part, c, :], QT[part, c, tcol(t)], start=False, stop=True,
                                            skip_group_check=True)
                    if t == NT - 1:
                        ins.then_inc(s_oa, 1)
                        pe.wait_ge(s_oa, 2 * c + 1)
                        for hh in range(2):
                            part = slice(64 * hh, 64 * hh + 64)
                            for b in range(DB):
                                ins = pe.matmul(bank(5 + hh)[part, c * P + b * DT:c * P + (b + 1) * DT],
                                                S0[part, b, c, :], QT[part, c, SEQ + b * DT:SEQ + (b + 1) * DT],
                                                start=False, stop=(b == DB - 1), skip_group_check=True)
                        if c == 0:
                            ins.then_inc(s_oa, 1)
                ins.then_inc(s_op, 1)
                pe.wait_ge(s_ke, t + 1)
                if t < NT - 1:
                    for h in range(4):
                        c, hh = h // 2, h % 2
                        ins = pe.matmul(bank(7)[64 * hh:64 * hh + 64, c * HD:(c + 1) * HD],
                                        KHT[:, t % 2, h * HD:(h + 1) * HD], GI[:, t, h * HD:(h + 1) * HD],
                                        start=True, stop=True)
                    ins.then_inc(s_pp, 1)
                else:
                    for c in range(2):
                        for hh in range(2):
                            h = 2 * c + hh
                            pe.wait_ge(s_vb, h + 1)
                            ins = pe.matmul(bank((7, 4)[c])[64 * hh:64 * hh + 64, :],
                                            KHT[0:NS, t % 2, h * HD:(h + 1) * HD],
                                            VB[0:NS].rearrange("p b v -> p (b v)"), start=True, stop=True)
                            ins.then_inc(s_pp, 1)

            for g, (ta, tb) in enumerate(HG_GROUPS):
                for n in range(8):
                    m = LEVELS[n - 1] if n else 0
                    if n:
                        pe.wait_ge(s_G, 7 * g + n)
                    else:
                        pe.wait_ge(s_kk, 1)
                        if g == 0:
                            pe.wait_ge(s_hz, 1)
                    for t in range(ta, tb):
                        if t == NT - 1 and m >= DT:
                            continue
                        if n:
                            heads_att(t, GL[(7 * g + n) % 3], GL[(7 * g + n) % 3], ta * P, m)
                        else:
                            heads_att(t, KK, GQ, 0, 0)
                pe.wait_ge(s_ad, na)
                if g == 0:
                    pe.wait_ge(s_qs, 1)
                    pe.wait_ge(s_hin, 16)
                for t in range(ta, tb):
                    tile_out(t)
            pe.wait_ge(s_n1, 1)
            pe.wait_ge(s_sv, NT)
            for n in range(2):
                for a, b in ((0, 512), (512, 1024), (1024, TOK)):
                    ins = pe.matmul(ps[:, n * 1536 + a:n * 1536 + b], e["cs"]("heads"), QT[:, n, a:b],
                                    start=True, stop=True)
            ins.then_inc(s_n2, 1)

        @block.scalar
        def _(act):
            ch = chains(e, act, "act")
            dst = [CH, CB, CC, GQ, GF, GG]
            nf = [0]

            def feat():
                f = nf[0]
                nf[0] += 1
                act.wait_ge(s_fp, f + 1)
                if f == 8:
                    act.wait_ge(s_cu, 1)
                act.copy(dst[f // 2][:, f % 2, :], ps[:, (f % 2) * 1536:(f % 2) * 1536 + TOK]).then_inc(s_fe, 1)

            def turned(n, t, chunks):
                act.wait_ge(s_rp, n + 1)
                src = bank(n % 2, chunks * P).rearrange("p (c s) -> p c s", c=chunks)[:, :, 0:rows(t)]
                if chunks == 2:
                    act.copy(kT[:, :, tcol(t)], src).then_inc(s_re, 1)
                else:
                    act.mul(qT[:, :, tcol(t)], src, HD ** -0.5).then_inc(s_re, 1)

            for _ in range(8):
                feat()
            for n in range(2):
                for t in range(NT):
                    u, R = NT * n + t, rows(t)
                    act.wait_ge(s_up, u + 1)
                    if u >= 2:
                        act.wait_ge(s_rot, u - 1)
                    if n == 0:
                        act.copy(V[0:R, t, :], bank(6 + u % 2)[0:R, 256:512])
                        act.copy(zk[0:R, u % 2, 0:256], bank(6 + u % 2)[0:R, 0:256]).then_inc(s_ue, 1)
                    else:
                        act.copy(zk[0:R, u % 2, :], bank(6 + u % 2)[0:R, :]).then_inc(s_ue, 1)
                    if t >= 2:
                        turned(NT * n + t - 2, t - 2, 2 + 2 * n)
                for t in (NT - 2, NT - 1):
                    turned(NT * n + t, t, 2 + 2 * n)
            feat()
            feat()
            act.wait_ge(s_fe, 10)
            act.activation(GF, GF, ACT.Sigmoid).then_inc(s_sg, 1)
            for t in range(NT):
                u, R = 2 * NT + t, rows(t)
                act.wait_ge(s_up, u + 1)
                act.copy(GI[0:R, t, :], bank(6 + u % 2, 256)[0:R, :]).then_inc(s_ue, 1)
            act.wait_ge(s_kk, 1)
            act.activation(GF, GF, ACT.Ln).then_inc(s_lf, 1)
            feat()
            feat()
            act.wait_ge(s_b, 1)
            act.activation(E0, BB, ACT.Exp).then_inc(s_E, 1)
            act.wait_ge(s_kd, 1)
            act.activation(KH, KH, ACT.Exp).then_inc(s_E, 1)
            for g, (ta, tb) in enumerate(HG_GROUPS):
                w = min(tb * P, TOK) - ta * P
                for n in range(1, 8):
                    ww = w if LEVELS[n - 1] < DT or g < 2 else 2 * P
                    x = GL[(7 * g + n) % 3][:, :, 0:ww]
                    act.wait_ge(s_D, 7 * g + n)
                    act.activation(x, x, ACT.Exp).then_inc(s_E, 1)
                if g == 2:
                    act.wait_ge(s_fe, 12)
                    act.activation(GG, GG, ACT.Sigmoid).then_inc(s_sg, 1)
                for t in range(ta, tb):
                    R = rows(t)
                    act.wait_ge(s_kp, t + 1)
                    if t >= 2:
                        act.wait_ge(s_pp, t - 1)
                    act.copy(KHT[0:R, t % 2, :], bank(4, 256)[0:R, :]).then_inc(s_ke, 1)
                    act.wait_ge(s_op, t + 1)
                    for hh in range(2):
                        part = slice(64 * hh, 64 * hh + 64)
                        ins = act.copy(YT[part, 2:4, tcol(t)],
                                       bank(5 + hh, 256)[part].rearrange("p (c s) -> p c s", c=2)[:, :, 0:R])
                    ins.then_inc(s_oe, 1)
            act.wait_ge(s_oe, NT)
            act.activation(QT, YT[:, 2:4, :], ACT.Square).then_inc(s_n1, 1)
            act.wait_ge(s_n2, 1)
            for n in range(2):
                ins = act.activation(E0[:, n, :], ps[:, n * 1536:n * 1536 + TOK], ACT.Identity,
                                     bias=e["eps_t"], scale=1.0 / HD)
                ch.mark(ins)
            ch.wait()
            ch(act.activation(KH, E0, ACT.Ln))
            act.activation(KH, KH, ACT.Exp, scale=-0.5).then_inc(s_n3, 1)
            keep(e, ch, "act")

        @block.gpsimd
        def _(pool):
            ch = chains(e, pool, "pool")
            ch.mark(pool.memset(UP[:, :, 0:2], 0.0))
            ch.mark(pool.tensor_copy(US[:, 0, :, 0:2], cst0[:, 0]))
            ch.mark(pool.tensor_copy(US[:, 1, :, 0:2], cst0[:, 1]))
            pool.wait_ge(s_fe, 6)
            for c in range(2):
                ch.mark(pool.tensor_tensor(UP[:, c, 2:], CH[:, c, 0:SEQ], CC[:, c, 0:SEQ], ALU.mult))
                ins = pool.tensor_tensor(US[:, c, :, 2:], CH[:, c, SEQ:TOK].rearrange("p (b s) -> p b s", b=DB),
                                         CC[:, c, SEQ:TOK].rearrange("p (b s) -> p b s", b=DB), ALU.mult)
                ch(ins)
            pool.engine_nop().then_inc(s_cu, 1)

            def rotate(n, t, w):
                R, H = rows(t), w // HD
                cos = e["cs"]("cos64").rearrange("p (t n) -> p t n", t=NT)[0:R, t]
                sin = e["cs"]("sin64").rearrange("p (t n) -> p t n", t=NT)[0:R, t]
                z = zk[0:R, n % 2, 0:w].rearrange("p (h n) -> p h n", h=H)
                a = tr[0:R, 0, 0:w].rearrange("p (h n) -> p h n", h=H)
                b = tr[0:R, 1, 0:w].rearrange("p (h n) -> p h n", h=H)
                pool.wait_ge(s_ue, n + 1)
                if n:
                    pool.wait_ge(s_rot, n)
                ch.mark(pool.tensor_tensor(a, z, cos.unsqueeze(1).broadcast_to([R, H, 64]), ALU.mult))
                ch.mark(pool.tensor_tensor(b[:, :, 0:32], z[:, :, 32:64],
                                           sin[:, 0:32].unsqueeze(1).broadcast_to([R, H, 32]), ALU.mult))
                ch(pool.tensor_tensor(b[:, :, 32:64], z[:, :, 0:32],
                                      sin[:, 32:64].unsqueeze(1).broadcast_to([R, H, 32]), ALU.mult))
                if n >= 2:
                    pool.wait_ge(s_rp, n - 1)
                if w == 256:
                    if n >= 2:
                        pool.wait_ge(s_krd[n % 2], 16 * (n // 2))
                    pool.tensor_tensor(rk[0:R, n % 2, 0:w], tr[0:R, 0, 0:w], tr[0:R, 1, 0:w], ALU.add
                                       ).then_inc(s_rot, 1)
                else:
                    if n < NT + 2:
                        pool.wait_ge(s_krd[0], 16 * 5)
                        pool.wait_ge(s_krd[1], 16 * 4)
                    for p in range(2):
                        sl = slice(p * 256, p * 256 + 256)
                        ins = pool.tensor_tensor(
                            rk[0:R, n % 2, sl].rearrange("p (g k n) -> p k g n", g=2, k=2),
                            tr[0:R, 0, sl].rearrange("p (k g n) -> p k g n", g=2, k=2),
                            tr[0:R, 1, sl].rearrange("p (k g n) -> p k g n", g=2, k=2), ALU.add)
                        if p == 0:
                            ch.mark(ins)
                        else:
                            ch(ins)
                    pool.engine_nop().then_inc(s_rot, 1)

            for t in range(NT):
                rotate(t, t, 256)
            for t in range(NT):
                rotate(NT + t, t, 512)
            for c in range(2):
                for part in range(3):
                    a = 512 * part
                    if part < 2:
                        dst, src, n = CB[:, c, a:a + 512], lambda j: UP[:, c, a + j:a + j + 512], 512
                    else:
                        dst, src, n = (CB[:, c, SEQ:TOK].rearrange("p (b s) -> p b s", b=DB),
                                       lambda j: US[:, c, :, j:j + DT], NS)
                    a0, a1 = tr[:, 0, 0:n], tr[:, 1, 0:n]
                    if part == 2:
                        a0, a1 = (x.rearrange("p (b s) -> p b s", b=DB) for x in (a0, a1))
                    ch(pool.tensor_scalar(a0, src(0), w0[:, 0, c:c + 1], None, ALU.mult))
                    ch(pool.tensor_scalar(a1, src(1), w0[:, 1, c:c + 1], None, ALU.mult))
                    ch(pool.tensor_tensor(a0, a0, a1, ALU.add))
                    ch(pool.tensor_scalar(a1, src(2), w0[:, 2, c:c + 1], None, ALU.mult))
                    ch(pool.tensor_tensor(a0, a0, a1, ALU.add))
                    ch(pool.tensor_tensor(dst, dst, a0, ALU.mult))
            pool.engine_nop().then_inc(s_cv, 1)
            pool.wait_ge(s_co, 64)
            ch(pool.memset(st(0), 0.0))
            pool.memset(at("U", 0, 2048), 0.0).then_inc(s_hz, 1)
            pool.wait_ge(s_sg, 1)
            pool.wait_ge(s_tk, 1)
            ch(pool.tensor_scalar(KK, GF, -1.0, 1.0, ALU.mult, ALU.add))
            for c in range(2):
                ch.mark(pool.tensor_scalar(KK[:, c, :], KK[:, c, :], e["oml"][:, c:c + 1], None, ALU.mult))
                ch.mark(pool.tensor_scalar(GF[:, c, :], GF[:, c, :], e["oml"][:, c:c + 1], e["lb"][:, c:c + 1],
                                           ALU.mult, ALU.add))
            ch.wait()
            pool.engine_nop().then_inc(s_kk, 1)
            pool.wait_ge(s_b, 1)
            for g, (ta, tb) in enumerate(HG_GROUPS):
                w = min(tb * P, TOK) - ta * P

                def views(n, x, c0):
                    m = LEVELS[n - 1]
                    ww = w if m < DT or g < 2 else 2 * P
                    return [x[:, c, c0:c0 + ww].rearrange("p (n a m) -> p n a m", a=2, m=m) for c in range(2)]

                def diff(n):
                    m = LEVELS[n - 1]
                    L = 7 * g + n
                    if L == 2:
                        pool.wait_ge(s_fp, 12)
                        pool.wait_ge(s_up, 3 * NT)
                    if L > 3:
                        pool.wait_ge(s_ap, products_until((L - 4) // 7, (L - 4) % 7 + 1))
                    out, b = views(n, GL[L % 3], 0), views(n, BB, ta * P)
                    for c in range(2):
                        nb = b[c].shape[1]
                        ref = b[c][:, :, 0, m - 1:m].broadcast_to([P, nb, m])
                        ch.mark(pool.tensor_tensor(out[c][:, :, 0, :], ref, b[c][:, :, 0, :], ALU.subtract))
                        ch.mark(pool.tensor_tensor(out[c][:, :, 1, :], b[c][:, :, 1, :], ref, ALU.subtract))
                    ch.wait()
                    pool.engine_nop().then_inc(s_D, 1)

                def mult(n):
                    out, k, q = views(n, GL[(7 * g + n) % 3], 0), views(n, KK, ta * P), views(n, GQ, ta * P)
                    for c in range(2):
                        ch.mark(pool.tensor_tensor(out[c][:, :, 0, :], out[c][:, :, 0, :], k[c][:, :, 0, :], ALU.mult))
                        ch.mark(pool.tensor_tensor(out[c][:, :, 1, :], out[c][:, :, 1, :], q[c][:, :, 1, :], ALU.mult))
                    ch.wait()
                    pool.engine_nop().then_inc(s_G, 1)

                for n in range(8):
                    if n < 7:
                        diff(n + 1)
                    if n:
                        pool.wait_ge(s_E, 2 + 7 * g + n)
                        mult(n)
            for h in range(4):
                if h == 0:
                    pool.wait_ge(s_hin, 16)
                else:
                    pool.wait_ge(s_pp, NT - 1 + h)
                pool.tensor_tensor(VB[0:NS], GI[0:NS, NT - 1, h * HD:(h + 1) * HD].unsqueeze(1).broadcast_to([NS, DB, HD]),
                                   e["cs"]("batch")[0:NS].unsqueeze(2).broadcast_to([NS, DB, HD]), ALU.mult
                                   ).then_inc(s_vb, 1)
            pool.wait_ge(s_sg, 2)
            for c in range(2):
                ch.mark(pool.tensor_scalar(GG[:, c, :], GG[:, c, :], hgn[:, c:c + 1], None, ALU.mult))
            ch.wait()
            pool.wait_ge(s_n1, 1)
            pool.tensor_tensor(YT[:, 2:4, :], YT[:, 2:4, :], GG, ALU.mult).then_inc(s_n4, 1)
            keep(e, ch, "pool")

        @block.vector
        def _(dve):
            ch = chains(e, dve, "dve")
            sel, _ = selections()
            rounds, mark_picked = topk(e, dve, ch)

            ch.mark(dve.tensor_copy(M16[:, 0:P], e["causal"]))
            ch.mark(dve.memset(M16[:, P:2 * P], 0.0))
            ch.mark(dve.tensor_copy(M16[:, 2 * P:3 * P], e["causal"]))
            for x in sel[:5]:
                with dve.Fori(0, TOPK // 8 // 4) as _:
                    rounds(x, 4)
                mark_picked(x)
            dve.engine_nop().then_inc(s_tk, 1)
            with dve.Fori(0, TOPK // 8 // 8) as _:
                rounds(sel[5], 4)
            dve.wait_ge(s_lf, 1)
            dve.wait_ge(s_up, 3 * NT)
            for c in range(2):
                ins = dve.tensor_tensor_scan(BB[:, c, :], e["start16"], GF[:, c, :], 0.0, ALU.mult, ALU.add)
            ins.then_inc(s_b, 1)
            dve.wait_ge(s_b, 1)
            dve.wait_ge(s_fp, 12)
            for c in range(2):
                for v, n, m in ((slice(0, SEQ), NT - 1, P), (slice(SEQ, TOK), DB, DT)):
                    bv = BB[:, c, v].rearrange("p (n m) -> p n m", m=m)
                    ch.mark(dve.tensor_tensor(KH[:, c, v].rearrange("p (n m) -> p n m", m=m),
                                              bv[:, :, m - 1:m].broadcast_to([P, n, m]), bv, ALU.subtract))
            ch.wait()
            dve.engine_nop().then_inc(s_kd, 1)
            dve.wait_ge(s_cv, 1)
            ch.mark(dve.tensor_copy(YT[:, 0:2, :], CB))
            na = 0
            dve.wait_ge(s_hz, 1)
            for g, (ta, tb) in enumerate(HG_GROUPS):
                for n in range(8):
                    m = LEVELS[n - 1] if n else 0
                    for t in range(ta, tb):
                        if t == NT - 1 and m >= DT:
                            continue
                        R = rows(t)
                        dve.wait_ge(s_ap, na + 1)
                        if g and n == 0:
                            dve.wait_ge(s_op, t - 2)
                        src = ps[:, 1024 * (na % 2):1024 * (na % 2) + 1024].rearrange("p (b s) -> p b s", b=2)
                        out = att[:, slot(t), :].rearrange("p (b s) -> p b s", b=2)
                        q = second(lvl(n)[0:R, 0:R], m)
                        for b in range(2):
                            ins = dve.copy_predicated(
                                second(out[0:R, b, :].rearrange("p (c s) -> p c s", c=2)[:, :, 0:R], m),
                                q.unsqueeze(1).broadcast_to([R, 2, *q.shape[1:]]),
                                second(src[0:R, b, 0:256].rearrange("p (c s) -> p c s", c=2)[:, :, 0:R], m))
                        ins.then_inc(s_ad, 1)
                        na += 1
                    if g:
                        rounds(sel[5], 1)
                    if g == 0 and n == 2:
                        dve.wait_ge(s_E, 2)
                        ch.mark(dve.tensor_tensor(QT, GQ, E0, ALU.mult))
                        ch(dve.tensor_tensor(KH, KK, KH, ALU.mult))
                        dve.engine_nop().then_inc(s_qs, 1)
                for t in range(ta, tb):
                    if t < NT - 1:
                        dve.wait_ge(s_pp, t + 1)
                        if t == 0:
                            dve.wait_ge(s_E, 1)
                        if t >= 1:
                            dve.wait_ge(s_op, t)
                            dve.wait_ge(s_sv, t)
                        for c in range(2):
                            ins = dve.scalar_tensor_tensor(st(t + 1)[:, c, :], st(t)[:, c, :],
                                                           E0[:, c, t * P + P - 1:t * P + P],
                                                           bank(7)[:, c * HD:(c + 1) * HD], ALU.mult, ALU.add)
                            if c == 0:
                                ch.mark(ins)
                        ins.then_inc(s_sv, 1)
                    else:
                        dve.wait_ge(s_op, NT)
                        for c in range(2):
                            x = S0[:, :, c, :]
                            last = E0[:, c, SEQ:TOK].rearrange("p (b s) -> p b s", b=DB)[:, :, DT - 1:DT]
                            ch(dve.tensor_tensor(x, x, last.broadcast_to([P, DB, HD]), ALU.mult))
                        dve.wait_ge(s_pp, NT - 1 + 4)
                        for c in range(2):
                            x = S0[:, :, c, :]
                            ins = dve.tensor_tensor(x, x, bank((7, 4)[c]).rearrange("p (b s) -> p b s", b=DB), ALU.add)
                            if c == 0:
                                ch.mark(ins)
                        ins.then_inc(s_sv, 1)
            dve.wait_ge(s_n3, 1)
            ch.wait()
            for c in range(2):
                ch(dve.tensor_tensor(QT[:, c, :], KH[:, c, :], E0[:, c, :], ALU.mult))
                ch(dve.scalar_tensor_tensor(QT[:, c, :], QT[:, c, :], -0.5, KH[:, c, :], ALU.mult, ALU.mult))
                ch(dve.scalar_tensor_tensor(QT[:, c, :], QT[:, c, :], 1.5, KH[:, c, :], ALU.add, ALU.mult))
            dve.wait_ge(s_n4, 1)
            ch(dve.tensor_tensor(YT[:, 2:4, :], YT[:, 2:4, :], QT, ALU.mult))
            mark_picked(sel[5])
            keep(e, ch, "dve")


def attend_block(e):
    nc, i, o, at, bank, tcol, sem, layer = (e[k] for k in ("nc", "i", "o", "at", "bank", "tcol", "sem", "layer"))
    ident, ident16, ps = e["ident"], e["ident16"], e["ps"]
    qT, kT, V = at("X", 0, 4, TOK), at("X", 4 * TOK, 2, TOK), at("X", 6 * TOK, NT, 256)
    YT = at("A", 0, KC, TOK)
    M16 = at("M", 0, 2304 + LS // 2).bitcast(BF16)
    KV = [[at(*x, NPG // 2, 512) for x in half] for half in (
        (("W", 0), ("W", 4096)), (("C", 0), ("C", 4096)), (("X", 0), ("S", 0)))]
    Pb, PT = at("S", 0, 2, SEQ), at("S", 2 * SEQ, 2, SEQ)
    PS, PTS = at("S", 4 * SEQ, LS), at("G", 0, NPG + 1, P)
    yo, QA, YR = at("U", 0, 2, 512), at("U", 1024, DB, 2, 32), at("U", 1536, 256)
    RS, NM, RI = e["stat"][:, 0:16], e["stat"][:, 16:18], e["stat"][:, 24:40]
    nsteps = (NT - 1) * NH

    s_kv = [sem(f"kv_cached{n}") for n in range(3)]
    s_zk, s_zv, s_zw = sem("ss_mask"), sem("ss_o_copied"), sem("ss_o_turned")
    s_ss, s_mx, s_ex, s_tg, s_ga, s_gd, s_pv, s_on = (sem(n) for n in (
        "s_done", "s_max", "s_exp", "p_turned", "p_copied_act", "p_copied_dve", "pv_done", "o_scaled"))
    s_qz, s_qa = sem("qa_zeroed"), sem("qa_ready")
    s_zs, s_zm, s_ze, s_zn, s_zt, s_zp, s_zo = (sem(n) for n in (
        "ss_done", "ss_max", "ss_exp", "ss_scaled", "ss_turned", "ss_pv", "ss_out"))
    s_zt_copied = sem("ss_turned_copied")

    groups, by_step = [], {}
    for n in range(nsteps + 3):
        mine = []
        if n < nsteps:
            for j0 in range(0, n // NH + 1, 4):
                mine.append(("p", n, j0, min(4, n // NH + 1 - j0)))
        if n > NH and n % NH == 2:
            mine.append(("y", n // NH - 1, 0, 4))
        by_step[n] = [(len(groups) + k, g) for k, g in enumerate(mine)]
        groups += mine
    ngp = len(groups)

    def waits_group(eng, q):
        eng.wait_ge((s_ga, s_gd)[q % 2], q // 2 + 1)

    def copy_group(eng, copy, q, g):
        eng.wait_ge(s_tg, q + 1)
        kind, n, j0, cnt = g
        if kind == "p":
            if n >= 2:
                eng.wait_ge(s_pv, n - 1)
            ins = copy(PT[:, n % 2, j0 * P:(j0 + cnt) * P], bank(4 + q % 2, cnt * P))
        else:
            ins = copy(YT[:, 4:8, tcol(n)], bank(4 + q % 2).rearrange("p (c s) -> p c s", c=4))
        ins.then_inc((s_ga, s_gd)[q % 2], 1)

    with nc.Block() as block:
        @block.sync
        def _(sp):
            def place_free(b, half):
                if b == 2:
                    sp.wait_ge(s_on, NT - 1)
                    sp.wait_ge(s_qa, 1)
                if b >= 3:
                    sp.wait_ge(s_zp, 2 * (b - 3) + half + 1)

            for b in range(DB):
                for half in range(2):
                    for_pages(sp, e, b * NPG + half * (NPG // 2),
                              lambda pg, page: sp.dma_start(
                                  KV[b % 3][half][:, pg, :], i["kv"][page].rearrange("n p w -> (n p) w")
                              ).then_inc(s_kv[b % 3], 16),
                              lambda: place_free(b, half))

        @block.tensor
        def _(pe):
            def scores(n):
                t, h = divmod(n, NH)
                W = (t + 1) * P
                kv, g = divmod(h, 2)
                part = slice(64 * (kv % 2), 64 * (kv % 2) + 64)
                if n >= 2:
                    pe.wait_ge(s_ex, n - 1)
                m0 = t * (t + 1) // 2 * P
                for a in range(0, W, 512):
                    b = min(a + 512, W)
                    out = ps[:, (n % 2) * 1024 + a:(n % 2) * 1024 + b]
                    pe.matmul(out, ident16, M16[:, m0 + a:m0 + b], start=True, stop=False)
                    ins = pe.matmul(out, qT[part, (kv // 2) * 2 + g, tcol(t)], kT[part, kv // 2, a:b],
                                    start=False, stop=True)
                ins.then_inc(s_ss, 1)

            def turn(n):
                for q, (kind, x, j0, cnt) in by_step[n]:
                    if q >= 2:
                        waits_group(pe, q - 2)
                    if kind == "p":
                        pe.wait_ge(s_ex, n + 1)
                        for k in range(cnt):
                            ins = pe.transpose(bank(4 + q % 2)[:, k * P:(k + 1) * P],
                                               Pb[:, n % 2, (j0 + k) * P:(j0 + k + 1) * P], ident)
                    else:
                        pe.wait_ge(s_on, x + 1)
                        for k in range(4):
                            ins = pe.transpose(bank(4 + q % 2)[:, k * P:(k + 1) * P],
                                               yo[:, x % 2, k * P:(k + 1) * P], ident)
                    ins.then_inc(s_tg, 1)

            scores(0)
            scores(1)
            turn(0)
            for n in range(nsteps + 2):
                if n + 2 < nsteps:
                    scores(n + 2)
                turn(n + 1)
                if n < nsteps:
                    t, h = divmod(n, NH)
                    if h == 0 and t >= 2:
                        pe.wait_ge(s_on, t - 1)
                    for q, (kind, x, j0, cnt) in by_step[n]:
                        if kind != "p":
                            continue
                        waits_group(pe, q)
                        for j in range(j0, j0 + cnt):
                            ins = pe.matmul(bank(6 + t % 2)[:, h * HD:(h + 1) * HD], PT[:, n % 2, j * P:(j + 1) * P],
                                            V[:, j, (h // 2) * HD:(h // 2 + 1) * HD],
                                            start=(j == 0), stop=(j == t))
                    ins.then_inc(s_pv, 1)
            pe.wait_ge(s_qa, 1)
            pe.wait_ge(s_zk, 1)
            pe.wait_ge(s_ga, (ngp + 1) // 2)
            pe.wait_ge(s_gd, ngp // 2)
            pe.wait_ge(s_on, NT - 1)
            for bp in range(DB // 2):
                for b in (2 * bp, 2 * bp + 1):
                    pe.wait_ge(s_kv[b % 3], 16 * NPG * (b // 3 + 1))
                if bp:
                    pe.wait_ge(s_ze, bp)
                for a in range(0, LS, 512):
                    b = min(a + 512, LS)
                    pe.matmul(ps[:, a:b], e["spread"][0:NS, bp, :], M16[0:NS, 4608 + a:4608 + b],
                              start=True, stop=False, skip_group_check=True)
                    for b2 in range(2):
                        for pair in range(2):
                            r0 = 32 * (2 * b2 + pair)
                            keys, out = kT[:, pair, SEQ:TOK], ps[r0:r0 + 32, a:b]
                            if a < PAST:
                                j = a // PAGE
                                keys = KV[(2 * bp + b2) % 3][j // 8][:, j % 8:j % 8 + 4, pair * P:(pair + 1) * P]
                                out = out.rearrange("p (j s) -> p j s", s=PAGE)
                            ins = pe.matmul(out, QA[:, 2 * bp + b2, pair, :], keys,
                                            start=False, stop=True, skip_group_check=True)
                ins.then_inc(s_zs, 1)
                pe.wait_ge(s_zn, bp + 1)
                for g in range(5):
                    cnt = min(4, NPG + 1 - 4 * g)
                    if 5 * bp + g >= 2:
                        pe.wait_ge(s_zt_copied, 5 * bp + g - 1)
                    for k in range(cnt):
                        j = 4 * g + k
                        w = P if j < NPG else NS
                        ins = pe.transpose(bank(5 + (5 * bp + g) % 2)[0:w, k * P:(k + 1) * P],
                                           PS[:, j * P:j * P + w], ident)
                    ins.then_inc(s_zt, 1)
                pe.wait_ge(s_zt_copied, 5 * bp + 5)
                if bp:
                    pe.wait_ge(s_zv, bp)
                for b2 in range(2):
                    out, cols = bank(7, 256)[64 * b2:64 * b2 + 64, :], slice(64 * b2, 64 * b2 + 64)
                    for j in range(NPG):
                        ins = pe.matmul(out, PTS[:, j, cols], KV[(2 * bp + b2) % 3][j // 8][:, j % 8, 256:512],
                                        start=(j == 0), stop=False)
                        if j == NPG // 2 - 1:
                            ins.then_inc(s_zp, 1)
                    pe.matmul(out, PTS[0:NS, NPG, cols], V[0:NS, NT - 1, :], start=False, stop=True).then_inc(s_zp, 1)
                pe.wait_ge(s_zv, bp + 1)
                if bp:
                    pe.wait_ge(s_zo, bp)
                for pair in range(2):
                    ins = pe.transpose(bank(7)[:, 256 + pair * P:256 + (pair + 1) * P], YR[:, pair * P:(pair + 1) * P],
                                       ident)
                ins.then_inc(s_zw, 1)

        @block.scalar
        def _(act):
            def exp(n):
                W = (n // NH + 1) * P
                act.wait_ge(s_mx, n + 1)
                if n >= 2:
                    act.wait_ge(s_tg, max(q for q, g in by_step[n - 2] if g[0] == "p") + 1)
                if n % NH == 0 and n >= 2 * NH:
                    act.wait_ge(s_on, n // NH - 1)
                act.activation(Pb[:, n % 2, 0:W], ps[:, (n % 2) * 1024:(n % 2) * 1024 + W], ACT.Exp,
                               bias=NM[:, n % 2:n % 2 + 1],
                               accum_out=RS[:, (n // NH % 2) * 8 + n % NH:(n // NH % 2) * 8 + n % NH + 1]
                               ).then_inc(s_ex, 1)

            exp(0)
            for n in range(-1, nsteps + 2):
                if n + 2 < nsteps:
                    exp(n + 2)
                for q, g in by_step[n + 1]:
                    if q % 2 == 0:
                        copy_group(act, act.copy, q, g)
            for bp in range(DB // 2):
                act.wait_ge(s_zm, bp + 1)
                if bp:
                    act.wait_ge(s_zt, 5 * bp)
                act.activation(PS, ps[:, 0:LS], ACT.Exp, bias=NM[:, 0:1], accum_out=RS[:, 0:1]).then_inc(s_ze, 1)
                for g in range(5):
                    cnt, w = (4, P) if g < 4 else (1, NS)
                    act.wait_ge(s_zt, 5 * bp + g + 1)
                    if bp and g == 0:
                        act.wait_ge(s_zp, 4 * bp)
                    act.copy(PTS[0:w, 4 * g:4 * g + cnt, :].rearrange("p a b -> p (a b)"),
                             bank(5 + (5 * bp + g) % 2, cnt * P)[0:w]).then_inc(s_zt_copied, 1)
                act.wait_ge(s_zp, 4 * bp + 4)
                if bp:
                    act.wait_ge(s_zw, bp)
                act.copy(YR, bank(7, 256)).then_inc(s_zv, 1)

        @block.gpsimd
        def _(pool):
            pool.memset(at("U", 1024, DB * 64), 0.0).then_inc(s_qz, 1)

        @block.vector
        def _(dve):
            ch = chains(e, dve, "dve")
            _, samples = selections()
            rounds, mark_picked = topk(e, dve, ch)
            dve.wait_ge(s_qz, 1)
            for k in range(2):
                part = slice(64 * k, 64 * k + 64)
                for pair in range(2):
                    for g in range(2):
                        c = k * 16 + g * 8
                        ch.mark(dve.tensor_copy(QA[part, :, pair, c:c + 8],
                                                qT[part, 2 * pair + g, SEQ:TOK].rearrange("p (b s) -> p b s", b=DB)))
            ch.wait()
            dve.engine_nop().then_inc(s_qa, 1)

            def rowmax(n):
                W = (n // NH + 1) * P
                dve.wait_ge(s_ss, n + 1)
                if n >= 2:
                    dve.wait_ge(s_ex, n - 1)
                dve.tensor_reduce(NM[:, n % 2:n % 2 + 1], ps[:, (n % 2) * 1024:(n % 2) * 1024 + W], AX, ALU.max,
                                  negate=True).then_inc(s_mx, 1)

            rowmax(0)
            for n in range(-1, nsteps + 2):
                if n + 2 < nsteps:
                    rowmax(n + 2)
                if 0 < n <= nsteps and n % NH == 0:
                    t = n // NH - 1
                    rs, ri = RS[:, (t % 2) * 8:(t % 2) * 8 + 8], RI[:, (t % 2) * 8:(t % 2) * 8 + 8]
                    dve.wait_ge(s_pv, n)
                    dve.wait_ge(s_ex, n)
                    ch(dve.reciprocal(ri, rs))
                    if t >= 2:
                        y = next(q for q, g in enumerate(groups) if g[0] == "y" and g[1] == t - 2)
                        dve.wait_ge(s_tg, y + 1)
                    dve.tensor_tensor(yo[:, t % 2, :].rearrange("p (h d) -> p h d", h=NH),
                                      bank(6 + t % 2).rearrange("p (h d) -> p h d", h=NH),
                                      ri.unsqueeze(2).broadcast_to([P, NH, HD]), ALU.mult).then_inc(s_on, 1)
                for q, g in by_step[n + 1]:
                    if q % 2:
                        copy_group(dve, dve.tensor_copy, q, g)
                if 2 * NH <= n < nsteps and n % 3:
                    rounds(samples, 1)
            mark_picked(samples)
            dve.engine_nop().then_inc(s_zk, 1)
            for bp in range(DB // 2):
                dve.wait_ge(s_zs, bp + 1)
                dve.tensor_reduce(NM[:, 0:1], ps[:, 0:LS], AX, ALU.max, negate=True).then_inc(s_zm, 1)
                dve.wait_ge(s_ze, bp + 1)
                ch(dve.reciprocal(RI[:, 0:1], RS[:, 0:1]))
                dve.tensor_scalar(PS, PS, RI[:, 0:1], None, ALU.mult).then_inc(s_zn, 1)
                dve.wait_ge(s_zw, bp + 1)
                for k in range(2):
                    for g in range(2):
                        for b2 in range(2):
                            src = bank(7)[64 * k:64 * k + 64, 256:512].rearrange(
                                "p (a b q x s) -> p a b q x s", a=2, b=2, q=2, s=DT)
                            for pair in range(2):
                                s0 = SEQ + (2 * bp + b2) * DT
                                ins = dve.tensor_copy(YT[64 * g:64 * g + 64, 4 + 2 * pair + k, s0:s0 + DT],
                                                      src[:, pair, b2, pair, 2 * k + g, :])
                                if (k, g, b2, pair) != (1, 1, 1, 1):
                                    ch.mark(ins)
                ins.then_inc(s_zo, 1)
            dve.wait_ge(s_zo, DB // 2)
            keep(e, ch, "dve")


class Norm:

    def __init__(self, e, name, X, lnt):
        self.e, self.X, self.g, self.b = e, X, lnt[:, 0:D], lnt[:, D:2 * D]
        sem = e["sem"]
        self.in_, self.var, self.root, self.unit, self.ready = (
            sem(name + x) for x in ("_params", "_var", "_root", "_unit", "_ready"))
        self.st = e["stat"][:, 40:64].rearrange("p (a b) -> p a b", a=2)
        self.mv = e["stat"][:, 64:72]
        self.rt = e["stat"][:, 72:80]

    def load(self, sp, n, layer):
        sp.dma_start(self.g, lay(self.e["i"]["ln"], layer)[:, n, :].broadcast_to([P, D])).then_inc(self.in_, 16)
        sp.dma_start(self.b, lay(self.e["i"]["ln"], layer)[:, n + 1, :].broadcast_to([P, D])).then_inc(self.in_, 16)

    def stats(self, ch, dve, t):
        R, k = rows(t), t % 2
        for a in range(2):
            ins = dve.bn_stats(self.st[0:R, k, 6 * a:6 * a + 6], self.X[0:R, t, 512 * a:512 * a + 512])
            ch.mark(ins)
        ch.wait()
        mv = self.mv[0:R, 4 * k:4 * k + 4]
        ch(dve.bn_aggr(mv[:, 0:2], self.st[0:R, k, :]))
        dve.tensor_scalar(mv[:, 2:3], mv[:, 1:2], EPS, None, ALU.add).then_inc(self.var, 1)

    def act(self, act, ch, t):
        R, k = rows(t), t % 2
        act.wait_ge(self.var, t + 1)
        ch(act.activation(self.rt[0:R, 4 * k:4 * k + 1], self.mv[0:R, 4 * k + 2:4 * k + 3], ACT.Ln))
        act.activation(self.rt[0:R, 4 * k + 1:4 * k + 2], self.rt[0:R, 4 * k:4 * k + 1], ACT.Exp,
                       scale=-0.5).then_inc(self.root, 1)

    def unit_rows(self, ch, dve, t):
        R, k = rows(t), t % 2
        v, r = self.mv[0:R, 4 * k + 2:4 * k + 3], self.rt[0:R, 4 * k + 1:4 * k + 2]
        a, b = self.rt[0:R, 4 * k + 2:4 * k + 3], self.rt[0:R, 4 * k + 3:4 * k + 4]
        dve.wait_ge(self.root, t + 1)
        ch(dve.scalar_tensor_tensor(a, r, v, r, ALU.mult, ALU.mult))
        ch(dve.tensor_scalar(a, a, -0.5, 1.5, ALU.mult, ALU.add))
        ch(dve.tensor_tensor(b, r, a, ALU.mult))
        x = self.X[0:R, t, :]
        dve.tensor_scalar(x, x, self.mv[0:R, 4 * k:4 * k + 1], b, ALU.subtract, ALU.mult).then_inc(self.unit, 1)

    def pool(self, ch, pool, t):
        R = rows(t)
        x = self.X[0:R, t, :]
        if t == 0:
            pool.wait_ge(self.in_, 32)
        pool.wait_ge(self.unit, t + 1)
        ch(pool.tensor_tensor(x, x, self.g[0:R], ALU.mult))
        pool.tensor_tensor(x, x, self.b[0:R], ALU.add).then_inc(self.ready, 1)


def out_block(e):
    nc, i, o, at, bank, tcol, sem, layer = (e[k] for k in ("nc", "i", "o", "at", "bank", "tcol", "sem", "layer"))
    ident, ps = e["ident"], e["ps"]
    X, YT = at("X", 0, NT, D), at("A", 0, KC, TOK)
    WO = at("W", 0, KC, D)
    MV, MKT = at(RR, 0, 2, 512), at(RR, 1024, XH, NMEM)
    MK = at(RR, 2048, 2, 512)
    MT = at(RR, 3072, KC, NMEM)
    WK, WV = at(RR, 5120, KC, 512), at(RR, 9216, KC, 512)
    ln = Norm(e, "ln1", X, at(RR, 13312, 2 * D))
    s_m = [sem(f"mem_in{n}") for n in range(3)]
    s_wo, s_xi = [sem(f"w_out{n}") for n in range(2)], [sem(f"x_back{n}") for n in range(2)]
    s_mp, s_me, s_mt, s_mte, s_mo = (sem(n) for n in ("mem_done", "mem_copied", "mem_turned", "mem_turn_copied", "mem_out"))
    s_op, s_oa, s_ht, s_he = (sem(n) for n in ("out_done", "out_added", "h_turned", "h_copied"))

    with nc.Block() as block:
        @block.sync
        def _(sp):
            w = lambda n: lay(i[n], layer).rearrange("l (k p) n -> p (l k) n", p=P)
            sp.dma_start(MT, i["memT"].rearrange("(k p) m -> p k m", p=P)).then_inc(s_m[0], 16)
            sp.dma_start(WK, w("w_xk")).then_inc(s_m[1], 16)
            sp.dma_start(WV, w("w_xv")).then_inc(s_m[2], 16)
            for n in range(2):
                sp.dma_start(WO[:, 4 * n:4 * n + 4, :], w("w_out")[:, 4 * n:4 * n + 4, :]).then_inc(s_wo[n], 16)
            sp.dma_start(X[:, 0:NT - 1, :], o["y_prompt"][0].rearrange("(t p) d -> p t d", p=P)).then_inc(s_xi[0], 16)
            sp.dma_start(X[0:NS, NT - 1, :], o["y_sample"].rearrange("b t d -> (b t) d")).then_inc(s_xi[1], 16)
            ln.load(sp, 0, layer)
            sp.wait_ge(s_me, 4)
            sp.dma_start(lay(o["mem_k"], layer).rearrange("l b (m p) d -> p (l b m) d", p=P), MK).then_inc(s_mo, 16)
            sp.dma_start(lay(o["mem_v"], layer).rearrange("l b (m p) d -> p (l b m) d", p=P), MV).then_inc(s_mo, 16)
            sp.wait_ge(s_mo, 32)

        @block.tensor
        def _(pe):
            pe.wait_ge(s_m[0], 16)
            for n in range(4):
                w = (WK, WV)[n // 2]
                if n % 2 == 0:
                    pe.wait_ge(s_m[1 + n // 2], 16)
                for k in range(KC):
                    ins = pe.matmul(bank(n), MT[:, k, (n % 2) * P:(n % 2 + 1) * P], w[:, k, :],
                                    start=(k == 0), stop=(k == KC - 1))
                ins.then_inc(s_mp, 1)
            for m in range(2):
                pe.wait_ge(s_me, m + 1)
                for h in range(XH):
                    ins = pe.transpose(bank(4 + m)[:, h * P:(h + 1) * P], MK[:, m, h * P:(h + 1) * P], ident)
                ins.then_inc(s_mt, 1)
            pe.wait_ge(s_me, 4)
            pe.wait_ge(s_mte, 2)

            def turn(t):
                R = rows(t)
                pe.wait_ge(ln.ready, t + 1)
                if t:
                    pe.wait_ge(s_he, 2 * t)
                for half in range(2):
                    for c in range(4):
                        k = 4 * half + c
                        ins = pe.transpose(bank(4 + half)[:, c * P:c * P + R], X[0:R, t, k * P:(k + 1) * P],
                                           ident[0:R, 0:R])
                    ins.then_inc(s_ht, 1)

            for t in range(NT):
                R = rows(t)
                if t >= 2:
                    pe.wait_ge(s_oa, t - 1)
                for k in range(KC):
                    if t == 0 and k % 4 == 0:
                        pe.wait_ge(s_wo[k // 4], 16)
                    for a in range(2):
                        ins = pe.matmul(bank(2 * (t % 2) + a)[0:R, :], YT[:, k, tcol(t)], WO[:, k, 512 * a:512 * a + 512],
                                        start=(k == 0), stop=(k == KC - 1))
                ins.then_inc(s_op, 1)
                if t >= 2:
                    turn(t - 2)
            turn(NT - 2)
            turn(NT - 1)

        @block.scalar
        def _(act):
            ch = chains(e, act, "act")
            for n in range(4):
                act.wait_ge(s_mp, n + 1)
                act.copy((MK, MV)[n // 2][:, n % 2, :], bank(n)).then_inc(s_me, 1)
            for m in range(2):
                act.wait_ge(s_mt, m + 1)
                act.copy(MKT[:, :, m * P:(m + 1) * P], bank(4 + m).rearrange("p (h s) -> p h s", h=XH)
                         ).then_inc(s_mte, 1)

            def hcopy(t):
                for half in range(2):
                    act.wait_ge(s_ht, 2 * t + half + 1)
                    act.copy(YT[:, 4 * half:4 * half + 4, tcol(t)],
                             bank(4 + half).rearrange("p (c s) -> p c s", c=4)[:, :, 0:rows(t)]).then_inc(s_he, 1)

            for t in range(NT):
                ln.act(act, ch, t)
                if t >= 2:
                    hcopy(t - 2)
            hcopy(NT - 2)
            hcopy(NT - 1)
            keep(e, ch, "act")

        @block.gpsimd
        def _(pool):
            ch = chains(e, pool, "pool")
            for t in range(NT):
                ln.pool(ch, pool, t)
            keep(e, ch, "pool")

        @block.vector
        def _(dve):
            ch = chains(e, dve, "dve")
            dve.wait_ge(s_xi[0], 16)
            dve.wait_ge(s_xi[1], 16)
            for t in range(NT + 1):
                if t < NT:
                    R = rows(t)
                    dve.wait_ge(s_op, t + 1)
                    ins = dve.scalar_tensor_tensor(X[0:R, t, :], X[0:R, t, :], ALPHA,
                                                   ps[0:R, 1024 * (t % 2):1024 * (t % 2) + 1024], ALU.mult, ALU.add)
                    ins.then_inc(s_oa, 1)
                    dve.wait_ge(s_oa, t + 1)
                    ln.stats(ch, dve, t)
                if t:
                    ln.unit_rows(ch, dve, t - 1)
            keep(e, ch, "dve")


def cross_block(e):
    nc, i, o, at, bank, tcol, sem, layer = (e[k] for k in ("nc", "i", "o", "at", "bank", "tcol", "sem", "layer"))
    ident, ps = e["ident"], e["ps"]
    X, HT = at("X", 0, NT, D), at("A", 0, KC, TOK)
    WQ, WO = at("W", 0, KC, 512), at("W", 4096, 4, D)
    MV, MKT = at(RR, 0, 2, 512), at(RR, 1024, XH, NMEM)
    QX = at(RR, 2048, XH, TOK)
    r0 = 2048 + XH * TOK
    QM = at(RR, r0, DB, XH, NS)
    r1 = r0 + 11776
    SK = [at(RR, x, XH, NMEM) for x in (r0 + 2048, r0 + 3072, r1, r1 + 1024)]
    SV = [at(RR, x, 2, 512) for x in (r0 + 4096, r0 + 5120, r1 + 2048, r1 + 3072)]
    Pb, PT = at(RR, r0 + 6144, 2, XH * NMEM), at(RR, r0 + 8192, 2 * XH, P)
    OT = at(RR, r0 + 9216, XH, P)
    ln = Norm(e, "ln2", X, at(RR, r0 + 9728, 2 * D))
    NM, RS, RI = e["stat"][:, 0:8], e["stat"][:, 8:16], e["stat"][:, 16:24]
    s_wq, s_wo = sem("w_xq"), sem("w_xo")
    s_sk, s_sv = [sem(f"mem_keys{n}") for n in range(4)], [sem(f"mem_values{n}") for n in range(4)]
    s_qp, s_qe, s_qm = (sem(n) for n in ("xq_done", "xq_copied", "xq_masked"))
    s_sp, s_sb, s_mx, s_ex, s_pn, s_tp, s_te, s_pv, s_pe, s_xp, s_xa, s_ht, s_he, s_vb = (sem(n) for n in (
        "xs_done", "xs_batch", "xs_max", "xs_exp", "xp_scaled", "xp_turned", "xp_copied", "xo_done", "xo_copied",
        "xproj_done", "xproj_added", "h2_turned", "h2_copied", "xv_batch"))

    with nc.Block() as block:
        @block.sync
        def _(sp):
            sp.dma_start(WQ, lay(i["w_xq"], layer).rearrange("l (k p) n -> p (l k) n", p=P)).then_inc(s_wq, 16)
            sp.dma_start(WO, lay(i["w_xo"], layer).rearrange("l (k p) n -> p (l k) n", p=P)).then_inc(s_wo, 16)
            ln.load(sp, 2, layer)
            def keys_in(b):
                sp.dma_start(SK[b % 4], lay(i["mem_kT"], layer)[:, b].rearrange("l h d m -> d (l h) m")
                             ).then_inc(s_sk[b % 4], 16)

            def values_in(b):
                sp.dma_start(SV[b % 4], lay(i["mem_v"], layer)[:, b].rearrange("l (a p) d -> p (l a) d", p=P)
                             ).then_inc(s_sv[b % 4], 16)

            for b in range(4):
                keys_in(b)
                values_in(b)
            for b in range(4, DB):
                sp.wait_ge(s_sb, b - 3)
                keys_in(b)
            for b in range(4, DB):
                sp.wait_ge(s_vb, b - 3)
                values_in(b)

        @block.tensor
        def _(pe):
            pe.wait_ge(s_wq, 16)
            for c in range(XH):
                if c >= 2:
                    pe.wait_ge(s_qe, c - 1)
                for k in range(KC):
                    for a, b in ((0, 512), (512, 1024), (1024, TOK)):
                        ins = pe.matmul(ps[:, (c % 2) * 1536 + a:(c % 2) * 1536 + b], WQ[:, k, c * P:(c + 1) * P],
                                        HT[:, k, a:b], start=(k == 0), stop=(k == KC - 1))
                ins.then_inc(s_qp, 1)
            pe.wait_ge(s_qe, XH)

            def scores(t):
                R = rows(t)
                if t:
                    pe.wait_ge(s_ex, t)
                if t < NT - 1:
                    for h in range(XH):
                        ins = pe.matmul(ps[:, h * NMEM:(h + 1) * NMEM], QX[:, h, tcol(t)], MKT[:, h, :],
                                        start=True, stop=True)
                else:
                    pe.wait_ge(s_qm, 1)
                    for b in range(DB):
                        pe.wait_ge(s_sk[b % 4], 16 * (b // 4 + 1))
                        for h in range(XH):
                            ins = pe.matmul(ps[0:R, h * NMEM:(h + 1) * NMEM], QM[:, b, h, :], SK[b % 4][:, h, :],
                                            start=(b == 0 and h % 2 == 0), stop=(b == DB - 1),
                                            skip_group_check=True)
                        ins.then_inc(s_sb, 1)
                ins.then_inc(s_sp, 1) if t < NT - 1 else None

            def turn(t):
                R = rows(t)
                pe.wait_ge(ln.ready, t + 1)
                for half in range(2):
                    if 2 * t + half >= 1:
                        pe.wait_ge(s_he, 2 * t + half)
                    for c in range(4):
                        k = 4 * half + c
                        ins = pe.transpose(bank(7)[:, c * P:c * P + R], X[0:R, t, k * P:(k + 1) * P], ident[0:R, 0:R])
                    ins.then_inc(s_ht, 1)

            def turn_p(t):
                R = rows(t)
                pe.wait_ge(s_pn, t + 1)
                if t:
                    pe.wait_ge(s_te, t)
                for n in range(8):
                    ins = pe.transpose(bank(2 + n // 4)[:, (n % 4) * P:(n % 4) * P + R],
                                       Pb[0:R, t % 2, n * P:(n + 1) * P], ident[0:R, 0:R])
                ins.then_inc(s_tp, 1)

            def values(t):
                pe.wait_ge(s_te, t + 1)
                if t:
                    pe.wait_ge(s_pe, t)
                if t < NT - 1:
                    for h in range(XH):
                        for a in range(2):
                            ins = pe.matmul(bank(4)[:, h * P:(h + 1) * P], MV[:, a, h * P:(h + 1) * P],
                                            PT[:, 2 * h + a, :], start=(a == 0), stop=(a == 1))
                    ins.then_inc(s_pv, 1)
                else:
                    for b in range(DB):
                        pe.wait_ge(s_sv[b % 4], 16 * (b // 4 + 1))
                        for h in range(XH):
                            for a in range(2):
                                ins = pe.matmul(bank(4)[:, h * P + b * DT:h * P + (b + 1) * DT],
                                                SV[b % 4][:, a, h * P:(h + 1) * P],
                                                PT[:, 2 * h + a, b * DT:(b + 1) * DT], start=(a == 0), stop=(a == 1))
                        ins.then_inc(s_vb, 1)

            def project(t):
                R = rows(t)
                pe.wait_ge(s_pe, t + 1)
                if t == 0:
                    pe.wait_ge(s_wo, 16)
                else:
                    pe.wait_ge(s_xa, t)
                for k in range(XH):
                    for a in range(2):
                        ins = pe.matmul(bank(5 + a)[0:R, :], OT[:, k, 0:R], WO[:, k, 512 * a:512 * a + 512],
                                        start=(k == 0), stop=(k == XH - 1))
                ins.then_inc(s_xp, 1)

            scores(0)
            for t in range(NT + 3):
                if t + 1 < NT:
                    scores(t + 1)
                if t < NT:
                    turn_p(t)
                if 1 <= t <= NT:
                    project(t - 1)
                if t < NT:
                    values(t)
                if t >= 3:
                    turn(t - 3)

        @block.scalar
        def _(act):
            ch = chains(e, act, "act")
            for c in range(XH):
                act.wait_ge(s_qp, c + 1)
                act.mul(QX[:, c, :], ps[:, (c % 2) * 1536:(c % 2) * 1536 + TOK], XD ** -0.5).then_inc(s_qe, 1)

            def exp(t):
                R, k = rows(t), t % 2
                act.wait_ge(s_mx, t + 1)
                if t >= 2:
                    act.wait_ge(s_tp, t - 1)
                for h in range(XH):
                    ins = act.activation(Pb[0:R, k, h * NMEM:(h + 1) * NMEM], ps[0:R, h * NMEM:(h + 1) * NMEM],
                                         ACT.Exp, bias=NM[0:R, 4 * k + h:4 * k + h + 1],
                                         accum_out=RS[0:R, 4 * k + h:4 * k + h + 1])
                ins.then_inc(s_ex, 1)

            def hcopy(t):
                for half in range(2):
                    act.wait_ge(s_ht, 2 * t + half + 1)
                    act.copy(HT[:, 4 * half:4 * half + 4, tcol(t)],
                             bank(7).rearrange("p (c s) -> p c s", c=4)[:, :, 0:rows(t)]).then_inc(s_he, 1)

            exp(0)
            for t in range(NT + 3):
                if t < NT:
                    R = rows(t)
                    if t + 1 < NT:
                        exp(t + 1)
                    act.wait_ge(s_tp, t + 1)
                    if t:
                        act.wait_ge(s_pv, t)
                    act.copy(PT[:, :, 0:R], ps[:, 1024:2048].rearrange("p (n s) -> p n s", n=8)[:, :, 0:R]
                             ).then_inc(s_te, 1)
                    if t < NT - 1:
                        act.wait_ge(s_pv, t + 1)
                    else:
                        act.wait_ge(s_vb, DB)
                    if t:
                        act.wait_ge(s_xp, t)
                    act.copy(OT[:, :, 0:R], bank(4).rearrange("p (h s) -> p h s", h=XH)[:, :, 0:R]).then_inc(s_pe, 1)
                if 2 <= t < NT + 2:
                    ln.act(act, ch, t - 2)
                if t >= 3:
                    hcopy(t - 3)
            keep(e, ch, "act")

        @block.gpsimd
        def _(pool):
            ch = chains(e, pool, "pool")
            ch(pool.memset(at(RR, r0, DB * XH * NS), 0.0))
            pool.wait_ge(s_qe, XH)
            for b in range(DB):
                c = slice(b * DT, (b + 1) * DT)
                ch.mark(pool.tensor_copy(QM[:, b, :, c], QX[:, :, SEQ + b * DT:SEQ + (b + 1) * DT]))
            ch.wait()
            pool.engine_nop().then_inc(s_qm, 1)
            for t in range(NT):
                ln.pool(ch, pool, t)
            keep(e, ch, "pool")

        @block.vector
        def _(dve):
            ch = chains(e, dve, "dve")

            def rowmax(t):
                R, k = rows(t), t % 2
                if t < NT - 1:
                    dve.wait_ge(s_sp, t + 1)
                else:
                    dve.wait_ge(s_sb, DB)
                if t >= 2:
                    dve.wait_ge(s_ex, t - 1)
                dve.tensor_reduce(NM[0:R, 4 * k:4 * k + 4], ps[0:R, 0:1024].rearrange("p (h m) -> p h m", h=XH), AX,
                                  ALU.max, negate=True).then_inc(s_mx, 1)

            def scale(t):
                R, k = rows(t), t % 2
                dve.wait_ge(s_ex, t + 1)
                ch(dve.reciprocal(RI[0:R, 4 * k:4 * k + 4], RS[0:R, 4 * k:4 * k + 4]))
                p = Pb[0:R, k, :].rearrange("p (h m) -> p h m", h=XH)
                dve.tensor_tensor(p, p, RI[0:R, 4 * k:4 * k + 4].unsqueeze(2).broadcast_to([R, XH, NMEM]),
                                  ALU.mult).then_inc(s_pn, 1)

            rowmax(0)
            scale(0)
            for t in range(NT + 2):
                if t + 1 < NT:
                    rowmax(t + 1)
                    scale(t + 1)
                if 1 <= t <= NT:
                    R = rows(t - 1)
                    dve.wait_ge(s_xp, t)
                    dve.scalar_tensor_tensor(X[0:R, t - 1, :], X[0:R, t - 1, :], ALPHA, ps[0:R, 2560:3584],
                                             ALU.mult, ALU.add).then_inc(s_xa, 1)
                    dve.wait_ge(s_xa, t)
                    ln.stats(ch, dve, t - 1)
                if t >= 2:
                    ln.unit_rows(ch, dve, t - 2)
            keep(e, ch, "dve")


FFC = 2
FFG = DFF // (FFC * P)
FFN_RAW = KC * FFC * P + TOK
FFN_PARTS = 2 * (KC * TOK + FFC * TOK + FFC * D + KC * P)
SEG = [(0, 384), (384, 768), (768, TOK)]


def ffn_block(e):
    nc, i, o, at, bank, tcol, sem, layer = (e[k] for k in ("nc", "i", "o", "at", "bank", "tcol", "sem", "layer"))
    ps = e["ps"]
    X, HT = at("X", 0, NT, D), at("A", 0, KC, TOK)
    WU = [at(NHEAD, 0, KC, FFC * P), at("A", 0, KC, FFC * P)]
    WD = at("A", 2048, FFC, D)
    SQ = [at("A", 4096, TOK), at(NHEAD, 2048, TOK)]
    ln = Norm(e, "ln3", X, at("A", 4096 + TOK, 2 * D))
    parts, n = [], 0
    for c, w in ((KC, TOK), (FFC, TOK), (FFC, D), (KC, P)):
        parts.append([e["parts"][:, n + k * c * w:n + (k + 1) * c * w].rearrange("p (a b) -> p a b", a=c)
                      for k in range(2)])
        n += 2 * c * w
    (HH, HL), (UH, UL), (DH, DL), (WH, WL) = parts

    s_wu, s_wd = [sem(f"w_up{n}") for n in range(2)], sem("w_down")
    s_th, s_tl, s_hi, s_uh, s_dhi, s_dl = (sem(n) for n in (
        "h_high", "h_low", "w_up_high", "w_up_low", "w_down_high", "w_down_low"))
    s_ub, s_rl, s_sq, s_qh, s_ql, s_dn, s_ad = (sem(n) for n in (
        "up_halves", "up_relu", "u_squared", "u_high", "u_low", "down_done", "down_added"))
    UB0, DN0, AD0 = 2, 1, 2

    with nc.Block() as block:
        @block.sync
        def _(sp):
            wu = lay(i["w_up"], layer).rearrange("l (k p) n -> p (l k) n", p=P)
            wd = lay(i["w_down"], layer).rearrange("l (k p) n -> p (l k) n", p=P)

            def up_in(g, n):
                sp.dma_start(WU[n], wu[:, :, bass.ds(g * (FFC * P), FFC * P)]).then_inc(s_wu[n], 16)

            def down_in(g):
                sp.dma_start(WD, wd[:, bass.ds(g * FFC, FFC), :]).then_inc(s_wd, 16)

            up_in(0, 0)
            sp.wait_ge(s_tl, KC)
            down_in(0)
            ln.load(sp, 4, layer)
            up_in(1, 1)
            with sp.Fori(0, FFG // 2 - 1) as g2:
                for n in range(2):
                    sp.wait_ge(s_uh, g2 * (4 * FFC) + (n + 1) * (2 * FFC))
                    sp.nop()
                    up_in(g2 * 2 + (n + 2), n)
                    sp.wait_ge(s_dl, g2 * (2 * FFC) + (n + 1) * FFC)
                    sp.nop()
                    down_in(g2 * 2 + (n + 1))
            sp.wait_ge(s_dl, (FFG - 1) * FFC)
            down_in(FFG - 1)
        @block.tensor
        def _(pe):
            with pe.Fori(0, FFG // 2) as g2:
                for n in range(2):
                    for c in range(FFC):
                        if c == 0:
                            pe.wait_ge(s_ad, g2 * (2 * NT) + (n * NT + AD0 - 1))
                        for half in range(2):
                            pe.wait_ge(s_uh, g2 * (4 * FFC) + (2 * (FFC * n + c) + half + 1))
                            if n == 0 and c == 0:
                                pe.wait_ge(s_tl, 4 * (half + 1))
                            for k in range(4 * half, 4 * half + 4):
                                for w, h in ((WH, HH), (WH, HL), (WL, HH)):
                                    for b, (x, y) in enumerate(SEG):
                                        ins = pe.matmul(bank(3 * c + b, y - x), w[:, k, :], h[:, k, x:y],
                                                        start=(k == 0 and h is HH and w is WH),
                                                        stop=(k == KC - 1 and w is WL))
                            ins.then_inc(s_ub, 1)
                    pe.wait_ge(s_dl, g2 * (2 * FFC) + (n + 1) * FFC)

                    def down(t, c):
                        R, b0 = rows(t), (6, 0)[t % 2]
                        for u, d in ((UH, DH), (UH, DL), (UL, DH)):
                            for a in range(2):
                                ins = pe.matmul(bank(b0 + a)[0:R, :], u[:, c, tcol(t)],
                                                d[:, c, 512 * a:512 * a + 512],
                                                start=(c == 0 and u is UH and d is DH),
                                                stop=(c == FFC - 1 and u is UL))
                        return ins

                    pe.wait_ge(s_ql, g2 * (6 * FFC) + (3 * (FFC * n + 1)))
                    pe.wait_ge(s_ad, g2 * (2 * NT) + (n * NT + AD0))
                    down(0, 0)
                    down(1, 0)
                    for t in range(NT):
                        if t % 3 == 0:
                            pe.wait_ge(s_ql, g2 * (6 * FFC) + (3 * (FFC * n + FFC - 1) + t // 3 + 1))
                        if t >= 2:
                            pe.wait_ge(s_ad, g2 * (2 * NT) + (n * NT + t - 1 + AD0))
                            down(t, 0)
                        down(t, 1).then_inc(s_dn, 1)

        @block.scalar
        def _(act):
            ch = chains(e, act, "act")
            for k in range(KC):
                act.copy(HH[:, k, :], HT[:, k, :]).then_inc(s_th, 1)
            with act.Fori(0, FFG // 2) as g2:
                for n in range(2):
                    def up_high(c, half):
                        act.wait_ge(s_ub, g2 * (4 * FFC) + (2 * (FFC * n + c) + half - 1 + UB0))
                        ks = slice(4 * half, 4 * half + 4)
                        act.copy(WH[:, ks, :], WU[n][:, ks, c * P:(c + 1) * P]).then_inc(s_hi, 1)

                    def down_high(c):
                        act.copy(DH[:, c, :], WD[:, c, :]).then_inc(s_dhi, 1)

                    act.wait_ge(s_wu[n], g2 * 16 + 16)
                    up_high(0, 0)
                    up_high(0, 1)
                    act.wait_ge(s_wd, g2 * 32 + 16 * (n + 1))
                    act.wait_ge(s_dn, g2 * (2 * NT) + (n * NT + DN0))
                    down_high(0)
                    up_high(1, 0)
                    down_high(1)
                    up_high(1, 1)
                    for c in range(FFC):
                        def square_high(b):
                            x, y = SEG[b]
                            act.wait_ge(s_sq, g2 * (6 * FFC) + (3 * (FFC * n + c) + b + 1))
                            act.copy(UH[:, c, x:y], SQ[c][:, x:y]).then_inc(s_qh, 1)

                        act.wait_ge(s_ub, g2 * (4 * FFC) + (2 * (FFC * n + c) + 2 + UB0))
                        for b, (x, y) in enumerate(SEG):
                            act.activation(SQ[c][:, x:y], bank(3 * c + b, y - x), ACT.Relu).then_inc(s_rl, 1)
                            if b:
                                square_high(b - 1)
                        square_high(2)
            for t in range(NT):
                ln.act(act, ch, t)
            keep(e, ch, "act")

        @block.gpsimd
        def _(pool):
            ch = chains(e, pool, "pool")
            with pool.Fori(0, FFG // 2) as g2:
                for n in range(2):
                    def up_low(c, half):
                        pool.wait_ge(s_hi, g2 * (4 * FFC) + (2 * (FFC * n + c) + half + 1))
                        ks = slice(4 * half, 4 * half + 4)
                        pool.tensor_tensor(WL[:, ks, :], WU[n][:, ks, c * P:(c + 1) * P], WH[:, ks, :], ALU.subtract
                                           ).then_inc(s_uh, 1)

                    def down_low(c):
                        pool.wait_ge(s_dhi, g2 * (2 * FFC) + (FFC * n + c + 1))
                        pool.tensor_tensor(DL[:, c, :], WD[:, c, :], DH[:, c, :], ALU.subtract).then_inc(s_dl, 1)

                    up_low(0, 0)
                    up_low(0, 1)
                    down_low(0)
                    up_low(1, 0)
                    down_low(1)
                    up_low(1, 1)
            for t in range(0, NT, 2):
                ln.pool(ch, pool, t)
            keep(e, ch, "pool")

        @block.vector
        def _(dve):
            ch = chains(e, dve, "dve")
            dve.engine_nop().then_inc(s_ub, UB0)
            dve.engine_nop().then_inc(s_dn, DN0)
            dve.engine_nop().then_inc(s_ad, AD0)
            for k in range(KC):
                dve.wait_ge(s_th, k + 1)
                dve.tensor_tensor(HL[:, k, :], HT[:, k, :], HH[:, k, :], ALU.subtract).then_inc(s_tl, 1)
            for t in range(NT):
                R = rows(t)
                ch.mark(dve.tensor_scalar(X[0:R, t, :], X[0:R, t, :], ALPHA, None, ALU.mult))
            ch.wait()
            with dve.Fori(0, FFG // 2) as g2:
                for n in range(2):
                    dve.wait_ge(s_ad, g2 * (2 * NT) + (n * NT + AD0))
                    for c in range(FFC):
                        def low(b):
                            x, y = SEG[b]
                            dve.wait_ge(s_qh, g2 * (6 * FFC) + (3 * (FFC * n + c) + b + 1))
                            dve.tensor_tensor(UL[:, c, x:y], SQ[c][:, x:y], UH[:, c, x:y], ALU.subtract
                                              ).then_inc(s_ql, 1)

                        for b, (x, y) in enumerate(SEG):
                            z = SQ[c][:, x:y]
                            dve.wait_ge(s_rl, g2 * (6 * FFC) + (3 * (FFC * n + c) + b + 1))
                            dve.tensor_tensor(z, z, z, ALU.mult).then_inc(s_sq, 1)
                            if b:
                                low(b - 1)
                        low(2)
                    for t in range(NT):
                        R = rows(t)
                        dve.wait_ge(s_dn, g2 * (2 * NT) + (n * NT + t + 1 + DN0))
                        b0 = (6, 0)[t % 2] * 512
                        dve.tensor_tensor(X[0:R, t, :], X[0:R, t, :], ps[0:R, b0:b0 + 1024], ALU.add).then_inc(s_ad, 1)
            dve.wait_ge(s_ad, FFG * NT + AD0)
            for t in range(NT + 1):
                if t < NT:
                    ln.stats(ch, dve, t)
                if t:
                    ln.unit_rows(ch, dve, t - 1)
                if t and t % 2 == 0:
                    ln.pool(ch, dve, t - 1)
            keep(e, ch, "dve")


def constants():
    import numpy as np

    f4 = np.float32
    c = np.zeros((P, NCST), f4)

    def put(name, x):
        a, b = CST[name]
        c[:x.shape[0], a:b] = x.reshape(x.shape[0], b - a)

    put("ident", np.eye(P, dtype=f4))
    pos = np.zeros((P, NT), np.int64)
    for t in range(NT - 1):
        pos[:, t] = t * P + np.arange(P)
    pos[:NS, NT - 1] = PAST + np.arange(NS) % DT
    for n, half in ((64, 32), (32, 16)):
        inv = (f4(10000.0) ** (-np.arange(half, dtype=f4) / f4(half))).astype(f4)
        ang = pos.astype(f4)[:, :, None] * inv
        co, si = np.cos(ang).astype(f4), np.sin(ang).astype(f4)
        put(f"cos{n}", np.concatenate([co, co], -1))
        put(f"sin{n}", np.concatenate([-si, si], -1))
    a = np.arange(P)
    put("causal", np.where(a[None] <= a[:, None], 0.0, NEG).astype(f4))
    b = np.arange(NS)
    put("own", np.where((b[None] // DT == b[:, None] // DT) & (b[None] <= b[:, None]), 0.0, NEG).astype(f4))
    put("heads", (a[None] // 64 == a[:, None] // 64).astype(f4))
    put("batch", (b[:, None] // DT == np.arange(DB)[None]).astype(f4))

    c16 = np.zeros((P, NCST16), f4)
    c16[:, 0:P] = np.eye(P)
    start = np.ones(TOK)
    start[0:SEQ:P] = 0
    start[SEQ::DT] = 0
    c16[:, P:P + TOK] = start
    col = np.arange(P)
    for bp in range(4):
        c16[:NS, P + TOK + bp * P:P + TOK + (bp + 1) * P] = (
            b[:, None] == (2 * bp + col // 64)[None] * DT + (col % DT)[None])
    m = np.zeros((P, NMASK), f4)
    m[:, 0:P] = np.eye(P)
    for n, s in enumerate(LEVELS):
        m[:, (n + 1) * P:(n + 2) * P] = ((a[:, None] // (2 * s) == a[None] // (2 * s)) & (a[:, None] % (2 * s) < s)
                                         & (a[None] % (2 * s) >= s))
    return c, c16, m


_OUTS = [("y_prompt", (1, SEQ, D)), ("y_sample", (DB, DT, D)),
         ("k_prompt", (DEPTH, 1, SEQ, 256)), ("v_prompt", (DEPTH, 1, SEQ, 256)), ("kidx_prompt", (DEPTH, 1, SEQ, ID)),
         ("k_sample", (DEPTH, DB, DT, 256)), ("v_sample", (DEPTH, DB, DT, 256)), ("kidx_sample", (DEPTH, DB, DT, ID)),
         ("hgrn_prompt", (DEPTH, 1, 4, 64, 64)), ("hgrn_sample", (DEPTH, DB, 4, 64, 64)),
         ("conv_prompt", (DEPTH, P, 4)), ("conv_sample", (DEPTH, P, 2 * DB * 2)),
         ("mem_k", (DEPTH, 1, NMEM, 512)), ("mem_v", (DEPTH, 1, NMEM, 512))]


def kernel(**inputs):
    import numpy as np
    import concourse.bacc as bacc
    from concourse.bass_utils import run_bass_kernel_spmd

    x = {k: np.asarray(v) for k, v in inputs.items()}
    f4 = np.float32
    chunks = lambda a: np.moveaxis(a.reshape(*a.shape[:-1], 2, P), -1, 1)
    cst, cst16, masks = constants()
    par = np.concatenate([chunks(x["w_conv"]).reshape(DEPTH, P, 6), chunks(x["hg_norm"]).reshape(DEPTH, P, 2),
                          np.transpose(x["state_conv"].reshape(DEPTH, DB, 2, 2, P), (0, 4, 3, 1, 2)).reshape(DEPTH, P, 32)],
                         axis=2)
    arrays = {
        "x_prompt": x["x_prompt"], "x_sample": x["x_sample"],
        "w_in": x["w_in"], "w_out": x["w_out"], "w_xq": x["w_xq"], "w_xk": x["w_xk"], "w_xv": x["w_xv"],
        "w_xo": x["w_xo"], "w_up": x["w_up"], "w_down": x["w_down"],
        "kidxT": np.swapaxes(x["cache_kidx"].reshape(DEPTH * NPHYS, PAGE, ID), 1, 2),
        "kv": np.concatenate([
            np.moveaxis(x["cache_k"].reshape(DEPTH * NPHYS, PAGE, 2, P), 1, 3).swapaxes(1, 2).reshape(DEPTH * NPHYS, P, 256),
            x["cache_v"].reshape(DEPTH * NPHYS, PAGE, NKV * HD)], axis=2),
        "state_hgrn": x["state_hgrn"],
        "mem_kT": np.transpose(x["cache_mem_k"], (0, 1, 3, 4, 2)),
        "mem_v": x["cache_mem_v"].reshape(DEPTH, DB, NMEM, XH * XD),
        "memT": x["mem_prompt"][0].T,
        "page_table": x["page_table"].reshape(1, DB * NPG),
        "params": par,
        "lb_logits": np.transpose(x["hg_lb_logits"].reshape(DEPTH, 2, P), (2, 0, 1)).reshape(P, 4),
        "ln": np.stack([x[k] for k in ("ln1_g", "ln1_b", "ln2_g", "ln2_b", "ln3_g", "ln3_b")], axis=1),
        "cst": cst, "cst_narrow": np.concatenate([cst16, masks], axis=1),
    }
    arrays = {k: np.ascontiguousarray(v) for k, v in arrays.items()}
    nc = bacc.Bacc("TRN2", target_bir_lowering=False, num_devices=1)
    ins = {k: nc.dram_tensor("in_" + k, v.shape, mybir.dt.from_np(v.dtype), kind="ExternalInput").ap()
           for k, v in arrays.items()}
    outs = {k: nc.dram_tensor("out_" + k, s, F32, kind="ExternalOutput").ap() for k, s in _OUTS}
    build(nc, ins, outs)
    r = run_bass_kernel_spmd(nc, [{"in_" + k: v for k, v in arrays.items()}], core_ids=[0]).results[0]
    g = {k: r["out_" + k] for k, _ in _OUTS}
    conv_p = np.transpose(g["conv_prompt"].reshape(DEPTH, P, 2, 2), (0, 3, 2, 1)).reshape(DEPTH, 1, 2, 256)
    conv_s = np.transpose(g["conv_sample"].reshape(DEPTH, P, 2, DB, 2), (0, 3, 4, 2, 1)).reshape(DEPTH, DB, 2, 256)
    kv = lambda a, b, s: a.reshape(DEPTH, b, s, NKV, HD)
    return (g["y_prompt"], g["y_sample"], kv(g["k_prompt"], 1, SEQ), kv(g["v_prompt"], 1, SEQ), g["kidx_prompt"],
            kv(g["k_sample"], DB, DT), kv(g["v_sample"], DB, DT), g["kidx_sample"],
            g["hgrn_prompt"], g["hgrn_sample"], conv_p, conv_s,
            g["mem_k"].reshape(DEPTH, 1, NMEM, XH, XD), g["mem_v"].reshape(DEPTH, 1, NMEM, XH, XD))
```
